# Optimizing a Trainium2 kernel written in Bass

```python
import math
import jax, jax.numpy as jnp
from jax import lax
import numpy as np

D_MODEL = 2048
BATCH = 1
SEQ = 512
DEPTH = 2

N_EVEN = (DEPTH + 1) // 2
N_ODD = DEPTH // 2
RWKV_WIDTH = D_MODEL // 2
RWKV_HEAD = 64
RWKV_HEADS = RWKV_WIDTH // RWKV_HEAD
RWKV_LORA = 64
S5_WIDTH = D_MODEL // 2
S5_GROUP = 16
S5_GROUPS = S5_WIDTH // S5_GROUP
S5_STATE = 64
A_IN = 4 * RWKV_WIDTH + 2 * RWKV_LORA
B_IN = 2 * S5_WIDTH
EVEN_IN = A_IN + B_IN
EVEN_MIX = RWKV_WIDTH + S5_WIDTH
MLA_HEADS = 16
QK_NOPE = 128
QK_ROPE = 64
V_HEAD = 128
Q_LORA = 512
KV_LORA = 512
MLA_WIDTH = MLA_HEADS * V_HEAD
ODD_IN = Q_LORA + KV_LORA + QK_ROPE + MLA_WIDTH
ROPE_BASE = 10000.0
Q_BLOCK = 128
NORM_EPS = 1e-6
LNX_EPS = 64e-5

kernel_name = 'hybrid_rwkv7_s5_mla_trunk'

def rms_norm(x, g):
    xf = x.astype(jnp.float32)
    xf = xf * lax.rsqrt(jnp.mean(xf * xf, axis=-1, keepdims=True) + NORM_EPS)
    return xf * g.astype(jnp.float32)

def ada_modulation(c, w, b):
    m = (jax.nn.silu(c.astype(jnp.float32)) @ w + b)[:, None, :]
    return m[..., :D_MODEL], m[..., D_MODEL:2 * D_MODEL], m[..., 2 * D_MODEL:]

def token_shift(p, mu):
    prev = jnp.pad(p, ((0, 0), (1, 0), (0, 0)))[:, :-1]
    return p + (prev - p) * mu

def rwkv7_time_mix(p, mu, w0, w2, a0, a2, k_k, k_a, r_k, lnx_g, lnx_b):
    bsz, seq, _ = p.shape
    W, H, N, R = RWKV_WIDTH, RWKV_HEADS, RWKV_HEAD, RWKV_LORA
    p = token_shift(p.astype(jnp.float32), mu)
    r, k, v, g = p[..., :W], p[..., W:2 * W], p[..., 2 * W:3 * W], p[..., 3 * W:4 * W]
    w_lo, a_lo = p[..., 4 * W:4 * W + R], p[..., 4 * W + R:]
    w = -jax.nn.softplus(-(w0 + jnp.tanh(w_lo) @ w2)) - 0.5
    decay = jnp.exp(-jnp.exp(w))
    a = jax.nn.sigmoid(a0 + a_lo @ a2)
    heads = lambda t: t.reshape(bsz, seq, H, N)
    kk = heads(k * k_k)
    kk = kk * lax.rsqrt(jnp.maximum(jnp.sum(kk * kk, -1, keepdims=True), 1e-24))
    k = k * (1.0 + (a - 1.0) * k_a)
    r, k, v, decay, a = heads(r), heads(k), heads(v), heads(decay), heads(a)

    def step(state, inp):
        r_t, dec_t, k_t, v_t, rem_t, rep_t = inp
        sa = jnp.einsum('bhvk,bhk->bhv', state, rem_t)
        state = (state * dec_t[:, :, None, :] + sa[..., None] * rep_t[:, :, None, :]
                 + v_t[..., None] * k_t[:, :, None, :])
        return state, jnp.einsum('bhvk,bhk->bhv', state, r_t)

    tm = lambda t: jnp.swapaxes(t, 0, 1)
    xs = (tm(r), tm(decay), tm(k), tm(v), tm(-kk), tm(kk * a))
    s0 = jnp.zeros((bsz, H, N, N), jnp.float32)
    _, y = lax.scan(step, s0, xs)
    y = tm(y)
    mean = jnp.mean(y, -1, keepdims=True)
    var = jnp.mean(jnp.square(y - mean), -1, keepdims=True)
    y = ((y - mean) * lax.rsqrt(var + LNX_EPS)).reshape(bsz, seq, W) * lnx_g + lnx_b
    bonus = jnp.sum(r * k * r_k.reshape(H, N), -1, keepdims=True) * v
    y = y + bonus.reshape(bsz, seq, W)
    return y * jax.nn.silu(g)

def complex_linear_combine(left, right):
    a1r, a1i, b1r, b1i = left
    a2r, a2i, b2r, b2i = right
    return (a2r * a1r - a2i * a1i, a2r * a1i + a2i * a1r,
            a2r * b1r - a2i * b1i + b2r, a2r * b1i + a2i * b1r + b2i)

def s5_ssm(u, lam_re, lam_im, log_dt, b_re, b_im, c_re, c_im, d, glu_w, glu_b):
    bsz, seq, _ = u.shape
    G, P, N = S5_GROUPS, S5_GROUP, S5_STATE
    u = u.astype(jnp.float32)
    ug = u.reshape(bsz, seq, G, P)
    lam_re = lam_re.astype(jnp.float32)
    lam_im = lam_im.astype(jnp.float32)
    dt = jnp.exp(log_dt.astype(jnp.float32))[:, None]
    mag = jnp.exp(lam_re * dt)
    e_re, e_im = mag * jnp.cos(lam_im * dt), mag * jnp.sin(lam_im * dt)
    den = lam_re * lam_re + lam_im * lam_im
    coef_re = ((e_re - 1.0) * lam_re + e_im * lam_im) / den
    coef_im = (e_im * lam_re - (e_re - 1.0) * lam_im) / den
    bb_re = coef_re[..., None] * b_re - coef_im[..., None] * b_im
    bb_im = coef_re[..., None] * b_im + coef_im[..., None] * b_re
    bu_re = jnp.einsum('blgp,gnp->blgn', ug, bb_re)
    bu_im = jnp.einsum('blgp,gnp->blgn', ug, bb_im)
    a_re = jnp.broadcast_to(e_re, (1, seq, G, N))
    a_im = jnp.broadcast_to(e_im, (1, seq, G, N))
    _, _, x_re, x_im = lax.associative_scan(complex_linear_combine, (a_re, a_im, bu_re, bu_im), axis=1)
    y = jnp.einsum('gpn,blgn->blgp', c_re, x_re) - jnp.einsum('gpn,blgn->blgp', c_im, x_im)
    y = y.reshape(bsz, seq, S5_WIDTH) + d * u
    y = jax.nn.gelu(y)
    return y * jax.nn.sigmoid(y @ glu_w + glu_b)

def rope_tables(positions):
    inv_freq = 1.0 / (ROPE_BASE ** (jnp.arange(0, QK_ROPE, 2, dtype=jnp.float32) / QK_ROPE))
    ang = positions.astype(jnp.float32)[..., None] * inv_freq
    return jnp.cos(ang), jnp.sin(ang)

def apply_rope(t, cos, sin):
    half = t.shape[-1] // 2
    t1, t2 = t[..., :half], t[..., half:]
    return jnp.concatenate([t1 * cos - t2 * sin, t2 * cos + t1 * sin], axis=-1)

def mla_attention(p, cos, sin, q_norm, w_q_up, kv_norm, w_kv_up):
    bsz, seq, _ = p.shape
    H = MLA_HEADS
    p = p.astype(jnp.float32)
    o1, o2, o3 = Q_LORA, Q_LORA + KV_LORA, Q_LORA + KV_LORA + QK_ROPE
    c_q, c_kv, k_pe, g = p[..., :o1], p[..., o1:o2], p[..., o2:o3], p[..., o3:]
    q = (rms_norm(c_q, q_norm) @ w_q_up).reshape(bsz, seq, H, QK_NOPE + QK_ROPE)
    kv = (rms_norm(c_kv, kv_norm) @ w_kv_up).reshape(bsz, seq, H, QK_NOPE + V_HEAD)
    q_nope = q[..., :QK_NOPE]
    q_pe = apply_rope(q[..., QK_NOPE:], cos[:, :, None], sin[:, :, None])
    k_nope, v = kv[..., :QK_NOPE], kv[..., QK_NOPE:]
    k_pe = apply_rope(k_pe, cos, sin)
    n_blk = seq // Q_BLOCK
    blocks = lambda t: jnp.moveaxis(t.reshape(bsz, n_blk, Q_BLOCK, H, t.shape[-1]), 1, 0)
    k_idx = jnp.arange(seq)
    scale = 1.0 / math.sqrt(QK_NOPE + QK_ROPE)

    def attend(inp):
        qn, qp, blk = inp
        s = (jnp.einsum('bqhd,bkhd->bhqk', qn, k_nope)
             + jnp.einsum('bqhd,bkd->bhqk', qp, k_pe)).astype(jnp.float32)
        q_idx = blk * Q_BLOCK + jnp.arange(Q_BLOCK)
        causal = q_idx[:, None] >= k_idx[None, :]
        s = jnp.where(causal, s * scale, -1e30)
        probs = jax.nn.softmax(s, axis=-1)
        return jnp.einsum('bhqk,bkhd->bqhd', probs, v)

    o = lax.map(attend, (blocks(q_nope), blocks(q_pe), jnp.arange(n_blk)))
    o = jnp.moveaxis(o, 0, 1).reshape(bsz, seq, H * V_HEAD)
    return o * jax.nn.silu(g)

def setup_inputs(seed: int = 0) -> dict:
    key = jax.random.key(seed)
    keys = jax.random.split(key, 64)
    counter = [0]

    def nk():
        counter[0] += 1
        return keys[counter[0] - 1]

    def nrm(shape, scale):
        return scale * jax.random.normal(nk(), shape, jnp.float32)

    def gain(shape):
        return 1.0 + nrm(shape, 0.05)

    def unif(shape, lo, hi):
        return jax.random.uniform(nk(), shape, jnp.float32, lo, hi)

    D, NE, NO = D_MODEL, N_EVEN, N_ODD
    x = nrm((BATCH, SEQ, D), 1.0)
    c = nrm((BATCH, D), 1.0)
    positions = (jax.random.randint(nk(), (BATCH, 1), 0, 1024, jnp.int32)
                 + jnp.arange(SEQ, dtype=jnp.int32)[None, :])
    s5_n = jnp.pi * jnp.arange(S5_STATE, dtype=jnp.float32)
    return {
        'x': x, 'c': c, 'positions': positions,
        'ev_ada_w': nrm((NE, D, 3 * D), 0.5 * D ** -0.5),
        'ev_ada_b': nrm((NE, 3 * D), 0.01),
        'ev_norm_pre': gain((NE, D)),
        'ev_norm_post': gain((NE, D)),
        'ev_w_in': nrm((NE, D, EVEN_IN), D ** -0.5),
        'ev_mu': unif((NE, A_IN), 0.0, 1.0),
        'ev_w0': unif((NE, RWKV_WIDTH), -6.0, -1.0),
        'ev_w2': nrm((NE, RWKV_LORA, RWKV_WIDTH), 0.5 * RWKV_LORA ** -0.5),
        'ev_a0': nrm((NE, RWKV_WIDTH), 0.1),
        'ev_a2': nrm((NE, RWKV_LORA, RWKV_WIDTH), 0.5 * RWKV_LORA ** -0.5),
        'ev_k_k': 0.85 + nrm((NE, RWKV_WIDTH), 0.05),
        'ev_k_a': gain((NE, RWKV_WIDTH)),
        'ev_r_k': nrm((NE, RWKV_WIDTH), 0.1),
        'ev_lnx_g': gain((NE, RWKV_WIDTH)),
        'ev_lnx_b': nrm((NE, RWKV_WIDTH), 0.01),
        'ev_lam_re': -0.5 + nrm((NE, S5_GROUPS, S5_STATE), 0.01),
        'ev_lam_im': s5_n + nrm((NE, S5_GROUPS, S5_STATE), 0.01),
        'ev_log_dt': unif((NE, S5_GROUPS), math.log(1e-3), math.log(1e-1)),
        'ev_b_re': nrm((NE, S5_GROUPS, S5_STATE, S5_GROUP), (2.0 * S5_GROUP) ** -0.5),
        'ev_b_im': nrm((NE, S5_GROUPS, S5_STATE, S5_GROUP), (2.0 * S5_GROUP) ** -0.5),
        'ev_c_re': nrm((NE, S5_GROUPS, S5_GROUP, S5_STATE), (2.0 * S5_STATE) ** -0.5),
        'ev_c_im': nrm((NE, S5_GROUPS, S5_GROUP, S5_STATE), (2.0 * S5_STATE) ** -0.5),
        'ev_d': nrm((NE, S5_WIDTH), 1.0),
        'ev_glu_w': nrm((NE, S5_WIDTH, S5_WIDTH), S5_WIDTH ** -0.5),
        'ev_glu_b': nrm((NE, S5_WIDTH), 0.01),
        'ev_w_out': nrm((NE, EVEN_MIX, D), EVEN_MIX ** -0.5),
        'od_ada_w': nrm((NO, D, 3 * D), 0.5 * D ** -0.5),
        'od_ada_b': nrm((NO, 3 * D), 0.01),
        'od_norm_pre': gain((NO, D)),
        'od_norm_post': gain((NO, D)),
        'od_w_in': nrm((NO, D, ODD_IN), D ** -0.5),
        'od_q_norm': gain((NO, Q_LORA)),
        'od_w_q_up': nrm((NO, Q_LORA, MLA_HEADS * (QK_NOPE + QK_ROPE)), Q_LORA ** -0.5),
        'od_kv_norm': gain((NO, KV_LORA)),
        'od_w_kv_up': nrm((NO, KV_LORA, MLA_HEADS * (QK_NOPE + V_HEAD)), KV_LORA ** -0.5),
        'od_w_out': nrm((NO, MLA_WIDTH, D), MLA_WIDTH ** -0.5),
    }

def reference(x, c, positions, ev_ada_w, ev_ada_b, ev_norm_pre, ev_norm_post, ev_w_in, ev_mu,
              ev_w0, ev_w2, ev_a0, ev_a2, ev_k_k, ev_k_a, ev_r_k, ev_lnx_g, ev_lnx_b,
              ev_lam_re, ev_lam_im, ev_log_dt, ev_b_re, ev_b_im, ev_c_re, ev_c_im, ev_d,
              ev_glu_w, ev_glu_b, ev_w_out, od_ada_w, od_ada_b, od_norm_pre, od_norm_post,
              od_w_in, od_q_norm, od_w_q_up, od_kv_norm, od_w_kv_up, od_w_out):
    h = x.astype(jnp.float32)
    cos, sin = rope_tables(positions)
    for i in range(DEPTH):
        j = i // 2
        if i % 2 == 0:
            shift, scale, gate = ada_modulation(c, ev_ada_w[j], ev_ada_b[j])
            z = rms_norm(h, ev_norm_pre[j]) * (1.0 + scale) + shift
            p = z @ ev_w_in[j]
            y_a = rwkv7_time_mix(p[..., :A_IN], ev_mu[j], ev_w0[j], ev_w2[j], ev_a0[j], ev_a2[j],
                                 ev_k_k[j], ev_k_a[j], ev_r_k[j], ev_lnx_g[j], ev_lnx_b[j])
            y_b = s5_ssm(p[..., A_IN:A_IN + S5_WIDTH], ev_lam_re[j], ev_lam_im[j], ev_log_dt[j],
                         ev_b_re[j], ev_b_im[j], ev_c_re[j], ev_c_im[j], ev_d[j],
                         ev_glu_w[j], ev_glu_b[j])
            y_b = y_b * jax.nn.silu(p[..., A_IN + S5_WIDTH:].astype(jnp.float32))
            y = jnp.concatenate([y_a, y_b], axis=-1) @ ev_w_out[j]
            post = ev_norm_post[j]
        else:
            shift, scale, gate = ada_modulation(c, od_ada_w[j], od_ada_b[j])
            z = rms_norm(h, od_norm_pre[j]) * (1.0 + scale) + shift
            p = z @ od_w_in[j]
            y = mla_attention(p, cos, sin, od_q_norm[j], od_w_q_up[j], od_kv_norm[j],
                              od_w_kv_up[j]) @ od_w_out[j]
            post = od_norm_post[j]
        h = h + gate * rms_norm(y, post)
    return h.astype(x.dtype)


_drawn_inputs = setup_inputs


def setup_inputs(seed=0):
    import zlib

    import numpy as np

    out = dict(_drawn_inputs(seed))
    spreads = {}
    factors = {'ev_ada_b': 4.292,
     'ev_norm_post': 3.676,
     'ev_w2': 4.727,
     'ev_a0': 5.068,
     'ev_lnx_g': 4.437,
     'ev_lnx_b': 8.0,
     'ev_lam_re': 64.0,
     'ev_lam_im': 50.72,
     'ev_log_dt': 60.384,
     'ev_b_re': 64.0,
     'ev_b_im': 64.0,
     'ev_c_re': 64.0,
     'ev_c_im': 64.0,
     'ev_glu_b': 41.262,
     'od_ada_b': 4.437,
     'od_norm_pre': 3.44,
     'od_norm_post': 3.769,
     'od_q_norm': 8.0,
     'od_kv_norm': 3.721}
    for name, (base, spread) in spreads.items():
        noise = np.random.default_rng([zlib.crc32(name.encode()), seed]).standard_normal(out[name].shape)
        drawn = base * np.exp(spread * noise) if base else spread * noise
        out[name] = __import__('jax').numpy.asarray(drawn.astype(out[name].dtype))
    for name, factor in factors.items():
        out[name] = (out[name] * factor).astype(out[name].dtype)
    return out
```

```python
import concourse.bass as bass
from concourse import mybir
from contextlib import ExitStack
import numpy as np

F32 = mybir.dt.float32
F32R = mybir.dt.float32r
ALU = mybir.AluOpType
ACT = mybir.ActivationFunctionType
AX = mybir.AxisListType

P = 128
D = 2048
L = 512
KT = D // P
TT = L // P
W = D // 2
FT = W // P
HN = 64
CH = 64
NC = L // CH
LEVELS = 6
DECAY = float(np.exp(-0.5))
G, GP, NS = 64, 16, 64
T8 = P // GP
C8 = L // T8
GB = P // GP
NP = 2 * T8 + 1
MAGIC = 12582912.0
TURN = 6.283185307179586
TURN_A = 6.28125
TURN_B = TURN - TURN_A
SAFE_TURN = 6.283185
EPS = 1e-6
LNX_EPS = 64e-5
H = 16
SCALE = 192 ** -0.5
PIECE = 2048
QUARTER = 3 * D // 4

P_IN0 = 0
P_GLU = P_IN0 + 1 + 24 * 2
P_OUT0 = P_GLU + 4
P_IN1 = P_OUT0 + 16
P_UP = P_IN1 + 1 + 12 * 2
P_OUT1 = P_UP + 16
N_PIECES = P_OUT1 + 16

VECTORS = (("c", 16), ("mu", 33), ("pre0", 16), ("ab0", 32), ("w0", 8), ("a0", 8),
           ("kk", 8), ("ka", 8), ("rk", 8), ("lnxg", 8), ("lnxb", 8), ("glub", 8),
           ("pre1", 16), ("ab1", 32), ("qn", 4), ("kvn", 4))
COLS, NCOLS = {}, 0
for _name, _n in VECTORS:
    COLS[_name] = (NCOLS, _n)
    NCOLS += _n


class Chain:

    def __init__(self, eng, sem):
        self.eng, self.sem, self.base, self.n = eng, sem, 0, 0

    def __call__(self, ins):
        ins.then_inc(self.sem, 1)
        self.n += 1

    def at(self):
        return self.base + self.n

    def wait(self):
        self.eng.wait_ge(self.sem, self.base + self.n)

    def enter(self, i, per, first=0):
        self.saved, self.per = self.base + self.n, per
        self.base, self.n = i * per + (self.saved - first * per), 0

    def leave(self, turns):
        assert self.n == self.per, (self.n, self.per)
        self.base, self.n = self.saved + turns * self.per, 0


class Banks:

    def __init__(self, banks):
        self.banks, self.jobs = banks, []

    def add(self, key, reader):
        self.jobs.append((key, reader))

    def number(self, key):
        return [k for k, _ in self.jobs].index(key) + 1

    def reader(self, key):
        return dict(self.jobs)[key]

    def reads(self, key):
        who = self.reader(key)
        return [k for k, r in self.jobs if r == who].index(key) + 1

    def total(self, who):
        return sum(r == who for _, r in self.jobs)

    def bank(self, key):
        return self.banks[(self.number(key) - 1) % len(self.banks)]

    def before(self, key):
        n = self.number(key) - 1 - len(self.banks)
        return self.jobs[n][0] if n >= 0 else None


def rwkv_jobs():
    jobs = Banks(range(6))
    for u in range(2):
        jobs.add(("decay", u), "act")
        jobs.add(("rate", u), "act")
    for u in range(2):
        jobs.add(("norm", u), "dve")
    for u in range(2):
        jobs.add(("bonus", u), "dve")
    for u in range(2):
        for x in "bk":
            for c in range(0, NC, 2):
                jobs.add(("pairs", x, u, c), "dve")
        for x in "bkv":
            for c in range(0, NC, 4):
                jobs.add(("turn", x, u, c), "act")
    for n in range(LEVELS):
        for u in range(2):
            for c in range(0, NC, 4):
                jobs.add(("at", n, u, c), "dve")
        for u in range(2):
            for c in range(0, NC, 4):
                if n < LEVELS - 1:
                    jobs.add(("inv", n, u, c), "dve")
                jobs.add(("invT", n, u, c), "dve")
    for c in range(NC):
        for x, who in (("w", "act"), ("u", "act"), ("s", "dve")):
            for u in range(2):
                jobs.add((x, c, u), who)
    for x in ("mean", "var"):
        for u in range(2):
            jobs.add((x, u), "dve" if x == "mean" else "act")
    return jobs


def s5_jobs():
    jobs = Banks(range(8))
    for key in ("uc", "wv0", "wv1", "k0", "k1", "v", "vs", "zs", "y0", "y1", "yt"):
        jobs.add(key, "dve" if key in ("vs", "zs", "k0", "k1") else "act")
    return jobs


def attention_jobs():
    jobs = Banks(range(6))
    for a in range(2):
        jobs.add(("qn", a), "act")
        jobs.add(("qp", a), "dve")
        jobs.add(("key", a), "act")
    for n in range(2):
        jobs.add(("v", n), "act")
    for x, who in (("s", "act"), ("pt", "dve")):
        for a in range(2):
            for b in range(TT):
                jobs.add((x, a, b), who)
    assert len(jobs.jobs) % 6 == 0
    return jobs


def trunk(nc, A, out):
    ctx = ExitStack()
    with ctx:
        slab_bytes = (nc.sbuf_usable_end - nc.sbuf_base - 1024) // 32 * 32
        slab = nc.alloc_sbuf_tensor("slab", [P, slab_bytes // 4], F32)
        start = nc.sbuf_base - slab_bytes
        top = [start]

        def sb(name, shape, dt=F32):
            size = 4
            for n in shape[1:]:
                size *= n
            here = top[0]
            top[0] += (size + 31) // 32 * 32
            assert top[0] <= start + slab_bytes, (name, top[0] - start - slab_bytes)
            return nc.alloc_sbuf_tensor_at(name, shape, dt, offset=here)

        def sem(name):
            return ctx.enter_context(nc.semaphore(name))

        def dram(name, shape):
            return nc.dram_tensor(name, shape, F32).ap()

        mixed_d = dram("mixed_d", [16, 2, P, L])
        sgate_d = dram("sgate_d", [4, 2, P, L])
        mix_d = dram("mix_d", [8, 2, P, L])
        gy_d = dram("gy_d", [FT, P, L])
        h1_d = dram("h1_d", [L, D])
        u_d = dram("u_d", [L, W])

        raw = [sb(f"raw{s}", [P, PIECE]) for s in range(2)]
        whi = [sb(f"whi{s}", [P, PIECE], F32R) for s in range(2)]
        wlo = [sb(f"wlo{s}", [P, PIECE], F32R) for s in range(2)]
        cols = sb("cols", [P, NCOLS])
        ident = sb("ident", [P, P])
        ones = sb("ones", [P, P])
        csilu = sb("csilu", [P, 16])
        modc = [sb(f"modc{i}", [P, 32]) for i in range(2)]
        small = sb("small", [P, 16])
        gp = [sb("gp0", [P, D]), None]
        keep = top[0]

        xt = sb("xt", [P, TT, D])
        post_b = sb("post_b", [P, D])
        top1 = top[0]
        top[0] = keep
        gp[1] = sb("gp1", [P, D])
        lo_in = sb("lo_in", [P, L])
        shift = sb("shift", [P, 2, L + 1])
        res = [sb(f"res{s}", [P, 2, L]) for s in range(2)]
        ures = [sb(f"ures{s}", [P, TT, 256]) for s in range(2)]
        assert top[0] <= top1
        keep2 = keep + (D + L) * 4
        top[0] = top1
        ztmp = sb("ztmp", [P, 2, L])
        acc = sb("acc", [P, 4, QUARTER])
        ada = [sb(f"ada{s}", [P, QUARTER]) for s in range(2)]
        zh = sb("zh", [P, KT, L], F32R)
        zl = sb("zl", [P, KT, L], F32R)

        top[0] = keep2
        blk1 = sb("blk1", [P, P])
        starts = sb("starts", [P, L])
        tri = sb("tri", [P, 3 * CH])
        corner = sb("corner", [P, LEVELS, P])
        two = lambda name, shape: [sb(f"{name}{u}", shape) for u in range(2)]
        rkv = two("rkv", [P, 3, L])
        lora = two("lora", [P, 2, P])
        sg = two("sg", [P, L])
        rate = two("rate", [P, L])
        cum = two("cum", [P, L])
        grow = two("grow", [P, NC, CH + 1])
        bonus = two("bonus", [P, L])
        ra = two("ra", [P, NC, 3 * CH])
        wu = two("wu", [P, 2, P])
        state = two("state", [P, 2, P])
        b_t, k_t, v_t = two("b_t", [P, NC, P]), two("k_t", [P, NC, P]), two("v_t", [P, NC, P])
        here = top[0]
        shrink = two("shrink", [P, L])
        kn, sq, root = two("kn", [P, L]), two("sq", [P, L]), two("root", [P, L])
        kp, bv = two("kp", [P, L]), two("bv", [P, L])
        top[0] = here
        rb, rk = two("rb", [P, NC, 3 * CH]), two("rk_", [P, NC, 3 * CH])
        b_d, k_d, v_d = two("b_d", [P, NC, P]), two("k_d", [P, NC, P]), two("v_d", [P, NC, P])
        inv, at_inv, inv_t = b_d, k_d, v_d
        rj = rwkv_jobs()

        top[0] = keep2
        swap = sb("swap", [P, P])
        sign = sb("sign", [P, 2])
        expo = sb("expo", [P, NP])
        count = sb("count", [P, C8])
        lam = sb("lam", [P, 3, G])
        d_row = sb("d_row", [GP, G, GP])
        bc = sb("bc", [P, 4, G, GP])
        e1 = [sb(f"e1_{n}", [P, G]) for n in range(12)]
        pw_re, pw_im, pt1, pt2 = (sb(n, [P, NP, G]) for n in ("pw_re", "pw_im", "pt1", "pt2"))
        turn8, mag8 = sb("turn8", [P, G]), sb("mag8", [P, G])
        bb = [sb(f"bb{n}", [P, GB, GP]) for n in range(2)]
        cosc, sinc, decay8 = (sb(n, [P, GB, C8]) for n in ("cosc", "sinc", "decay8"))
        t5a, t5b = sb("t5a", [P, GB, C8]), sb("t5b", [P, GB, C8])
        wvt = sb("wvt", [P, GB, T8, GP])
        wvt2 = sb("wvt2", [P, GB, T8 + 1, GP])
        wc = sb("wc", [P, GB, T8 + 1, GP])
        wv = sb("wv", [P, GB, P])
        w3 = sb("w3", [P, GB, P])
        kpad = sb("kpad", [GP, GB, 2 * P])
        ucm = sb("ucm", [C8, T8, P])
        ugm = sb("ugm", [C8, GB, P])
        uc = sb("uc", [P, GB, C8])
        vin, zst, xst = (sb(n, [P, GB, C8]) for n in ("vin", "zst", "xst"))
        ycm = sb("ycm", [C8, T8, P])
        gy_out = sb("gy_out", [P, L])
        sj = s5_jobs()

        top[0] = keep2
        gy = sb("gy", [P, FT, L])
        gsig = [sb(f"gsig{s}", [P, 2, L]) for s in range(2)]
        sgt = [sb(f"sgt{s}", [P, 2, L]) for s in range(2)]
        assert top[0] <= keep + 80 * 1024

        top[0] = keep2
        x6 = sb("x6", [P, TT, D])
        y6 = sb("y6", [P, TT, D])
        ztmp6 = sb("ztmp6", [P, 2, L])
        assert top[0] <= keep + 80 * 1024

        top[0] = keep2
        sg1 = sb("sg1", [P, H, L])
        key_pe = sb("key_pe", [P, L])
        rot = sb("rot", [P, L])
        rope_c = sb("rope_c", [P, 2])
        fold = sb("fold", [P, P])
        here = top[0]
        cq = sb("cq", [P, 8, L])
        ktmp = sb("ktmp", [P, L])
        pos = sb("pos", [P, L], mybir.dt.int32)
        r1, r2, rms_kv = sb("r1", [P, L]), sb("r2", [P, L]), sb("rms_kv", [P, L])
        assert top[0] <= keep + 80 * 1024
        top[0] = here
        probs = [sb(f"probs{a}", [P, TT, L]) for a in range(2)]
        qn, qp, key9 = ([sb(f"{n}{a}", [P, L]) for a in range(2)] for n in ("qn", "qp", "key"))
        v9 = sb("v9", [P, TT, 2 * P])
        assert top[0] <= keep + 80 * 1024
        top[0] = keep + 144 * 1024
        pt9 = [sb(f"pt9{n}", [P, L]) for n in range(2)]
        neg_tri = sb("neg_tri", [P, P])
        stat = sb("stat", [P, 3, 8])
        aj = attention_jobs()

        ps = [ctx.enter_context(nc.psum_tensor(f"ps{i}", [P, 512], F32)) for i in range(8)]

        def col(name, i, n=1):
            o = COLS[name][0]
            return cols[:, o + i:o + i + n]

        def rcol(name, i, j=0, step=1, rows=slice(0, P)):
            o, n = COLS[name]
            return cols[rows, o:o + n // step * step].rearrange("p (a b) -> p a b", b=step)[:, i, j:j + 1]

        raw_full = [sem(f"raw_full{s}") for s in range(2)]
        hi_ready, lo_ready, piece_used = sem("hi_ready"), sem("lo_ready"), sem("piece_used")
        phase_over = sem("phase_over")
        dve_chain, act_chain = sem("dve_chain"), sem("act_chain")
        cols_in, ident_in, x_in, gb_in = sem("cols_in"), sem("ident_in"), sem("x_in"), sem("gb_in")
        consts_set, csilu_set = sem("consts_set"), sem("csilu_set")
        ada_full = [sem(f"ada_full{s}") for s in range(2)]
        ada_used = sem("ada_used")
        acc_ready, mod_sums, mod_ready = sem("acc_ready"), sem("mod_sums"), sem("mod_ready")
        x_normed, x_turned, z_scaled = sem("x_normed"), sem("x_turned"), sem("z_scaled")
        z_ready, root_done = sem("z_ready"), sem("root_done")
        proj_out = sem("proj_out")
        mixed = sem("mixed")
        res_stored = [sem(f"res_stored{s}") for s in range(2)]
        u_stored = [sem(f"u_stored{s}") for s in range(2)]

        mask_in = sem("mask_in")
        pair_in = [sem(f"pair_in{u}") for u in range(2)]
        r_job, r_dve, r_act = sem("r_job"), sem("r_dve"), sem("r_act")
        key_squared, cum_done, exp_done, norm_max = (sem(n) for n in (
            "key_squared", "cum_done", "exp_done", "norm_max"))
        norm_root, bonus_in, operands, v_blocks, state_zero = (sem(n) for n in (
            "norm_root", "bonus_in", "operands", "v_blocks", "state_zero"))
        y_out, y_centred, y_squared, y_root = (sem(n) for n in (
            "y_out", "y_centred", "y_squared", "y_root"))
        y_ready, y_copied = sem("y_ready"), sem("y_copied")
        mix_stored = sem("mix_stored")

        s5_in, ucm_in, kpad_ready, u_grouped = sem("s5_in"), sem("ucm_in"), sem("kpad_ready"), sem("u_grouped")
        s_job, s_dve, s_act = sem("s_job"), sem("s_dve"), sem("s_act")
        s5_angle, s5_sine, s5_mag = sem("s5_angle"), sem("s5_sine"), sem("s5_mag")
        w_ready, x_ready, w3_in = sem("w_ready"), sem("x_ready"), sem("w3_in")
        gy_stored, gy_in, sgt_in = sem("gy_stored"), sem("gy_in"), [sem(f"sgt_in{s}") for s in range(2)]
        gy_split, glu_out, glu_mixed = sem("gy_split"), sem("glu_out"), sem("glu_mixed")
        glu_stored = [sem(f"glu_stored{s}") for s in range(2)]

        mix_in, mix_split, out_read, h_in = (sem(n) for n in ("mix_in", "mix_split", "out_read", "h_in"))
        h_ready, h_stored = sem("h_ready"), sem("h_stored")
        rope_in, angle, rope_sine = sem("rope_in"), sem("angle"), sem("rope_sine")
        in1_read, key_rotated, key_folded = (sem(n) for n in (
            "in1_read", "key_rotated", "key_folded"))
        c_squared, c_summed, c_root, c_split = (sem(n) for n in (
            "c_squared", "c_summed", "c_root", "c_split"))
        a_job, a_act, a_dve = sem("a_job"), sem("a_act"), sem("a_dve")
        max_ready, probs_ready, o_ready, o_read = (sem(n) for n in (
            "max_ready", "probs_ready", "o_ready", "o_read"))

        block = ctx.enter_context(nc.Block())

        def load_piece(sp, k, n):
            s = n % 2
            if isinstance(k, int) and k == 0 and n < 2:
                pass
            else:
                sp.wait_ge(hi_ready, k * 2 + (n - 1))
                sp.wait_ge(lo_ready, k * 2 + (n - 1))
            sp.dma_start(raw[s][:, :], A["ws"][k + n // 2, s]).then_inc(raw_full[s], 16)

        def split_hi(act, k, n):
            s = n % 2
            act.wait_ge(raw_full[s], k * 16 + (n // 2 + 1) * 16)
            if not (isinstance(k, int) and k == 0 and n < 2):
                act.wait_ge(piece_used, k * 2 + (n - 1))
            act.activation(whi[s][:, :], raw[s][:, :], ACT.Copy).then_inc(hi_ready, 1)

        def split_lo(pool, k, n):
            s = n % 2
            pool.wait_ge(hi_ready, k * 2 + (n + 1))
            pool.tensor_tensor(wlo[s][:, :], raw[s][:, :], whi[s][:, :].bitcast(F32),
                               ALU.subtract).then_inc(lo_ready, 1)

        def piece_ready(pe, k, n):
            pe.wait_ge(hi_ready, k * 2 + (n + 1))
            pe.wait_ge(lo_ready, k * 2 + (n + 1))

        def over(eng, n):
            eng.drain().then_inc(phase_over, 1)
            eng.wait_ge(phase_over, 3 * n)

        def load_ada(sp, layer, k, q):
            s = q % 2
            if not (isinstance(k, int) and k == 0 and q < 2 and layer == 0):
                sp.wait_ge(ada_used, k * 4 + (64 * layer + q - 1))
            sp.dma_start(ada[s][:, :], A["ada"][layer, k, q]).then_inc(ada_full[s], 16)

        @block.sync
        def _(sp):
            sp.dma_start(cols[:, :], A["cols"]).then_inc(cols_in, 16)
            sp.dma_start(ident[:, :], A["ident"]).then_inc(ident_in, 16)
            for q in range(4):
                load_ada(sp, 0, 0, q)
            sp.dma_start(xt[:, :, :], A["x"].rearrange("(a p) d -> p a d", p=P)).then_inc(x_in, 16)
            with sp.Fori(1, KT) as k:
                for q in range(4):
                    load_ada(sp, 0, k, q)
            load_piece(sp, 0, 0)
            load_piece(sp, 0, 1)
            load_piece(sp, 0, 2)
            sp.wait_ge(phase_over, 3)
            sp.dma_start(post_b[:, :], A["rows"][3].partition_broadcast(P)).then_inc(gb_in, 16)
            sp.dma_start(gp[1][:, :], A["rows"][2].partition_broadcast(P)).then_inc(gb_in, 16)
            with sp.Fori(0, KT) as g:
                load_piece(sp, g, 3)
                load_piece(sp, g, 4)
                for q in range(4):
                    load_ada(sp, 1, g, q)
            with sp.Fori(KT, (P_GLU - 1) // 2) as g:
                load_piece(sp, g, 3)
                load_piece(sp, g, 4)
            sp.wait_ge(phase_over, 6)
            for s in range(2):
                sp.wait_ge(res_stored[s], 16 * 10)
                sp.wait_ge(u_stored[s], 32)
            for name, buf in (("blk1", blk1), ("starts", starts), ("tri", tri), ("corner", corner)):
                sp.dma_start(buf[...], A[name]).then_inc(mask_in, 16)
            with sp.Fori(0, FT // 2) as k:
                sp.wait_ge(phase_over, k * 3 + 6)
                for u in range(2):
                    sp.dma_start(rkv[u][:, :, :], mixed_d.rearrange("(a b) u p t -> b u p a t", a=4)
                                 [k, u, :, 0:3]).then_inc(pair_in[u], 16)
                    sp.dma_start(lora[u][:, :, :], A["lora"][k, u]).then_inc(pair_in[u], 16)
                    sp.dma_start(sg[u][:, :], mixed_d.rearrange("(a b) u p t -> b u p a t", a=4)
                                 [k, u, :, 3]).then_inc(pair_in[u], 16)
            sp.wait_ge(phase_over, 3 * 6)
            for buf, src in ((swap, "swap"), (sign, "sign"), (expo, "expo"), (count, "count"),
                             (lam, "lam"), (bc, "bc")):
                sp.dma_start(buf[...], A[src]).then_inc(s5_in, 16)
            sp.dma_start(d_row[:, :, :].rearrange("p g q -> p (g q)"),
                         A["d"].partition_broadcast(GP)).then_inc(s5_in, 16)

            def skewed(sp, b):
                sp.wait_ge(kpad_ready, b + 1)
                for i in range(T8):
                    sp.dma_start(w3[i * GP:(i + 1) * GP, :, :], kpad[:, :, P - i * GP:2 * P - i * GP])\
                      .then_inc(w3_in, 16)

            sp.dma_start(ucm[:, :, :], u_d.rearrange("(c j) (b f) -> b c j f", j=T8, f=P)[0])\
              .then_inc(ucm_in, 16)
            with sp.Fori(0, FT - 1) as b:
                skewed(sp, b)
                sp.wait_ge(u_grouped, b + 1)
                sp.dma_start(ucm[:, :, :], u_d.rearrange("(c j) (b f) -> b c j f", j=T8, f=P)[b + 1])\
                  .then_inc(ucm_in, 16)
            skewed(sp, FT - 1)
            sp.wait_ge(phase_over, 3 * 7)
            sp.dma_start(gy[:, :, :], gy_d.rearrange("f p t -> p f t")).then_inc(gy_in, 16)
            for n in range(4):
                if n >= 2:
                    sp.wait_ge(glu_mixed, n - 1)
                sp.dma_start(sgt[n % 2][:, :, :], sgate_d[n].rearrange("j p t -> p j t"))\
                  .then_inc(sgt_in[n % 2], 16)
                load_piece(sp, 0, P_GLU + 2 + n)
            for s in range(2):
                sp.wait_ge(glu_stored[s], 32)

            sp.wait_ge(phase_over, 3 * 8)
            sp.dma_start(y6[:, :, :].rearrange("p a (b t) -> p (a b) t", t=L),
                         mix_d.rearrange("a u p t -> p (a u) t")).then_inc(mix_in, 16)
            sp.dma_start(x6[:, :, :], A["x"].rearrange("(a p) d -> p a d", p=P)).then_inc(h_in, 16)
            with sp.Fori(0, 8) as k:
                load_piece(sp, k, P_OUT0 + 2)
                load_piece(sp, k, P_OUT0 + 3)
            sp.wait_ge(h_ready, 1)
            sp.dma_start(h1_d.rearrange("(a p) d -> p a d", p=P), x6[:, :, :]).then_inc(h_stored, 16)
            sp.wait_ge(phase_over, 3 * 10)
            sp.wait_ge(h_stored, 16)
            sp.dma_start(pos[:, :], A["pos"].partition_broadcast(P)).then_inc(rope_in, 16)
            sp.dma_start(rope_c[:, :], A["rope_c"]).then_inc(rope_in, 16)
            sp.dma_start(fold[:, :], A["fold"]).then_inc(rope_in, 16)
            sp.dma_start(neg_tri[:, :], A["neg_tri"]).then_inc(rope_in, 16)
            load_piece(sp, 0, P_IN1 + 2)
            with sp.Fori(0, 12) as k:
                load_piece(sp, k, P_IN1 + 3)
                load_piece(sp, k, P_IN1 + 4)
            with sp.Fori(0, 8) as k:
                load_piece(sp, k, P_UP + 2)
                load_piece(sp, k, P_UP + 3)
            sp.wait_ge(mix_split, 2 * KT)
            sp.dma_start(x6[:, :, :], h1_d.rearrange("(a p) d -> p a d", p=P)).then_inc(h_in, 16)
            with sp.Fori(0, 7) as k:
                load_piece(sp, k, P_OUT1 + 2)
                load_piece(sp, k, P_OUT1 + 3)
            sp.wait_ge(h_ready, 2)
            sp.dma_start(out[0].rearrange("(a p) d -> p a d", p=P), x6[:, :, :]).then_inc(h_stored, 16)
            sp.wait_ge(h_stored, 32)

        @block.gpsimd
        def _(pool):
            pool.memset(ones[:, :], 1.0).then_inc(consts_set, 1)
            with pool.Fori(0, N_PIECES // 2) as k:
                split_lo(pool, k, 0)
                split_lo(pool, k, 1)

        @block.scalar
        def _(act):
            ch = Chain(act, act_chain)
            act.dma_start(post_b[:, :], A["rows"][1].partition_broadcast(P)).then_inc(gb_in, 16)
            act.dma_start(gp[0][:, :], A["rows"][0].partition_broadcast(P)).then_inc(gb_in, 16)
            act.wait_ge(cols_in, 16)
            act.activation(csilu[:, :], col("c", 0, 16), ACT.Silu).then_inc(csilu_set, 1)

            def norm_stage(layer, xt, ztmp):
                if layer == 0:
                    act.wait_ge(x_in, 16)
                else:
                    act.wait_ge(h_ready, 1)
                for t in range(TT):
                    ch(act.activation(zl[:, 4 * t:4 * t + 4, :].rearrange("p a b -> p (a b)"), xt[:, t, :],
                                      ACT.Square, accum_out=small[:, t:t + 1]))
                ch.wait()
                act.activation(small[:, 4:8], small[:, 0:4], ACT.Sqrt, bias=EPS,
                               scale=1.0 / D).then_inc(root_done, 1)
                act.wait_ge(mod_ready, layer + 1)
                for k in range(KT):
                    act.wait_ge(x_turned, KT * layer + k + 1)
                    if k >= 2:
                        act.wait_ge(z_ready, KT * layer + k - 1)
                    act.activation(ztmp[:, k % 2, :], ps[2 + k % 2][:, :], ACT.Identity,
                                   bias=modc[layer][:, k:k + 1],
                                   scale=modc[layer][:, 16 + k:17 + k]).then_inc(z_scaled, 1)

            norm_stage(0, xt, ztmp)
            split_hi(act, 0, 0)
            over(act, 1)

            split_hi(act, 0, 1)
            act.wait_ge(piece_used, 1)
            act.activation(shift[:, 0, 1:257], ps[7][:, 0:256], ACT.Copy).then_inc(proj_out, 1)
            act.activation(shift[:, 0, 257:], ps[7][:, 256:], ACT.Copy).then_inc(proj_out, 1)
            split_hi(act, 0, 2)
            act.wait_ge(mixed, 1)
            act.activation(lo_in[0:64, :], lo_in[0:64, :], ACT.Tanh)

            def copy_group(k, u):
                split_hi(act, k * 2, 2 * u + 3)
                split_hi(act, k * 2, 2 * u + 4)
                act.wait_ge(piece_used, k * 4 + (2 * u + 3))
                act.wait_ge(mixed, k * 2 + (u + 1))
                ch(act.activation(shift[:, 0, 1:], ps[2 * u][:, :], ACT.Copy))
                act.activation(shift[:, 1, 1:], ps[2 * u + 1][:, :], ACT.Copy).then_inc(proj_out, 1)

            def store_group(k, u, silu):
                act.wait_ge(mixed, k * 2 + (u + 2))
                if silu:
                    ch(act.activation(res[u][:, :, :], res[u][:, :, :], ACT.Silu))
                    ch.wait()
                act.dma_start(mixed_d[k * 2 + u].rearrange("j p t -> p j t"),
                              res[u][:, :, :]).then_inc(res_stored[u], 16)

            with act.Fori(0, 6) as k:
                ch.enter(k, 2)
                for u in range(2):
                    copy_group(k, u)
                    store_group(k, u, False)
                ch.leave(6)
            with act.Fori(6, 8) as k:
                ch.enter(k, 4, 6)
                for u in range(2):
                    copy_group(k, u)
                    store_group(k, u, True)
                ch.leave(2)
            def u_group(k, u, first):
                split_hi(act, k * 2, 2 * u + 3)
                split_hi(act, k * 2, 2 * u + 4)
                act.wait_ge(piece_used, k * 4 + (2 * u + 3))
                if not first:
                    act.wait_ge(u_stored[u], (k - 8) * 16)
                for t in range(TT):
                    o = act.activation(ures[u][:, t, :], ps[4 - 4 * u + t][:, 0:256], ACT.Copy)
                    if t < TT - 1:
                        ch(o)
                o.then_inc(proj_out, 1)
                ch.wait()
                act.wait_ge(proj_out, k * 2 + (u + 3))
                act.dma_start(u_d.rearrange("(a p) (g w) -> g p a w", p=P, w=256)[(k - 8) * 2 + u],
                              ures[u][:, :, :]).then_inc(u_stored[u], 16)

            for k in range(8, 10):
                for u in range(2):
                    u_group(k, u, k == 8)
            for k in range(10, 12):
                for u in range(2):
                    if k * 4 + 2 * u + 4 < P_GLU:
                        split_hi(act, k * 2, 2 * u + 3)
                        split_hi(act, k * 2, 2 * u + 4)
                    act.wait_ge(piece_used, k * 4 + (2 * u + 3))
                    act.wait_ge(res_stored[u], 16 * (k - 2))
                    ch(act.activation(res[u][:, 0, :], ps[4 + 2 * u][:, :], ACT.Silu))
                    act.activation(res[u][:, 1, :], ps[5 + 2 * u][:, :], ACT.Silu).then_inc(proj_out, 1)
                    ch.wait()
                    act.wait_ge(proj_out, k * 2 + (u + 3))
                    act.dma_start(sgate_d[(k - 10) * 2 + u].rearrange("j p t -> p j t"),
                                  res[u][:, :, :]).then_inc(res_stored[u], 16)
            over(act, 2)

            act.wait_ge(state_zero, 6)
            with act.Fori(0, FT // 2) as k:
                ch.enter(k, 2)

                def job(key):
                    act.wait_ge(r_job, k * len(rj.jobs) + rj.number(key))
                    return ps[rj.bank(key)]

                for u in range(2):
                    act.wait_ge(pair_in[u], k * 48 + 48)
                    act.activation(sq[u][:, :], rkv[u][:, 1, :], ACT.Square,
                                   scale=rcol("kk", k, u, 2)).then_inc(key_squared, 1)
                for u in range(2):
                    b = job(("decay", u))
                    act.activation(cum[u][:, :], b[:, :], ACT.Sigmoid,
                                   bias=rcol("w0", k, u, 2)).then_inc(r_act, 1)
                    b = job(("rate", u))
                    act.activation(rate[u][:, :], b[:, :], ACT.Sigmoid,
                                   bias=rcol("a0", k, u, 2)).then_inc(r_act, 1)
                for u in range(2):
                    for h in range(2):
                        act.activation(
                            v_d[u][64 * h:64 * h + 64, :, 64 * h:64 * h + 64],
                            rkv[u][64 * h:64 * h + 64, 2, :].rearrange("p (c t) -> p c t", c=NC),
                            ACT.Copy).then_inc(v_blocks, 1)
                for u in range(2):
                    act.wait_ge(norm_max, k * 2 + (u + 1))
                    act.activation(root[u][:, :], root[u][:, :], ACT.Sqrt).then_inc(norm_root, 1)
                for u in range(2):
                    act.wait_ge(cum_done, k * 2 + (u + 1))
                    ch(act.activation(grow[u][:, :, 1:], cum[u][:, :].rearrange(
                        "p (c t) -> p c t", c=NC), ACT.Exp))
                    act.activation(shrink[u][:, :], cum[u][:, :], ACT.Exp, scale=-1.0)\
                       .then_inc(exp_done, 1)
                for u in range(2):
                    for x, to in (("b", b_t), ("k", k_t), ("v", v_t)):
                        for c in range(0, NC, 4):
                            b = job(("turn", x, u, c))
                            act.activation(to[u][:, c:c + 4, :].rearrange("p c s -> p (c s)"),
                                           b[:, :], ACT.Copy).then_inc(r_act, 1)
                for c in range(NC):
                    for n, x in enumerate("wu"):
                        for u in range(2):
                            b = job((x, c, u))
                            act.activation(wu[u][:, n, :], b[:, 0:P], ACT.Copy).then_inc(r_act, 1)
                for u in range(2):
                    act.wait_ge(y_centred, k * 2 + (u + 1))
                    act.activation(sq[u][:, :], cum[u][:, :], ACT.Square).then_inc(y_squared, 1)
                for u in range(2):
                    b = job(("var", u))
                    act.activation(root[u][:, :], b[:, :], ACT.Sqrt, bias=LNX_EPS,
                                   scale=1.0 / HN).then_inc(r_act, 1)
                for u in range(2):
                    act.wait_ge(y_ready, k * 2 + (u + 1))
                    act.dma_start(mix_d[k, u], cum[u][:, :]).then_inc(mix_stored, 16)
                over(act, k + 3)
                act.wait_ge(mix_stored, k * 32 + 32)
                ch.leave(FT // 2)

            act.wait_ge(s5_in, 16 * 7)
            act.activation(e1[0][:, :], lam[:, 2, :], ACT.Exp).then_inc(s5_mag, 1)
            act.wait_ge(s5_angle, 1)
            act.activation(e1[3][:, :], e1[1][:, :], ACT.Exp).then_inc(s5_mag, 1)
            act.activation(pt1[:, :, :], pw_re[:, :, :], ACT.Exp).then_inc(s5_mag, 1)
            act.activation(mag8[:, :], mag8[:, :], ACT.Exp).then_inc(s5_mag, 1)
            act.activation(e1[4][:, :], e1[2][:, :], ACT.Sin, scale=SAFE_TURN).then_inc(s5_sine, 1)
            act.activation(e1[5][:, :], e1[2][:, :], ACT.Sin, scale=SAFE_TURN / 2).then_inc(s5_sine, 1)
            act.activation(pt2[:, :, :], pw_im[:, :, :], ACT.Sin, scale=SAFE_TURN / 2).then_inc(s5_sine, 1)
            act.wait_ge(s5_sine, 3)
            act.activation(pw_im[:, :, :], pw_im[:, :, :], ACT.Sin, scale=SAFE_TURN).then_inc(s5_sine, 1)
            with act.Fori(0, FT) as b:
                ch.enter(b, 1)

                def job5(key):
                    act.wait_ge(s_job, b * len(sj.jobs) + sj.number(key))
                    return ps[sj.bank(key)]

                act.wait_ge(ucm_in, b * 16 + 16)
                act.activation(ugm[:, :, :].rearrange("c g (j p) -> c j g p", j=T8),
                               ucm[:, :, :].rearrange("c j (g p) -> c j g p", g=GB),
                               ACT.Copy).then_inc(u_grouped, 1)
                act.wait_ge(s5_angle, b + 2)
                ch(act.activation(cosc[:, :, :], t5a[:, :, :], ACT.Sin, scale=SAFE_TURN / 2))
                act.activation(sinc[:, :, :], t5a[:, :, :], ACT.Sin, scale=SAFE_TURN).then_inc(s5_sine, 1)
                p = job5("uc")
                act.activation(uc[:, :, :].rearrange("p g c -> p (g c)"), p[:, :], ACT.Copy).then_inc(s_act, 1)
                for n in range(2):
                    p = job5(f"wv{n}")
                    act.activation(wv[:, 4 * n:4 * n + 4, :].rearrange("p g c -> p (g c)"), p[:, :],
                                   ACT.Copy).then_inc(s_act, 1)
                p = job5("v")
                act.activation(vin[:, :, :].rearrange("p g c -> p (g c)"), p[:, :], ACT.Copy).then_inc(s_act, 1)
                for n in range(2):
                    p = job5(f"y{n}")
                    act.activation(
                        ycm[:, :, 64 * n:64 * n + 64].rearrange("c j (g p) -> c j g p", p=GP),
                        p[0:C8, :].rearrange("c (g j p) -> c j g p", g=4, p=GP), ACT.Copy).then_inc(s_act, 1)
                p = job5("yt")
                act.activation(gy_out[:, :].rearrange("p (c j) -> p c j", j=T8),
                               p[:, :].rearrange("p (j c) -> p c j", c=C8),
                               ACT.Gelu_apprx_tanh).then_inc(s_act, 1)
                act.wait_ge(s_act, b * sj.total("act") + sj.reads("yt"))
                act.dma_start(gy_d[b], gy_out[:, :]).then_inc(gy_stored, 16)
                act.wait_ge(gy_stored, b * 16 + 16)
                ch.leave(FT)
            over(act, 7)

            for n in range(4):
                u = n % 2
                split_hi(act, 0, P_GLU + n)
                act.wait_ge(piece_used, P_GLU + n + 1)
                if n >= 2:
                    act.wait_ge(glu_mixed, n - 1)
                    act.wait_ge(glu_stored[u], 16)
                ch(act.activation(gsig[u][:, 0, :], ps[2 * u][:, :], ACT.Sigmoid, bias=col("glub", 2 * n)))
                act.activation(gsig[u][:, 1, :], ps[2 * u + 1][:, :], ACT.Sigmoid,
                               bias=col("glub", 2 * n + 1)).then_inc(glu_out, 1)
                act.wait_ge(glu_mixed, n + 1)
                act.dma_start(mix_d[4 + n].rearrange("j p t -> p j t"), gsig[u][:, :, :])\
                   .then_inc(glu_stored[u], 16)
            for s in range(2):
                act.wait_ge(glu_stored[s], 32)
            over(act, 8)

            def out_group(layer, k, u, last=False):
                first = (P_OUT0, P_OUT1)[layer] + 2 * u + 2
                if not last:
                    for h in range(2):
                        split_hi(act, k * 2, first + h)
                act.wait_ge(piece_used, k * 4 + first)
                for t in range(TT):
                    o = act.activation(
                        y6[:, t, :].rearrange("p (a b w) -> p a b w", b=2, w=256)[:, k, u],
                        ps[4 * u + t][:, 0:256], ACT.Copy)
                    ch(o) if t < TT - 1 else o.then_inc(out_read, 1)

            def out_stage(layer):
                act.wait_ge(mix_split, KT * (layer + 1))
                act.sem_inc(out_read, 2)
                with act.Fori(0, 3) as k:
                    ch.enter(k, 6)
                    for u in range(2):
                        out_group(layer, k, u)
                    ch.leave(3)
                for u in range(2):
                    out_group(layer, 3, u, last=(u == 1))
                act.wait_ge(out_read, 10 * layer + 10)
                ch.wait()
                for t in range(TT):
                    ch(act.activation(zl[:, 4 * t:4 * t + 4, :].rearrange("p a b -> p (a b)"),
                                      y6[:, t, :], ACT.Square, accum_out=small[:, t:t + 1]))
                ch.wait()
                act.activation(small[:, 4:8], small[:, 0:4], ACT.Sqrt, bias=EPS,
                               scale=1.0 / D).then_inc(root_done, 1)

            for h in range(2):
                split_hi(act, 0, P_OUT0 + h)
            out_stage(0)
            over(act, 9)

            norm_stage(1, x6, ztmp6)
            over(act, 10)

            act.wait_ge(angle, 1)
            act.activation(r2[:, :], r1[:, :], ACT.Sin, scale=SAFE_TURN / 2).then_inc(rope_sine, 1)
            act.wait_ge(rope_sine, 1)
            act.activation(r1[:, :], r1[:, :], ACT.Sin, scale=SAFE_TURN).then_inc(rope_sine, 1)
            for h in range(3):
                split_hi(act, 0, P_IN1 + h)
            act.sem_inc(in1_read, 2)

            def in1_group(k, u, to, func):
                for h in range(2):
                    split_hi(act, k * 2, P_IN1 + 3 + 2 * u + h)
                act.wait_ge(piece_used, k * 4 + (P_IN1 + 3 + 2 * u))
                ch(act.activation(to[0], ps[2 * u][:, :], func))
                act.activation(to[1], ps[2 * u + 1][:, :], func).then_inc(in1_read, 1)

            with act.Fori(0, 2) as k:
                ch.enter(k, 2)
                for u in range(2):
                    in1_group(k, u, [cq[:, :, :].rearrange("p (a b) t -> p a b t", b=4)[:, k, 2 * u + j]
                                     for j in range(2)], ACT.Copy)
                ch.leave(2)
            with act.Fori(0, 4) as k:
                ch.enter(k, 2)
                for u in range(2):
                    in1_group(k + 2, u, [sg1[:, :, :].rearrange("p (a b) t -> p a b t", b=4)[:, k, 2 * u + j]
                                         for j in range(2)], ACT.Silu)
                ch.leave(4)
            over(act, 11)

            for i in range(8):
                if i >= 2:
                    act.wait_ge(c_summed, i - 1)
                act.activation((r1, r2)[i % 2][:, :], cq[:, i, :], ACT.Square).then_inc(c_squared, 1)
            act.wait_ge(c_summed, 8)
            for n, to in enumerate((ktmp, rms_kv)):
                act.activation(to[:, :], ps[6 + n][:, :], ACT.Sqrt, bias=EPS, scale=1.0 / 512)\
                   .then_inc(c_root, 1)
            act.wait_ge(c_split, 8)
            act.sem_inc(a_act, aj.total("act"))
            with act.Fori(0, H // 2) as k:
                def job(key):
                    act.wait_ge(a_job, k * len(aj.jobs) + aj.number(key))
                    return ps[aj.bank(key)]

                for a in range(2):
                    for x, to in (("qn", qn), ("key", key9)):
                        p = job((x, a))
                        act.activation(to[a][:, :], p[:, :], ACT.Copy).then_inc(a_act, 1)
                for n in range(2):
                    p = job(("v", n))
                    act.activation(v9[:, 2 * n:2 * n + 2, :].rearrange("p t v -> p (t v)"), p[:, :],
                                   ACT.Copy).then_inc(a_act, 1)
                split_hi(act, k, P_UP + 2)
                split_hi(act, k, P_UP + 3)
                for a in range(2):
                    for b in range(TT):
                        i, w = TT * a + b, (b + 1) * P
                        act.wait_ge(max_ready, k * 8 + (i + 1))
                        p = job(("s", a, b))
                        act.activation(probs[a][:, b, 0:w], p[:, 0:w], ACT.Exp, scale=SCALE,
                                       bias=stat[:, 0, i:i + 1],
                                       accum_out=stat[:, 1, i:i + 1]).then_inc(a_act, 1)
            over(act, 12)

            out_stage(1)
            over(act, 13)

        @block.tensor
        def _(pe):
            pe.wait_ge(ident_in, 16)
            pe.wait_ge(consts_set, 1)

            def mod_sums_of(layer):
                pe.wait_ge(acc_ready, layer + 1)
                flat = acc[:, :, :].rearrange("p a b -> p (a b)")
                for j in range(32):
                    last = pe.matmul(ps[0][:, j:j + 1], flat[:, j * P:(j + 1) * P], ones[:, 0:1],
                                     start=True, stop=True)
                for j in range(4):
                    last = pe.matmul(ps[4 + j][:, :], ones[:, :],
                                     flat[:, 2 * D + 512 * j:2 * D + 512 * (j + 1)],
                                     start=True, stop=True)
                last.then_inc(mod_sums, 1)

            def turn_x(layer, xt):
                pe.wait_ge(x_normed, layer + 1)
                for k in range(KT):
                    if k >= 2:
                        pe.wait_ge(z_scaled, KT * layer + k - 1)
                    for t in range(TT):
                        last = pe.transpose(ps[2 + k % 2][:, t * P:(t + 1) * P],
                                            xt[:, t, k * P:(k + 1) * P], ident[:, :])
                    last.then_inc(x_turned, 1)

            def half_tile(bank, s, h, j, width, wide):
                for kk in range(wide):
                    k = h * wide + kk
                    o = kk * width + j * P
                    hi, lo = whi[s][:, o:o + P], wlo[s][:, o:o + P]
                    for n, (a, b) in enumerate(((hi, zh), (hi, zl), (lo, zh))):
                        last = pe.matmul(bank, a, b[:, k, :], start=(k == 0 and n == 0),
                                         stop=(k == KT - 1 and n == 2))
                return last

            def group(k, n, b):
                for h in range(2):
                    piece_ready(pe, k, n + h)
                    for j in range(2):
                        last = half_tile(ps[b + j][:, :], (n + h) % 2, h, j, 256, 8)
                    last.then_inc(piece_used, 1)
                return last

            mod_sums_of(0)
            turn_x(0, xt)
            pe.wait_ge(z_ready, KT)
            over(pe, 1)

            piece_ready(pe, 0, 0)
            half_tile(ps[7][:, :], 0, 0, 0, P, KT).then_inc(piece_used, 1)
            with pe.Fori(0, 8) as k:
                for u in range(2):
                    pe.wait_ge(proj_out, k * 2 + (u + 1))
                    group(k * 2, 2 * u + 1, 2 * u)
            with pe.Fori(8, 10) as k:
                for u in range(2):
                    pe.wait_ge(proj_out, k * 2 + (u + 1))
                    for h in range(2):
                        piece_ready(pe, k * 2, 2 * u + 1 + h)
                        s = (1 + h) % 2
                        for t in range(TT):
                            for kk in range(8):
                                kt = h * 8 + kk
                                hi, lo = (w[s][:, kk * 256:(kk + 1) * 256] for w in (whi, wlo))
                                for n, (a, b) in enumerate(((zh, hi), (zl, hi), (zh, lo))):
                                    last = pe.matmul(ps[4 - 4 * u + t][:, 0:256],
                                                     a[:, kt, t * P:(t + 1) * P], b,
                                                     start=(kt == 0 and n == 0),
                                                     stop=(kt == KT - 1 and n == 2))
                        last.then_inc(piece_used, 1)
            with pe.Fori(10, 12) as k:
                for u in range(2):
                    pe.wait_ge(proj_out, k * 2 + (u + 1))
                    group(k * 2, 2 * u + 1, 4 + 2 * u)
            pe.wait_ge(proj_out, 2 + 24)
            mod_sums_of(1)
            over(pe, 2)

            pe.wait_ge(mask_in, 64)
            with pe.Fori(0, FT // 2) as k:
                def has_read(*keys):
                    for who, count in (("dve", r_dve), ("act", r_act)):
                        reads = [rj.reads(x) for x in keys if rj.reader(x) == who]
                        if reads:
                            pe.wait_ge(count, k * rj.total(who) + max(reads))

                def bank(key, *needs):
                    old = rj.before(key)
                    has_read(*needs, *([] if old is None else [old]))
                    return ps[rj.bank(key)]

                def mm(out_ap, a, b, start, stop):
                    return pe.matmul(out_ap, a, b, start=start, stop=stop)

                for u in range(2):
                    pe.wait_ge(pair_in[u], k * 48 + 48)
                    for n, x in enumerate(("decay", "rate")):
                        b = bank((x, u))
                        mm(b[:, :], lora[u][:, n, :], lo_in[:, :], True, True).then_inc(r_job, 1)
                for u in range(2):
                    b = bank(("norm", u))
                    pe.wait_ge(key_squared, k * 2 + (u + 1))
                    mm(b[:, :], blk1[:, :], sq[u][:, :], True, True).then_inc(r_job, 1)
                for u in range(2):
                    b = bank(("bonus", u))
                    pe.wait_ge(bonus_in, k * 2 + (u + 1))
                    mm(b[:, :], blk1[:, :], bonus[u][:, :], True, True).then_inc(r_job, 1)
                for u in range(2):
                    for x, src in (("b", b_d), ("k", k_d)):
                        for c in range(0, NC, 2):
                            b = bank(("pairs", x, u, c))
                            pe.wait_ge(operands, k * 2 + (u + 1))
                            for i in range(2):
                                last = mm(b[:, i * 192:i * 192 + 192], src[u][:, c + i, :],
                                          ra[u][:, c + i, :], True, True)
                            last.then_inc(r_job, 1)
                    for x, src in (("b", b_d), ("k", k_d), ("v", v_d)):
                        for c in range(0, NC, 4):
                            b = bank(("turn", x, u, c))
                            if x == "v":
                                pe.wait_ge(v_blocks, k * 4 + (2 * u + 2))
                            for i in range(4):
                                last = pe.transpose(b[:, i * P:(i + 1) * P],
                                                    src[u][:, c + i, :], ident[:, :])
                            last.then_inc(r_job, 1)
                for n in range(LEVELS):
                    for u in range(2):
                        for c in range(0, NC, 4):
                            b = bank(("at", n, u, c), ("inv", n - 1, u, c) if n else
                                     ("pairs", "b", u, c + 2))
                            for i in range(4):
                                last = mm(b[:, i * P:(i + 1) * P], rb[u][:, c + i, CH:],
                                          ident[:, :] if n == 0 else inv[u][:, c + i, :],
                                          True, True)
                            last.then_inc(r_job, 1)
                    for u in range(2):
                        for c in range(0, NC, 4):
                            for x in ("inv", "invT") if n < LEVELS - 1 else ("invT",):
                                b = bank((x, n, u, c), ("at", n, u, c),
                                         *([("invT", n - 1, u, c)] if n else []))
                                for i in range(4):
                                    t = ident[:, :] if n == 0 else inv_t[u][:, c + i, :]
                                    y = at_inv[u][:, c + i, :]
                                    last = mm(b[:, i * P:(i + 1) * P], *((t, y) if x == "inv" else (y, t)),
                                              True, True)
                                last.then_inc(r_job, 1)
                for c in range(NC):
                    old, new = c % 2, (c + 1) % 2
                    for u in range(2):
                        b = bank(("w", c, u), *([] if c else [("turn", "v", u, 4),
                                                              ("pairs", "k", u, 6)]))
                        mm(b[:, 0:P], rk[u][:, c, CH:], v_t[u][:, c, :], True, False)
                        if c:
                            has_read(("s", c - 1, u))
                        else:
                            pe.wait_ge(state_zero, k * 2 + 8)
                        mm(b[:, 0:P], ra[u][:, c, CH:], state[u][:, old, :], False, True)\
                            .then_inc(r_job, 1)
                    for u in range(2):
                        b = bank(("u", c, u), ("w", c, u),
                                 *([] if c else [("invT", LEVELS - 1, u, 4)]))
                        mm(b[:, 0:P], inv_t[u][:, c, :], wu[u][:, 0, :], True, True).then_inc(r_job, 1)
                    for u in range(2):
                        b = bank(("s", c, u))
                        mm(b[:, 0:P], ident[:, :], state[u][:, old, :], True, False)
                        mm(b[:, 0:P], k_t[u][:, c, :], v_t[u][:, c, :], False, False)
                        has_read(("u", c, u))
                        mm(b[:, 0:P], b_t[u][:, c, :], wu[u][:, 1, :], False, True)\
                            .then_inc(r_job, 1)
                    for u in range(2):
                        y = ps[6 + u][:, c * CH:(c + 1) * CH]
                        mm(y, state[u][:, old, :], ra[u][:, c, 0:CH], True, False)
                        mm(y, wu[u][:, 1, :], rb[u][:, c, 0:CH], False, False)
                        last = mm(y, v_t[u][:, c, :], rk[u][:, c, 0:CH], False, True)
                        if c == NC - 1:
                            last.then_inc(y_out, 1)
                for u in range(2):
                    b = bank(("mean", u))
                    pe.wait_ge(y_copied, k * 2 + (u + 1))
                    mm(b[:, :], blk1[:, :], cum[u][:, :], True, True).then_inc(r_job, 1)
                for u in range(2):
                    b = bank(("var", u))
                    pe.wait_ge(y_squared, k * 2 + (u + 1))
                    mm(b[:, :], blk1[:, :], sq[u][:, :], True, True).then_inc(r_job, 1)
                over(pe, k + 3)

            pe.wait_ge(s5_in, 16 * 7)
            with pe.Fori(0, FT) as b:
                def read5(*keys):
                    for who, count in (("dve", s_dve), ("act", s_act)):
                        reads = [sj.reads(x) for x in keys if sj.reader(x) == who]
                        if reads:
                            pe.wait_ge(count, b * sj.total(who) + max(reads))

                def bank5(key, *needs):
                    old = sj.before(key)
                    read5(*needs, *([] if old is None else [old]))
                    return ps[sj.bank(key)]

                p = bank5("uc")
                pe.wait_ge(u_grouped, b + 1)
                for g in range(GB):
                    last = pe.matmul(p[:, g * C8:(g + 1) * C8], ugm[:, g, :], ident[0:C8, 0:C8],
                                     start=True, stop=True)
                last.then_inc(s_job, 1)
                pe.wait_ge(w_ready, b * 2 + 2)
                for n in range(2):
                    p = bank5(f"wv{n}")
                    for g in range(4):
                        last = pe.transpose(p[:, g * P:(g + 1) * P], wvt[:, 4 * n + g, :, :].rearrange(
                            "p j q -> p (j q)"), ident[:, :])
                    last.then_inc(s_job, 1)
                for n in range(2):
                    p = bank5(f"k{n}")
                    for g in range(4):
                        last = pe.matmul(p[0:GP, g * P:(g + 1) * P], bb[0][:, 4 * n + g, :],
                                         wc[:, 4 * n + g, 0:T8, :], start=True, stop=True)
                    last.then_inc(s_job, 1)
                p = bank5("v", "uc", "wv1")
                for g in range(GB):
                    last = pe.matmul(p[:, g * C8:(g + 1) * C8], wv[:, g, :], uc[:, g, :],
                                     start=True, stop=True)
                last.then_inc(s_job, 1)
                p = bank5("vs", "v")
                pe.matmul(p[:, :], swap[:, :], vin[:, :, :], start=True, stop=True).then_inc(s_job, 1)
                p = bank5("zs")
                pe.wait_ge(x_ready, b * 2 + 1)
                pe.matmul(p[:, :], swap[:, :], zst[:, :, :], start=True, stop=True).then_inc(s_job, 1)
                pe.wait_ge(x_ready, b * 2 + 2)
                pe.wait_ge(w3_in, b * 128 + 128)
                for n in range(2):
                    p = bank5(f"y{n}")
                    for g in range(4):
                        o = p[0:C8, g * P:(g + 1) * P]
                        pe.matmul(o, xst[:, 4 * n + g, :], wc[:, 4 * n + g, 1:, :], start=True, stop=False)
                        last = pe.matmul(o, uc[:, 4 * n + g, :], w3[:, 4 * n + g, :],
                                         start=False, stop=True)
                    last.then_inc(s_job, 1)
                p = bank5("yt", "y1")
                for j in range(T8):
                    last = pe.matmul(p[:, j * C8:(j + 1) * C8], ycm[:, j, :], ident[0:C8, 0:C8],
                                     start=True, stop=True)
                last.then_inc(s_job, 1)
            over(pe, 7)

            pe.wait_ge(gy_split, FT)
            for n in range(4):
                u = n % 2
                if n >= 2:
                    pe.wait_ge(glu_out, n - 1)
                piece_ready(pe, 0, P_GLU + n)
                s = (P_GLU + n) % 2
                for j in range(2):
                    for kt in range(FT):
                        o = kt * 256 + j * P
                        hi, lo = whi[s][:, o:o + P], wlo[s][:, o:o + P]
                        for m, (a, b) in enumerate(((hi, zh), (hi, zl), (lo, zh))):
                            last = pe.matmul(ps[2 * u + j][:, :], a, b[:, kt, :],
                                             start=(kt == 0 and m == 0), stop=(kt == FT - 1 and m == 2))
                last.then_inc(piece_used, 1)
            over(pe, 8)

            def out_gemm(layer, first_piece):
                pe.wait_ge(mix_split, KT * (layer + 1))
                with pe.Fori(0, 4) as k:
                    for u in range(2):
                        pe.wait_ge(out_read, k * 2 + (10 * layer + u + 1))
                        for h in range(2):
                            n = first_piece + 2 * u + h
                            piece_ready(pe, k * 2, n)
                            time_major(4 * u, n % 2, h)

            def time_major(bank, s, h):
                for t in range(TT):
                    for kk in range(8):
                        kt = h * 8 + kk
                        hi, lo = (w[s][:, kk * 256:(kk + 1) * 256] for w in (whi, wlo))
                        for n, (a, b) in enumerate(((zh, hi), (zl, hi), (zh, lo))):
                            last = pe.matmul(ps[bank + t][:, 0:256], a[:, kt, t * P:(t + 1) * P], b,
                                             start=(kt == 0 and n == 0), stop=(kt == KT - 1 and n == 2))
                last.then_inc(piece_used, 1)

            out_gemm(0, P_OUT0)
            over(pe, 9)

            turn_x(1, x6)
            pe.wait_ge(z_ready, 2 * KT)
            over(pe, 10)

            piece_ready(pe, 0, P_IN1)
            half_tile(ps[7][:, :], P_IN1 % 2, 0, 0, P, KT).then_inc(piece_used, 1)
            pe.wait_ge(key_rotated, 1)
            pe.matmul(ps[6][:, :], fold[:, :], ktmp[:, :], start=True, stop=True).then_inc(key_folded, 1)
            with pe.Fori(0, 6) as k:
                for u in range(2):
                    pe.wait_ge(in1_read, k * 2 + (u + 1))
                    group(k * 2, P_IN1 + 1 + 2 * u, 2 * u)
            over(pe, 11)

            for i in range(8):
                pe.wait_ge(c_squared, i + 1)
                pe.matmul(ps[6 + i // 4][:, :], ones[:, :], (r1, r2)[i % 2][:, :],
                          start=(i % 4 == 0), stop=(i % 4 == 3)).then_inc(c_summed, 1)
            pe.wait_ge(c_split, 8)
            with pe.Fori(0, H // 2) as k:
                def read9(*keys):
                    for who, count in (("dve", a_dve), ("act", a_act)):
                        turn = aj.total(who)
                        reads = [turn + aj.reads(x) for x in keys if aj.reader(x) == who]
                        if reads:
                            pe.wait_ge(count, k * turn + max(reads))

                def bank9(key, *needs):
                    old, counts = aj.before(key), {"dve": [], "act": []}
                    for x in (*needs, *([old] if old else [])):
                        counts[aj.reader(x)].append(aj.total(aj.reader(x)) + aj.reads(x))
                    if old is None:
                        x = aj.jobs[aj.number(key) - 1 - len(aj.banks)][0]
                        counts[aj.reader(x)].append(aj.reads(x))
                    for who, count in (("dve", a_dve), ("act", a_act)):
                        if counts[who]:
                            pe.wait_ge(count, k * aj.total(who) + max(counts[who]))
                    return ps[aj.bank(key)]

                def up(p, s, first, cs, left=False):
                    for kt in range(4):
                        o = kt * 512 + first
                        hi, lo = whi[s][:, o:o + P], wlo[s][:, o:o + P]
                        for n, (a, b) in enumerate(((hi, zh), (hi, zl), (lo, zh))):
                            last = pe.matmul(p[:, :], a, b[:, cs + kt, :], start=(kt == 0 and n == 0),
                                             stop=(kt == 3 and n == 2))
                            if left and kt == 0 and n == 0:
                                last.then_inc(piece_used, 1)
                    return last

                piece_ready(pe, k, P_UP)
                for a in range(2):
                    for n, x in enumerate(("qn", "qp", "key")):
                        p = bank9((x, a))
                        if x == "key":
                            if a == 0:
                                piece_ready(pe, k, P_UP + 1)
                            last = up(p, (P_UP + 1) % 2, a * P, 4, left=(a == 1))
                        else:
                            last = up(p, P_UP % 2, a * 256 + n * P, 0)
                        last.then_inc(a_job, 1)
                for n in range(2):
                    p = bank9(("v", n))
                    for t in range(2):
                        for kt in range(4):
                            o = kt * 512 + 256
                            s = (P_UP + 1) % 2
                            hi, lo = (w[s][:, o:o + 256] for w in (whi, wlo))
                            for m, (x, y) in enumerate(((zh, hi), (zl, hi), (zh, lo))):
                                tok = (2 * n + t) * P
                                last = pe.matmul(p[:, t * 256:(t + 1) * 256], x[:, 4 + kt, tok:tok + P],
                                                 y, start=(kt == 0 and m == 0), stop=(kt == 3 and m == 2))
                    last.then_inc(a_job, 1)
                for a in range(2):
                    for b in range(TT):
                        w, q = (b + 1) * P, slice(b * P, (b + 1) * P)
                        p = bank9(("s", a, b), ("qn", a), ("qp", a), ("key", a))
                        first = pe.matmul(p[:, 0:w], qn[a][:, q], key9[a][:, 0:w], start=True, stop=False)
                        if a == 0 and b == 0:
                            first.then_inc(piece_used, 1)
                        pe.matmul(p[:, q], ident[:, :], neg_tri[:, :], start=False, stop=False,
                                  skip_group_check=True)
                        pe.matmul(p[:, 0:w], qp[a][:, q], key_pe[:, 0:w], start=False, stop=True)\
                          .then_inc(a_job, 1)

                def turn_probs(i):
                    a, b = divmod(i, TT)
                    p = bank9(("pt", a, b))
                    pe.wait_ge(probs_ready, k * 8 + (i + 1))
                    for n in range(b + 1):
                        last = pe.transpose(p[:, n * P:(n + 1) * P], probs[a][:, b, n * P:(n + 1) * P],
                                            ident[:, :])
                    last.then_inc(a_job, 1)

                def weigh(i):
                    a, b = divmod(i, TT)
                    if b == 0:
                        pe.wait_ge(o_read, k * 2 + (a + 1))
                    read9(("pt", a, b))
                    for n in range(b + 1):
                        last = pe.matmul(ps[6 + a][:, b * P:(b + 1) * P], v9[:, n, a * P:(a + 1) * P],
                                         pt9[i % 2][:, n * P:(n + 1) * P], start=(n == 0), stop=(n == b))
                    if b == TT - 1:
                        last.then_inc(o_ready, 1)

                turn_probs(0)
                for i in range(1, 8):
                    turn_probs(i)
                    weigh(i - 1)
                weigh(7)
            over(pe, 12)

            out_gemm(1, P_OUT1)
            over(pe, 13)

        @block.vector
        def _(dve):
            ch = Chain(dve, dve_chain)
            ch(dve.memset(acc[:, :, :], 0.0))
            dve.wait_ge(csilu_set, 1)
            ch.wait()

            def add_ada(layer, k, q):
                dve.wait_ge(ada_full[q % 2], k * 32 + (512 * layer + 16 * (q // 2) + 16))
                dve.scalar_tensor_tensor(acc[:, q, :], ada[q % 2][:, :], csilu[:, k:k + 1] if
                                         isinstance(k, int) else
                                         csilu[:, :].rearrange("p (a b) -> p a b", b=1)[:, k, :],
                                         acc[:, q, :], ALU.mult, ALU.add).then_inc(ada_used, 1)

            def mod_finish(layer):
                if layer == 1:
                    dve.wait_ge(gb_in, 64)
                else:
                    dve.wait_ge(gb_in, 32)
                dve.wait_ge(mod_sums, layer + 1)
                m = modc[layer]
                ch(dve.tensor_tensor(m[:, :], ps[0][:, 0:32], col(f"ab{layer}", 0, 32), ALU.add))
                for j in range(4):
                    ch(dve.tensor_tensor(gp[layer][:, j * 512:(j + 1) * 512], ps[4 + j][:, :],
                                         gp[layer][:, j * 512:(j + 1) * 512], ALU.add))
                ch.wait()
                ch(dve.scalar_tensor_tensor(m[:, 16:32], m[:, 16:32], 1.0, col(f"pre{layer}", 0, 16),
                                            ALU.add, ALU.mult))
                ch(dve.tensor_tensor(gp[layer][:, :], gp[layer][:, :], post_b[:, :], ALU.mult))
                ch.wait()
                dve.sem_inc(mod_ready, 1)

            def norm_x(layer, xt):
                dve.wait_ge(root_done, 2 * layer + 1)
                ch(dve.reciprocal(small[:, 8:12], small[:, 4:8]))
                ch.wait()
                for t in range(TT):
                    o = dve.tensor_scalar(xt[:, t, :], xt[:, t, :], small[:, 8 + t:9 + t], None,
                                          ALU.mult)
                    if t < TT - 1:
                        ch(o)
                ch.wait()
                o.then_inc(x_normed, 1)

            def split_z(layer, ztmp):
                for k in range(KT):
                    dve.wait_ge(z_scaled, KT * layer + k + 1)
                    ch(dve.tensor_copy(zh[:, k, :], ztmp[:, k % 2, :]))
                    ch.wait()
                    dve.tensor_tensor(zl[:, k, :], ztmp[:, k % 2, :], zh[:, k, :].bitcast(F32),
                                      ALU.subtract).then_inc(z_ready, 1)

            for q in range(4):
                add_ada(0, 0, q)
            norm_x(0, xt)
            with dve.Fori(1, KT) as k:
                for q in range(4):
                    add_ada(0, k, q)
            dve.wait_ge(ada_used, 4 * KT)
            dve.sem_inc(acc_ready, 1)
            mod_finish(0)
            split_z(0, ztmp)
            over(dve, 1)

            ch(dve.memset(shift[:, :, 0:1], 0.0))
            ch(dve.memset(acc[:, :, :], 0.0))
            ch.wait()

            def mix(j, out_ap, mu, o_inc=None):
                ch(dve.tensor_tensor(out_ap, shift[:, j, 0:L], shift[:, j, 1:], ALU.subtract))
                ch.wait()
                return dve.scalar_tensor_tensor(out_ap, out_ap, mu, shift[:, j, 1:],
                                                ALU.mult, ALU.add)

            dve.wait_ge(proj_out, 2)
            mix(0, lo_in[:, :], col("mu", 32)).then_inc(mixed, 1)

            def mix_group(k, u, first):
                dve.wait_ge(proj_out, k * 2 + (u + 3))
                if not first:
                    dve.wait_ge(res_stored[u], k * 16)
                ch(mix(0, res[u][:, 0, :], rcol("mu", k, 2 * u, 4)))
                mix(1, res[u][:, 1, :], rcol("mu", k, 2 * u + 1, 4)).then_inc(mixed, 1)

            def turn(k, first):
                ch.enter(k, 6, 0 if first else 1)
                for u in range(2):
                    for q in range(4):
                        add_ada(1, k * 2 + u, q)
                    mix_group(k, u, first)
                ch.leave(1 if first else 7)

            turn(0, True)
            with dve.Fori(1, 8) as k:
                turn(k, False)
            dve.wait_ge(ada_used, 8 * KT)
            dve.sem_inc(acc_ready, 1)
            mod_finish(1)
            over(dve, 2)

            for u in range(2):
                for b in (b_d, k_d, v_d):
                    dve.memset(b[u][:, :, :], 0.0).then_inc(state_zero, 1)
                ch(dve.memset(ra[u][:, :, :], 0.0))
                ch(dve.memset(grow[u][:, :, 0:1], 1.0))
            ch.wait()
            dve.wait_ge(state_zero, 6)
            dve.wait_ge(mask_in, 64)

            def rwkv_turn(k):
                def read(key):
                    dve.wait_ge(r_job, k * len(rj.jobs) + rj.number(key))
                    return ps[rj.bank(key)]

                chunks = lambda ap: ap.rearrange("p (c t) -> p c t", c=NC)
                for u in range(2):
                    dve.memset(state[u][:, 0, :], 0.0).then_inc(state_zero, 1)
                for u in range(2):
                    b = read(("norm", u))
                    ch(dve.tensor_scalar(root[u][:, :], b[:, :], 1e-24, None, ALU.max))
                    ch.wait()
                    dve.sem_inc(norm_max, 1)
                    dve.sem_inc(r_dve, 1)
                for u in range(2):
                    dve.wait_ge(r_act, k * rj.total("act") + rj.reads(("decay", u)))
                    ch(dve.tensor_scalar(cum[u][:, :], cum[u][:, :], -DECAY, None, ALU.mult))
                    ch.wait()
                    dve.tensor_tensor_scan(cum[u][:, :], starts[:, :], cum[u][:, :], 0.0,
                                           ALU.mult, ALU.add).then_inc(cum_done, 1)
                for u in range(2):
                    r, key, v = (rkv[u][:, n, :] for n in range(3))
                    dve.wait_ge(norm_root, k * 2 + (u + 1))
                    dve.wait_ge(r_act, k * rj.total("act") + rj.reads(("rate", u)))
                    ch(dve.reciprocal(root[u][:, :], root[u][:, :]))
                    ch(dve.tensor_scalar(bv[u][:, :], rate[u][:, :], -1.0, rcol("ka", k, u, 2),
                                         ALU.add, ALU.mult))
                    ch.wait()
                    ch(dve.scalar_tensor_tensor(kn[u][:, :], key, rcol("kk", k, u, 2),
                                                root[u][:, :], ALU.mult, ALU.mult))
                    ch(dve.scalar_tensor_tensor(kp[u][:, :], bv[u][:, :], 1.0, key,
                                                ALU.add, ALU.mult))
                    ch.wait()
                    ch(dve.scalar_tensor_tensor(bonus[u][:, :], r, rcol("rk", k, u, 2),
                                                kp[u][:, :], ALU.mult, ALU.mult))
                    ch(dve.tensor_tensor(bv[u][:, :], kn[u][:, :], rate[u][:, :], ALU.mult))
                    ch.wait()
                    dve.sem_inc(bonus_in, 1)
                for u in range(2):
                    dve.wait_ge(exp_done, k * 2 + (u + 1))
                    ch(dve.tensor_tensor(ra[u][:, :, 0:CH], chunks(rkv[u][:, 0, :]),
                                         grow[u][:, :, 1:], ALU.mult))
                    for h in range(2):
                        rows, blk = slice(64 * h, 64 * h + 64), slice(64 * h, 64 * h + 64)
                        ch(dve.scalar_tensor_tensor(
                            ra[u][rows, :, CH + 64 * h:CH + 64 * h + 64], chunks(kn[u][rows, :]),
                            -1.0, grow[u][rows, :, 0:CH], ALU.mult, ALU.mult))
                        ch(dve.tensor_tensor(b_d[u][rows, :, blk], chunks(bv[u][rows, :]),
                                             chunks(shrink[u][rows, :]), ALU.mult))
                        ch(dve.tensor_tensor(k_d[u][rows, :, blk], chunks(kp[u][rows, :]),
                                             chunks(shrink[u][rows, :]), ALU.mult))
                    ch.wait()
                    dve.sem_inc(operands, 1)
                for u in range(2):
                    b = read(("bonus", u))
                    dve.tensor_tensor(bonus[u][:, :], b[:, :], rkv[u][:, 2, :], ALU.mult)\
                       .then_inc(r_dve, 1)
                for u in range(2):
                    for x, to in (("b", rb), ("k", rk)):
                        for c in range(0, NC, 2):
                            b = read(("pairs", x, u, c))
                            dve.tensor_tensor(
                                to[u][:, c:c + 2, :], b[:, 0:384].rearrange("p (c s) -> p c s", c=2),
                                tri[:, :].unsqueeze(1).broadcast_to((P, 2, 3 * CH)), ALU.mult)\
                               .then_inc(r_dve, 1)
                quad = lambda b: b[:, :].rearrange("p (c s) -> p c s", c=4)
                eye = ident[:, :].unsqueeze(1).broadcast_to((P, 4, P))
                for n in range(LEVELS):
                    for u in range(2):
                        for c in range(0, NC, 4):
                            b = read(("at", n, u, c))
                            dve.tensor_tensor(
                                at_inv[u][:, c:c + 4, :], quad(b),
                                corner[:, n, :].unsqueeze(1).broadcast_to((P, 4, P)), ALU.mult)\
                               .then_inc(r_dve, 1)
                    for u in range(2):
                        for c in range(0, NC, 4):
                            if n < LEVELS - 1:
                                b = read(("inv", n, u, c))
                                t = inv[u][:, c:c + 4, :]
                                dve.tensor_tensor(t, quad(b), eye if n == 0 else t, ALU.add)\
                                   .then_inc(r_dve, 1)
                            b = read(("invT", n, u, c))
                            t = inv_t[u][:, c:c + 4, :]
                            dve.tensor_tensor(t, quad(b), eye if n == 0 else t, ALU.add)\
                               .then_inc(r_dve, 1)
                for c in range(NC):
                    for u in range(2):
                        b = read(("s", c, u))
                        dve.tensor_scalar(state[u][:, (c + 1) % 2, :], b[:, 0:P],
                                          grow[u][:, c, CH:], None, ALU.mult).then_inc(r_dve, 1)
                for u in range(2):
                    dve.wait_ge(y_out, k * 2 + (u + 1))
                    dve.tensor_copy(cum[u][:, :], ps[6 + u][:, :]).then_inc(y_copied, 1)
                for u in range(2):
                    b = read(("mean", u))
                    ch(dve.scalar_tensor_tensor(cum[u][:, :], b[:, :], -1.0 / HN, cum[u][:, :],
                                                ALU.mult, ALU.add))
                    ch.wait()
                    dve.sem_inc(r_dve, 1)
                    dve.sem_inc(y_centred, 1)
                for u in range(2):
                    y = cum[u][:, :]
                    dve.wait_ge(r_act, k * rj.total("act") + rj.reads(("var", u)))
                    ch(dve.reciprocal(root[u][:, :], root[u][:, :]))
                    ch.wait()
                    ch(dve.tensor_tensor(y, y, root[u][:, :], ALU.mult))
                    ch.wait()
                    ch(dve.tensor_scalar(y, y, rcol("lnxg", k, u, 2), rcol("lnxb", k, u, 2),
                                         ALU.mult, ALU.add))
                    ch.wait()
                    ch(dve.tensor_tensor(y, y, bonus[u][:, :], ALU.add))
                    ch.wait()
                    dve.tensor_tensor(y, y, sg[u][:, :], ALU.mult).then_inc(y_ready, 1)
                over(dve, k + 3)

            with dve.Fori(0, FT // 2) as k:
                ch.enter(k, 40)
                rwkv_turn(k)
                ch.leave(FT // 2)

            def do(ins):
                ch(ins)
                ch.wait()

            def tt(o, a, b, op):
                do(dve.tensor_tensor(o, a, b, op))

            def ts(o, a, s1, op0, s2=None, op1=ALU.bypass):
                do(dve.tensor_scalar(o, a, s1, s2, op0, op1))

            def fraction(x, tmp):
                ts(tmp, x, MAGIC, ALU.add)
                ts(tmp, tmp, -MAGIC, ALU.add)
                tt(x, x, tmp, ALU.subtract)

            def to_turns(x, tmp):
                ts(tmp, x, 1.0 / TURN, ALU.mult, MAGIC, ALU.add)
                ts(tmp, tmp, -MAGIC, ALU.add)
                do(dve.scalar_tensor_tensor(x, tmp, -TURN_A, x, ALU.mult, ALU.add))
                do(dve.scalar_tensor_tensor(x, tmp, -TURN_B, x, ALU.mult, ALU.add))
                ts(x, x, 1.0 / TURN, ALU.mult, 0.5, ALU.min)
                ts(x, x, -0.5, ALU.max)

            e = [x[:, :] for x in e1]
            lam_re, lam_im = lam[:, 0, :], lam[:, 1, :]
            over_g = lambda ap: ap.unsqueeze(1).broadcast_to((P, NP, G))
            powers = expo[:, :].unsqueeze(2).broadcast_to((P, NP, G))
            dve.wait_ge(s5_in, 16 * 7)
            do(dve.memset(kpad[:, :, :], 0.0))
            do(dve.memset(xst[:, :, 0:1], 0.0))
            dve.wait_ge(s5_mag, 1)
            tt(e[1], lam_re, e[0], ALU.mult)
            tt(e[2], lam_im, e[0], ALU.mult)
            to_turns(e[2], e[6])
            tt(pw_re[:, :, :], over_g(e[1]), powers, ALU.mult)
            tt(pw_im[:, :, :], over_g(e[2]), powers, ALU.mult)
            fraction(pw_im[:, :, :], pt2[:, :, :])
            ts(mag8[:, :], e[1], float(T8), ALU.mult)
            ts(turn8[:, :], e[2], float(T8), ALU.mult)
            fraction(turn8[:, :], e[6])
            dve.sem_inc(s5_angle, 1)
            dve.wait_ge(s5_mag, 4)
            dve.wait_ge(s5_sine, 4)
            tt(pt2[:, :, :], pt2[:, :, :], pt2[:, :, :], ALU.mult)
            ts(pt2[:, :, :], pt2[:, :, :], -2.0, ALU.mult, 1.0, ALU.add)
            tt(pw_re[:, :, :], pt2[:, :, :], pt1[:, :, :], ALU.mult)
            do(dve.scalar_tensor_tensor(pw_im[:, :, :], pw_im[:, :, :], sign[:, 1:2], pt1[:, :, :],
                                        ALU.mult, ALU.mult))
            tt(e[5], e[5], e[5], ALU.mult)
            do(dve.scalar_tensor_tensor(e[5], e[5], -2.0, e[3], ALU.mult, ALU.mult))
            do(dve.scalar_tensor_tensor(e[5], e[3], -1.0, e[5], ALU.add, ALU.add))
            tt(e[4], e[4], e[3], ALU.mult)
            tt(e[6], lam_re, lam_re, ALU.mult)
            tt(e[7], lam_im, lam_im, ALU.mult)
            tt(e[6], e[6], e[7], ALU.add)
            do(dve.reciprocal(e[6], e[6]))
            tt(e[7], e[5], lam_re, ALU.mult)
            tt(e[8], e[4], lam_im, ALU.mult)
            tt(e[7], e[7], e[8], ALU.add)
            tt(e[7], e[7], e[6], ALU.mult)
            tt(e[8], e[4], lam_re, ALU.mult)
            tt(e[9], e[5], lam_im, ALU.mult)
            tt(e[8], e[8], e[9], ALU.subtract)
            tt(e[8], e[8], e[6], ALU.mult)
            ts(e[9], e[8], sign[:, 0:1], ALU.mult)
            ts(e[10], e[8], sign[:, 1:2], ALU.mult)
            for n in (2, 3):
                ts(bc[:, n, :, :], bc[:, n, :, :], sign[:, 0:1], ALU.mult)

            def s5_turn(b):
                def read(key):
                    dve.wait_ge(s_job, b * len(sj.jobs) + sj.number(key))
                    return ps[sj.bank(key)]

                cut = lambda ap: ap.rearrange("p (b g) -> p b g", g=GB)[:, b, :]
                cut3 = lambda ap: ap.rearrange("p (b g) q -> p b g q", g=GB)[:, b]
                over_c = lambda ap: ap.unsqueeze(2).broadcast_to((P, GB, C8))
                over_q = lambda ap: ap.unsqueeze(2).broadcast_to((P, GB, GP))
                tt(t5a[:, :, :], over_c(cut(turn8[:, :])),
                   count[:, :].unsqueeze(1).broadcast_to((P, GB, C8)), ALU.mult)
                fraction(t5a[:, :, :], t5b[:, :, :])
                dve.sem_inc(s5_angle, 1)
                for n in range(2):
                    tt(bb[n][:, :, :], cut3(bc[:, n]), over_q(cut(e[7])), ALU.mult)
                    tt(t5b[:, :, 0:GP], cut3(bc[:, 1 - n]), over_q(cut(e[10 - n])), ALU.mult)
                    tt(bb[n][:, :, :], bb[n][:, :, :], t5b[:, :, 0:GP], ALU.add)

                def outer(o, first, powers_n, one, two):
                    n = powers_n
                    shape = (P, GB, n, GP)
                    pr, pi = (ap[:, first:first + n, :].rearrange("p j (b g) -> p b g j", g=GB)
                              [:, b].unsqueeze(3).broadcast_to(shape)
                              for ap in (pw_re, pw_im))
                    one, two = (ap.unsqueeze(2).broadcast_to(shape) for ap in (one, two))
                    ch(dve.tensor_tensor(o, pr, one, ALU.mult))
                    ch(dve.tensor_tensor(wvt2[:, :, 0:n, :], pi, two, ALU.mult))
                    ch.wait()
                    return dve.tensor_tensor(o, o, wvt2[:, :, 0:n, :], ALU.add)

                outer(wvt[:, :, :, :], 0, T8, bb[0][:, :, :], bb[1][:, :, :]).then_inc(w_ready, 1)
                dve.wait_ge(w_ready, b * 2 + 1)
                outer(wc[:, :, :, :], T8, T8 + 1, cut3(bc[:, 2]), cut3(bc[:, 3])).then_inc(w_ready, 1)
                for n in range(2):
                    p = read(f"k{n}")
                    dve.tensor_copy(kpad[:, 4 * n:4 * n + 4, P:],
                                    p[0:GP, :].rearrange("p (g s) -> p g s", g=4)).then_inc(s_dve, 1)
                ch(dve.tensor_tensor(t5b[0:GP, :, 0:GP],
                                     ident[0:GP, 0:GP].unsqueeze(1).broadcast_to((GP, GB, GP)),
                                     d_row[:, :, :].rearrange("p (b g) q -> p b g q", g=GB)[:, b],
                                     ALU.mult))
                ch.wait()
                dve.wait_ge(s_dve, b * sj.total("dve") + sj.reads("k1"))
                do(dve.tensor_tensor(kpad[:, :, P:P + GP], kpad[:, :, P:P + GP],
                                     t5b[0:GP, :, 0:GP], ALU.add))
                dve.sem_inc(kpad_ready, 1)
                dve.wait_ge(s5_sine, b + 5)
                tt(cosc[:, :, :], cosc[:, :, :], cosc[:, :, :], ALU.mult)
                ts(cosc[:, :, :], cosc[:, :, :], -2.0, ALU.mult, 1.0, ALU.add)
                ts(sinc[:, :, :], sinc[:, :, :], sign[:, 0:1], ALU.mult)
                do(dve.tensor_copy(decay8[:, :, :], over_c(cut(mag8[:, :]))))
                do(dve.memset(decay8[:, :, 0:1], 0.0))
                p = read("vs")
                flat = lambda ap: ap.rearrange("p g c -> p (g c)")
                dve.wait_ge(s_act, b * sj.total("act") + sj.reads("v"))
                ch(dve.tensor_tensor(flat(t5a[:, :, :]), p[:, :], flat(sinc[:, :, :]), ALU.mult))
                ch.wait()
                dve.sem_inc(s_dve, 1)
                tt(t5b[:, :, :], vin[:, :, :], cosc[:, :, :], ALU.mult)
                tt(t5a[:, :, :], t5a[:, :, :], t5b[:, :, :], ALU.add)
                do(dve.tensor_tensor_scan(flat(zst[:, :, :]), flat(decay8[:, :, :]),
                                          flat(t5a[:, :, :]), 0.0, ALU.mult, ALU.add))
                dve.sem_inc(x_ready, 1)
                p = read("zs")
                ch(dve.tensor_tensor(t5a[:, :, :], p[:, :].rearrange("p (g c) -> p g c", g=GB),
                                     sinc[:, :, :], ALU.mult))
                ch.wait()
                dve.sem_inc(s_dve, 1)
                tt(t5b[:, :, :], zst[:, :, :], cosc[:, :, :], ALU.mult)
                do(dve.tensor_tensor(xst[:, :, 1:], t5b[:, :, 0:C8 - 1], t5a[:, :, 0:C8 - 1],
                                     ALU.subtract))
                dve.sem_inc(x_ready, 1)
                dve.wait_ge(s_job, (b + 1) * len(sj.jobs))

            with dve.Fori(0, FT) as b:
                ch.enter(b, 28)
                s5_turn(b)
                ch.leave(FT)
            over(dve, 7)

            dve.wait_ge(gy_in, 16)
            for f in range(FT):
                ch(dve.tensor_copy(zh[:, f, :], gy[:, f, :]))
                ch.wait()
                dve.tensor_tensor(zl[:, f, :], gy[:, f, :], zh[:, f, :].bitcast(F32),
                                  ALU.subtract).then_inc(gy_split, 1)
            for n in range(4):
                u = n % 2
                dve.wait_ge(glu_out, n + 1)
                dve.wait_ge(sgt_in[u], 16 * (n // 2 + 1))
                tt(gsig[u][:, :, :], gsig[u][:, :, :], gy[:, 2 * n:2 * n + 2, :], ALU.mult)
                dve.tensor_tensor(gsig[u][:, :, :], gsig[u][:, :, :], sgt[u][:, :, :],
                                  ALU.mult).then_inc(glu_mixed, 1)
            over(dve, 8)

            def split_mix(layer, tile):
                for kt in range(KT):
                    ch(dve.tensor_copy(zh[:, kt, :], tile(kt)))
                    ch.wait()
                    dve.tensor_tensor(zl[:, kt, :], tile(kt), zh[:, kt, :].bitcast(F32),
                                      ALU.subtract).then_inc(mix_split, 1)

            def add_residual(layer):
                dve.wait_ge(root_done, 2 * layer + 2)
                ch(dve.reciprocal(small[:, 8:12], small[:, 4:8]))
                ch.wait()
                for t in range(TT):
                    do(dve.scalar_tensor_tensor(y6[:, t, :], y6[:, t, :], small[:, 8 + t:9 + t],
                                                gp[layer][:, :], ALU.mult, ALU.mult))
                dve.wait_ge(h_in, 16 * (layer + 1))
                for t in range(TT):
                    ch(dve.tensor_tensor(x6[:, t, :], x6[:, t, :], y6[:, t, :], ALU.add))
                ch.wait()
                dve.sem_inc(h_ready, 1)

            dve.wait_ge(mix_in, 16)
            split_mix(0, lambda kt: y6[:, :, :].rearrange("p a (b t) -> p (a b) t", t=L)[:, kt, :])
            add_residual(0)
            over(dve, 9)

            dve.wait_ge(h_stored, 16)
            norm_x(1, x6)
            split_z(1, ztmp6)
            over(dve, 10)

            dve.wait_ge(rope_in, 64)
            do(dve.tensor_copy(r1[:, :], pos[:, :]))
            ts(r1[:, :], r1[:, :], rope_c[:, 0:1], ALU.mult)
            to_turns(r1[:, :], r2[:, :])
            dve.sem_inc(angle, 1)
            dve.wait_ge(rope_sine, 2)
            tt(r2[:, :], r2[:, :], r2[:, :], ALU.mult)
            ts(rot[0:64, :], r2[0:64, :], -2.0, ALU.mult, 1.0, ALU.add)
            ts(rot[64:, :], r1[64:, :], rope_c[64:, 1:2], ALU.mult)
            dve.wait_ge(piece_used, P_IN1 + 1)
            dve.tensor_tensor(ktmp[:, :], ps[7][:, :], rot[:, :], ALU.mult).then_inc(key_rotated, 1)
            dve.wait_ge(key_folded, 1)
            do(dve.tensor_copy(key_pe[:, :], ps[6][:, :]))
            over(dve, 11)

            dve.wait_ge(c_root, 2)
            for r in (ktmp, rms_kv):
                do(dve.reciprocal(r[:, :], r[:, :]))
            for i in range(8):
                c, r = cq[:, i, :], (ktmp, rms_kv)[i // 4][:, :]
                do(dve.scalar_tensor_tensor(c, c, col(("qn", "kvn")[i // 4], i % 4), r,
                                            ALU.mult, ALU.mult))
                do(dve.tensor_copy(zh[:, i, :], c))
                dve.tensor_tensor(zl[:, i, :], c, zh[:, i, :].bitcast(F32),
                                  ALU.subtract).then_inc(c_split, 1)
            dve.wait_ge(c_split, 8)
            dve.sem_inc(a_dve, aj.total("dve"))
            dve.sem_inc(o_read, 2)

            def attention_turn(k):
                def job(key):
                    dve.wait_ge(a_job, k * len(aj.jobs) + aj.number(key))
                    return ps[aj.bank(key)]

                for a in range(2):
                    p = job(("qp", a))
                    dve.tensor_tensor(qp[a][:, :], p[:, :], rot[:, :], ALU.mult).then_inc(a_dve, 1)
                for i in range(10):
                    if i < 8:
                        a, b = divmod(i, TT)
                        p = job(("s", a, b))
                        do(dve.tensor_reduce(stat[:, 0, i:i + 1], p[:, 0:(b + 1) * P], AX.X, ALU.max))
                        do(dve.tensor_scalar(stat[:, 0, i:i + 1], stat[:, 0, i:i + 1], -SCALE, None,
                                             ALU.mult))
                        dve.sem_inc(max_ready, 1)
                    if i >= 2:
                        n = i - 2
                        a, b = divmod(n, TT)
                        dve.wait_ge(a_act, k * aj.total("act") + (aj.total("act") + aj.reads(("s", a, b))))
                        do(dve.reciprocal(stat[:, 2, n:n + 1], stat[:, 1, n:n + 1]))
                        pr = probs[a][:, b, 0:(b + 1) * P]
                        dve.tensor_scalar(pr, pr, stat[:, 2, n:n + 1], None, ALU.mult)\
                           .then_inc(probs_ready, 1)
                for i in range(8):
                    a, b = divmod(i, TT)
                    p = job(("pt", a, b))
                    w = (b + 1) * P
                    dve.tensor_copy(pt9[i % 2][:, 0:w], p[:, 0:w]).then_inc(a_dve, 1)
                    if i in (5, 7):
                        a = (i - 5) // 2
                        dve.wait_ge(o_ready, k * 2 + (a + 1))
                        o = sg1[:, :, :].rearrange("p (h a) t -> p h a t", a=2)[:, k, a]
                        dve.tensor_tensor(o, o, ps[6 + a][:, :], ALU.mult).then_inc(o_read, 1)

            with dve.Fori(0, H // 2) as k:
                ch.enter(k, 24)
                attention_turn(k)
                ch.leave(H // 2)
            dve.wait_ge(o_read, H + 2)
            over(dve, 12)

            split_mix(1, lambda kt: sg1[:, kt, :])
            add_residual(1)
            over(dve, 13)


def arrange(i):
    f = lambda n: np.ascontiguousarray(i[n])

    def groups(w, rows, width):
        n = w.shape[1] // width
        w = w.reshape(rows // P, P, n, width).transpose(2, 1, 0, 3)
        return w.reshape(-1, P, rows // P * width)

    def halves(g):
        n = g.shape[0]
        return g.reshape(n, P, 2, PIECE).transpose(0, 2, 1, 3).reshape(2 * n, P, PIECE)

    w0 = f("ev_w_in")[0]
    a_in = 4 * W + 128
    pieces = [groups(w0[:, 4 * W:a_in], D, P),
              halves(groups(np.concatenate([w0[:, :4 * W], w0[:, a_in:]], 1), D, 256)),
              groups(f("ev_glu_w")[0], W, 256),
              halves(groups(f("ev_w_out")[0], D, 256))]
    w1 = f("od_w_in")[0]
    pe = w1[:, 1024:1088]
    pe_both = np.concatenate([pe, pe[:, 32:], pe[:, :32]], 1)
    pieces += [groups(pe_both, D, P),
               halves(groups(np.concatenate([w1[:, :1024], w1[:, 1088:]], 1), D, 256))]
    q = f("od_w_q_up")[0].reshape(512, 16, 192)
    q = np.concatenate([q, q[:, :, 160:192], q[:, :, 128:160]], 2)
    kv = f("od_w_kv_up")[0].reshape(512, 16, 256)
    for hp in range(8):
        pieces.append(groups(q[:, 2 * hp:2 * hp + 2].reshape(512, 512), 512, 512))
        k2 = kv[:, 2 * hp:2 * hp + 2, :128].reshape(512, 256)
        v2 = kv[:, 2 * hp:2 * hp + 2, 128:].reshape(512, 256)
        pieces.append(groups(np.concatenate([k2, v2], 1), 512, 512))
    pieces.append(halves(groups(f("od_w_out")[0], D, 256)))
    ws = np.concatenate(pieces, 0)
    assert ws.shape == (N_PIECES, P, PIECE), ws.shape
    ada = np.stack([f("ev_ada_w")[0], f("od_ada_w")[0]]).reshape(2, KT, P, 4, QUARTER)
    vec = {"c": f("c")[0], "mu": f("ev_mu")[0], "pre0": f("ev_norm_pre")[0],
           "ab0": f("ev_ada_b")[0, :2 * D], "w0": f("ev_w0")[0], "a0": f("ev_a0")[0],
           "kk": f("ev_k_k")[0], "ka": f("ev_k_a")[0], "rk": f("ev_r_k")[0],
           "lnxg": f("ev_lnx_g")[0], "lnxb": f("ev_lnx_b")[0], "glub": f("ev_glu_b")[0],
           "pre1": f("od_norm_pre")[0], "ab1": f("od_ada_b")[0, :2 * D],
           "qn": f("od_q_norm")[0], "kvn": f("od_kv_norm")[0]}
    cols = np.concatenate([vec[n].reshape(k, P).T for n, k in VECTORS], 1)
    return {
        **lora_and_masks(f), **s5_layout(f),
        "ws": ws.reshape(N_PIECES // 2, 2, P, PIECE), "ada": np.ascontiguousarray(ada.transpose(0, 1, 3, 2, 4)),
        "cols": np.ascontiguousarray(cols), "ident": np.eye(P, dtype=np.float32),
        "rows": np.stack([f("ev_ada_b")[0, 2 * D:], f("ev_norm_post")[0],
                          f("od_ada_b")[0, 2 * D:], f("od_norm_post")[0]]),
        "x": f("x")[0], **rotary_layout(), "pos": f("positions")[0],
    }


def rotary_layout():
    i = np.arange(P)
    freq = np.float32(1) / np.float32(10000) ** ((2 * (i % 32)).astype(np.float32) / np.float32(64))
    sign = np.where(i < 64, 0, np.where(i < 96, -1, 1))
    return {"rope_c": np.stack([freq, sign], 1).astype(np.float32),
            "fold": (i[:, None] % 64 == i[None] % 64).astype(np.float32),
            "neg_tri": np.where(i[None] > i[:, None], -1e30, 0).astype(np.float32)}


def lora_and_masks(f):
    w2, a2 = (f(n)[0].reshape(64, FT // 2, 2, P).transpose(1, 2, 0, 3) for n in ("ev_w2", "ev_a2"))
    zero = np.zeros_like(w2)
    lora = np.stack([np.concatenate([w2, zero], 2), np.concatenate([zero, a2], 2)], 3)
    i = np.arange(P)
    head, t = i // CH, i % CH
    tri = np.concatenate([t[:, None] <= np.arange(CH)[None],
                          (head[:, None] == head[None]) & (t[:, None] < t[None])], 1)
    corner = np.stack([(i[:, None] // (2 * m) == i[None] // (2 * m)) & (i[:, None] // m % 2 == 1)
                       & (i[None] // m % 2 == 0) for m in (2 ** n for n in range(LEVELS))], 1)
    return {"lora": lora, "tri": tri.astype(np.float32), "corner": corner.astype(np.float32),
            "blk1": (head[:, None] == head[None]).astype(np.float32),
            "starts": np.tile((np.arange(L) % CH != 0).astype(np.float32), (P, 1))}


def s5_layout(f):
    half = np.repeat(np.array([1, -1], np.float32), NS)
    both = lambda a: np.concatenate([a, a], 0)
    step = np.broadcast_to(f("ev_log_dt")[0], (P, G))
    lam = np.stack([both(f("ev_lam_re")[0].T), both(f("ev_lam_im")[0].T), step], 1)
    br, bi = (f(n)[0].transpose(1, 0, 2) for n in ("ev_b_re", "ev_b_im"))
    cr, ci = (f(n)[0].transpose(2, 0, 1) for n in ("ev_c_re", "ev_c_im"))
    bc = np.stack([np.concatenate(x, 0) for x in ((br, bi), (bi, br), (cr, ci), (ci, cr))], 1)
    swap = np.eye(P, dtype=np.float32)[(np.arange(P) + NS) % P]
    expo = np.array([*range(T8 - 1, -1, -1), *range(T8 + 1)], np.float32)
    return {"lam": np.ascontiguousarray(lam), "bc": np.ascontiguousarray(bc), "swap": swap,
            "sign": np.stack([half, -half], 1), "expo": np.tile(expo, (P, 1)),
            "count": np.tile(np.arange(C8, dtype=np.float32), (P, 1)), "d": f("ev_d")[0]}


def kernel(**inputs):
    import concourse.bacc as bacc
    from concourse.bass_utils import run_bass_kernel_spmd

    nc = bacc.Bacc("TRN2", target_bir_lowering=False, num_devices=1)
    arrays, aps = {}, {}
    for name, a in arrange({n: np.asarray(a) for n, a in inputs.items()}).items():
        a = np.ascontiguousarray(a)
        arrays[f"in_{name}_dram"] = a
        aps[name] = nc.dram_tensor(f"in_{name}_dram", a.shape, mybir.dt.from_np(a.dtype),
                                   kind="ExternalInput").ap()
    out = nc.dram_tensor("out_0_dram", (1, L, D), F32, kind="ExternalOutput").ap()
    trunk(nc, aps, out)
    result = run_bass_kernel_spmd(nc, [arrays], core_ids=[0])
    return result.results[0]["out_0_dram"]
```

```python
import concourse.bass as bass
from concourse import mybir
from contextlib import ExitStack
import numpy as np

F32 = mybir.dt.float32
F32R = mybir.dt.float32r
ALU = mybir.AluOpType
ACT = mybir.ActivationFunctionType
AX = mybir.AxisListType

P = 128
D = 2048
L = 512
KT = D // P
TT = L // P
W = D // 2
FT = W // P
HN = 64
CH = 64
NC = L // CH
LEVELS = 6
DECAY = float(np.exp(-0.5))
G, GP, NS = 64, 16, 64
T8 = P // GP
C8 = L // T8
GB = P // GP
NP = 2 * T8 + 1
MAGIC = 12582912.0
TURN = 6.283185307179586
TURN_A = 6.28125
TURN_B = TURN - TURN_A
SAFE_TURN = 6.283185
EPS = 1e-6
LNX_EPS = 64e-5
H = 16
SCALE = 192 ** -0.5
PIECE = 2048
A_SLOTS = 8

P_IN0 = 0
P_GLU = P_IN0 + 1 + 24 * 2
P_OUT0 = P_GLU + 4
P_IN1 = P_OUT0 + 16
P_UP = P_IN1 + 1 + 12 * 2
P_OUT1 = P_UP + 16
N_PIECES = P_OUT1 + 16

VECTORS = (("c", 16), ("mu", 33), ("pre0", 16), ("ab0", 32), ("w0", 8), ("a0", 8),
           ("kk", 8), ("ka", 8), ("rk", 8), ("lnxg", 8), ("lnxb", 8), ("glub", 8),
           ("pre1", 16), ("ab1", 32), ("qn", 4), ("kvn", 4))
COLS, NCOLS = {}, 0
for _name, _n in VECTORS:
    COLS[_name] = (NCOLS, _n)
    NCOLS += _n


class Chain:

    def __init__(self, eng, sem):
        self.eng, self.sem, self.base, self.n = eng, sem, 0, 0

    def __call__(self, ins):
        ins.then_inc(self.sem, 1)
        self.n += 1

    def at(self):
        return self.base + self.n

    def wait(self):
        self.eng.wait_ge(self.sem, self.base + self.n)

    def enter(self, i, per, first=0):
        self.saved, self.per = self.base + self.n, per
        self.base, self.n = i * per + (self.saved - first * per), 0

    def leave(self, turns):
        assert self.n == self.per, (self.n, self.per)
        self.base, self.n = self.saved + turns * self.per, 0


class Banks:

    def __init__(self, banks):
        self.banks, self.jobs = banks, []

    def add(self, key, reader):
        self.jobs.append((key, reader))

    def number(self, key):
        return [k for k, _ in self.jobs].index(key) + 1

    def engine(self, key):
        return dict(self.jobs)[key]

    def copies(self, key):
        who = self.engine(key)
        return [k for k, r in self.jobs if r == who].index(key) + 1

    def total(self, who):
        return sum(r == who for _, r in self.jobs)

    def bank(self, key):
        return self.banks[(self.number(key) - 1) % len(self.banks)]

    def before(self, key):
        n = self.number(key) - 1 - len(self.banks)
        return self.jobs[n][0] if n >= 0 else None


def rwkv_jobs():
    jobs = Banks(range(6))
    for u in range(2):
        jobs.add(("decay", u), "act")
        jobs.add(("rate", u), "act")
    for u in range(2):
        jobs.add(("norm", u), "dve")
    for u in range(2):
        jobs.add(("bonus", u), "dve")
    for u in range(2):
        for x in "bk":
            for c in range(0, NC, 2):
                jobs.add(("pairs", x, u, c), "dve")
        for x in "bkv":
            for c in range(0, NC, 4):
                jobs.add(("turn", x, u, c), "act")
    for n in range(LEVELS):
        for u in range(2):
            for c in range(0, NC, 4):
                jobs.add(("at", n, u, c), "dve")
        for u in range(2):
            for c in range(0, NC, 4):
                if n < LEVELS - 1:
                    jobs.add(("inv", n, u, c), "dve")
                jobs.add(("invT", n, u, c), "dve")
    for c in range(NC):
        for x, who in (("w", "act"), ("u", "act"), ("s", "dve")):
            for u in range(2):
                jobs.add((x, c, u), who)
    for x in ("mean", "var"):
        for u in range(2):
            jobs.add((x, u), "dve" if x == "mean" else "act")
    return jobs


S5_JOBS = {"v": 0, "vs": 1, "uc": 2, "wv0": 3, "wv1": 4, "zs": 5, "k0": 6, "k1": 7,
           "y0": 0, "y1": 1, "yt": 2}
S5_FRONT = ("uc", "wv0", "wv1", "k0", "k1")
S5_COPIES = ("v", "uc", "wv0", "wv1", "y0", "y1", "yt")


def s5_count(turn, key, among=tuple(S5_JOBS)):
    front = [x for x in among if x in S5_FRONT]
    if not isinstance(turn, int):
        k, odd = turn
        return k * (2 * len(among)) + ((odd - 1) * len(among) + len(front) + among.index(key) + 1)
    if turn == 0:
        return front.index(key) + 1
    here = [x for x in among if x not in S5_FRONT] if turn == FT else among
    return (turn - 1) * len(among) + len(front) + here.index(key) + 1


def s5_turns(engine, turn):
    def static(t):
        turn(t, *[divmod(x, 2) if x < FT else None for x in (t - 1, t, t + 1)])

    static(1)
    with engine.Fori(1, FT // 2 - 1) as k:
        turn((k, 0), (k - 1, 1), (k, 0), (k, 1))
        turn((k, 1), (k, 0), (k, 1), (k + 1, 0))
    for t in range(FT - 2, FT + 1):
        static(t)


def attention_jobs():
    jobs = Banks(range(6))
    for a in range(2):
        jobs.add(("qn", a), "act")
        jobs.add(("qp", a), "dve")
        jobs.add(("key", a), "act")
    for n in range(2):
        jobs.add(("v", n), "act")
    for x, who in (("s", "act"), ("pt", "dve")):
        for a in range(2):
            for b in range(TT):
                jobs.add((x, a, b), who)
    assert len(jobs.jobs) % 6 == 0
    return jobs


def trunk(nc, A, out):
    ctx = ExitStack()
    with ctx:
        slab_bytes = (nc.sbuf_usable_end - nc.sbuf_base - 1024) // 32 * 32
        slab = nc.alloc_sbuf_tensor("slab", [P, slab_bytes // 4], F32)
        start = nc.sbuf_base - slab_bytes
        top = [start]

        def sb(name, shape, dt=F32):
            size = 4
            for n in shape[1:]:
                size *= n
            here = top[0]
            top[0] += (size + 31) // 32 * 32
            assert top[0] <= start + slab_bytes, (name, top[0] - start - slab_bytes)
            return nc.alloc_sbuf_tensor_at(name, shape, dt, offset=here)

        def sem(name):
            return ctx.enter_context(nc.semaphore(name))

        def dram(name, shape):
            return nc.dram_tensor(name, shape, F32).ap()

        mixed_d = dram("mixed_d", [16, 2, P, L])
        sgate_d = dram("sgate_d", [4, 2, P, L])
        mix_d = dram("mix_d", [4, 2, P, L])
        gy_d = dram("gy_d", [FT, P, L])
        h1_d = dram("h1_d", [L, D])
        u_d = dram("u_d", [L, W])

        raw = [sb(f"raw{s}", [P, PIECE]) for s in range(2)]
        whi = [sb(f"whi{s}", [P, PIECE], F32R) for s in range(2)]
        wlo = [sb(f"wlo{s}", [P, PIECE], F32R) for s in range(2)]
        cols = sb("cols", [P, NCOLS])
        ident = sb("ident", [P, P])
        ones = sb("ones", [P, P])
        csilu = sb("csilu", [P, 16])
        modc = [sb(f"modc{i}", [P, 32]) for i in range(2)]
        small = sb("small", [P, 16])
        gp = [sb("gp0", [P, D]), None]
        keep = top[0]

        xt = sb("xt", [P, TT, D])
        top1 = top[0]
        top[0] = keep
        gp[1] = sb("gp1", [P, D])
        lo_in = sb("lo_in", [P, L])
        shift = sb("shift", [P, 2, L + 1])
        res = [sb(f"res{s}", [P, 2, L]) for s in range(2)]
        ures = [sb(f"ures{s}", [P, TT, 256]) for s in range(2)]
        assert top[0] <= top1
        keep2 = keep + (D + L) * 4
        top[0] = top1
        post_b = sb("post_b", [P, D])
        acc = sb("acc", [P, 3, D])
        here = top[0]
        ztmp = sb("ztmp", [P, 2, L])
        top[0] = here
        ada2 = [sb(f"ada2_{s}", [P, D]) for s in range(2)]
        here = top[0]
        ada1 = [sb(f"ada1_{s}", [P, D]) for s in range(A_SLOTS)]
        top[0] = here
        zh = sb("zh", [P, KT, L], F32R)
        zl = sb("zl", [P, KT, L], F32R)

        top[0] = keep2
        blk1 = sb("blk1", [P, P])
        starts = sb("starts", [P, L])
        tri = sb("tri", [P, 3 * CH])
        corner = sb("corner", [P, LEVELS, P])
        two = lambda name, shape: [sb(f"{name}{u}", shape) for u in range(2)]
        rkv = two("rkv", [P, 3, L])
        lora = two("lora", [P, 2, P])
        sg = two("sg", [P, L])
        rate = two("rate", [P, L])
        cum = two("cum", [P, L])
        grow = two("grow", [P, NC, CH + 1])
        bonus = two("bonus", [P, L])
        ra = two("ra", [P, NC, 3 * CH])
        wu = two("wu", [P, 2, P])
        state = two("state", [P, 2, P])
        b_t, k_t, v_t = two("b_t", [P, NC, P]), two("k_t", [P, NC, P]), two("v_t", [P, NC, P])
        here = top[0]
        shrink = two("shrink", [P, L])
        kn, sq, root = two("kn", [P, L]), two("sq", [P, L]), two("root", [P, L])
        kp, bv = two("kp", [P, L]), two("bv", [P, L])
        top[0] = here
        rb, rk = two("rb", [P, NC, 3 * CH]), two("rk_", [P, NC, 3 * CH])
        b_d, k_d, v_d = two("b_d", [P, NC, P]), two("k_d", [P, NC, P]), two("v_d", [P, NC, P])
        inv, at_inv, inv_t = b_d, k_d, v_d
        rj = rwkv_jobs()

        top[0] = keep2
        swap = sb("swap", [P, P])
        sign = sb("sign", [P, 2])
        expo = sb("expo", [P, NP])
        count = sb("count", [P, C8])
        lam = sb("lam", [P, 3, G])
        d_row = sb("d_row", [GP, G, GP])
        bc = sb("bc", [P, 4, G, GP])
        e1 = [sb(f"e1_{n}", [P, G]) for n in range(12)]
        pw_re, pw_im, pt1, pt2 = (sb(n, [P, NP, G]) for n in ("pw_re", "pw_im", "pt1", "pt2"))
        turn8, mag8 = sb("turn8", [P, G]), sb("mag8", [P, G])
        bb = [sb(f"bb{n}", [P, GB, GP]) for n in range(2)]
        t5f = sb("t5f", [P, GB, GP])
        turn5 = sb("turn5", [P, GB, C8])
        turn5_tmp = sb("turn5_tmp", [P, GB, C8])
        wvt = sb("wvt", [P, GB, T8, GP])
        wvt2 = sb("wvt2", [P, GB, T8 + 1, GP])
        ucm = sb("ucm", [C8, T8, P])
        ugm = sb("ugm", [C8, GB, P])
        cosc, sinc, decay8, uc = (two(n, [P, GB, C8]) for n in ("cosc", "sinc", "decay8", "uc"))
        wc = two("wc", [P, GB, (T8 + 1) * GP])
        wv, w3 = two("wv", [P, GB, P]), two("w3", [P, GB, P])
        kpad = [sb(f"kpad{n}", [GP, GB, 2 * P]) for n in range(2)]
        t5a, t5b = sb("t5a", [P, GB, C8]), sb("t5b", [P, GB, C8])
        vin, zst, xst = (sb(n, [P, GB, C8]) for n in ("vin", "zst", "xst"))
        ycm = sb("ycm", [C8, T8, P])
        gy_out = sb("gy_out", [P, L])

        top[0] = keep2
        gy = sb("gy", [P, FT, L])
        gsig = [sb(f"gsig{s}", [P, 2, L]) for s in range(2)]
        sgt = [sb(f"sgt{s}", [P, 2, L]) for s in range(2)]
        assert top[0] <= keep2 + TT * D * 4

        top[0] = keep2
        x6 = sb("x6", [P, TT, D])
        y6 = sb("y6", [P, TT, D])
        ztmp6 = sb("ztmp6", [P, 2, L])
        assert top[0] <= keep + 80 * 1024

        top[0] = keep2
        sg1 = sb("sg1", [P, H, L])
        key_pe = sb("key_pe", [P, L])
        rot = sb("rot", [P, L])
        rope_c = sb("rope_c", [P, 2])
        fold = sb("fold", [P, P])
        here = top[0]
        cq = sb("cq", [P, 8, L])
        ktmp = sb("ktmp", [P, L])
        pos = sb("pos", [P, L], mybir.dt.int32)
        r1, r2, rms_kv = sb("r1", [P, L]), sb("r2", [P, L]), sb("rms_kv", [P, L])
        assert top[0] <= keep + 80 * 1024
        top[0] = here
        probs = [sb(f"probs{a}", [P, TT, L]) for a in range(2)]
        qn, qp, key9 = ([sb(f"{n}{a}", [P, L]) for a in range(2)] for n in ("qn", "qp", "key"))
        v9 = sb("v9", [P, TT, 2 * P])
        assert top[0] <= keep + 80 * 1024
        top[0] = keep + 144 * 1024
        pt9 = [sb(f"pt9{n}", [P, L]) for n in range(2)]
        neg_tri = sb("neg_tri", [P, P])
        stat = sb("stat", [P, 3, 8])
        aj = attention_jobs()

        mix_tiles = y6[:, :, :].rearrange("p a (b t) -> p (a b) t", t=L)

        ps = [ctx.enter_context(nc.psum_tensor(f"ps{i}", [P, 512], F32)) for i in range(8)]

        def col(name, i, n=1):
            o = COLS[name][0]
            return cols[:, o + i:o + i + n]

        def rcol(name, i, j=0, step=1, rows=slice(0, P)):
            o, n = COLS[name]
            return cols[rows, o:o + n // step * step].rearrange("p (a b) -> p a b", b=step)[:, i, j:j + 1]

        raw_full = [sem(f"raw_full{s}") for s in range(2)]
        hi_ready, lo_ready, piece_used = sem("hi_ready"), sem("lo_ready"), sem("piece_used")
        phase_over = sem("phase_over")
        dve_chain, act_chain = sem("dve_chain"), sem("act_chain")
        cols_in, ident_in, x_in, gb_in, gp1_in = (sem(n) for n in (
            "cols_in", "ident_in", "x_in", "gb_in", "gp1_in"))
        consts_set, csilu_set = sem("consts_set"), sem("csilu_set")
        ada1_full = [sem(f"ada1_full{s}") for s in range(A_SLOTS)]
        ada2_full = [sem(f"ada2_full{s}") for s in range(2)]
        ada1_used, ada2_used = sem("ada1_used"), sem("ada2_used")
        acc_ready, mod_sums, mod_ready = sem("acc_ready"), sem("mod_sums"), sem("mod_ready")
        x_normed, x_turned, z_scaled = sem("x_normed"), sem("x_turned"), sem("z_scaled")
        z_ready, root_done = sem("z_ready"), sem("root_done")
        proj_out = sem("proj_out")
        mixed = sem("mixed")
        res_stored = [sem(f"res_stored{s}") for s in range(2)]
        u_stored = [sem(f"u_stored{s}") for s in range(2)]

        mask_in = sem("mask_in")
        pair_in = [sem(f"pair_in{u}") for u in range(2)]
        r_job, r_dve, r_act = sem("r_job"), sem("r_dve"), sem("r_act")
        key_squared, cum_done, exp_done, norm_max = (sem(n) for n in (
            "key_squared", "cum_done", "exp_done", "norm_max"))
        norm_root, bonus_in, operands, v_blocks, state_zero = (sem(n) for n in (
            "norm_root", "bonus_in", "operands", "v_blocks", "state_zero"))
        y_out, y_centred, y_squared, y_root = (sem(n) for n in (
            "y_out", "y_centred", "y_squared", "y_root"))
        y_ready, y_copied = sem("y_ready"), sem("y_copied")
        mix_stored = sem("mix_stored")

        s5_in, ucm_in, kpad_ready, u_grouped = (sem(n) for n in (
            "s5_in", "ucm_in", "kpad_ready", "u_grouped"))
        s_job, s_act = sem("s_job"), sem("s_act")
        s5_angle, s5_sine, s5_mag = sem("s5_angle"), sem("s5_sine"), sem("s5_mag")
        w_ready, x_ready, w3_in = sem("w_ready"), sem("x_ready"), [sem(f"w3_in{n}") for n in range(2)]
        gy_stored, gy_in, sgt_in = sem("gy_stored"), sem("gy_in"), [sem(f"sgt_in{s}") for s in range(2)]
        gy_split, glu_out, glu_mixed = sem("gy_split"), sem("glu_out"), sem("glu_mixed")

        mix_in, mix_split, out_read, h_in = (sem(n) for n in ("mix_in", "mix_split", "out_read", "h_in"))
        h_ready, h_stored = sem("h_ready"), sem("h_stored")
        rope_in, angle, rope_sine = sem("rope_in"), sem("angle"), sem("rope_sine")
        in1_read, key_rotated, key_folded = (sem(n) for n in (
            "in1_read", "key_rotated", "key_folded"))
        c_squared, c_summed, c_root, c_split = (sem(n) for n in (
            "c_squared", "c_summed", "c_root", "c_split"))
        a_job, a_act, a_dve = sem("a_job"), sem("a_act"), sem("a_dve")
        max_ready, probs_ready, o_ready, o_read = (sem(n) for n in (
            "max_ready", "probs_ready", "o_ready", "o_read"))

        block = ctx.enter_context(nc.Block())

        def load_piece(sp, k, n):
            s = n % 2
            if isinstance(k, int) and k == 0 and n < 2:
                pass
            else:
                sp.wait_ge(hi_ready, k * 2 + (n - 1))
                sp.wait_ge(lo_ready, k * 2 + (n - 1))
            sp.dma_start(raw[s][:, :], A["ws"][k + n // 2, s]).then_inc(raw_full[s], 16)

        def split_hi(act, k, n):
            s = n % 2
            act.wait_ge(raw_full[s], k * 16 + (n // 2 + 1) * 16)
            if not (isinstance(k, int) and k == 0 and n < 2):
                act.wait_ge(piece_used, k * 2 + (n - 1))
            act.activation(whi[s][:, :], raw[s][:, :], ACT.Copy).then_inc(hi_ready, 1)

        def split_lo(pool, k, n):
            s = n % 2
            pool.wait_ge(hi_ready, k * 2 + (n + 1))
            pool.tensor_tensor(wlo[s][:, :], raw[s][:, :], whi[s][:, :].bitcast(F32),
                               ALU.subtract).then_inc(lo_ready, 1)

        def piece_ready(pe, k, n):
            pe.wait_ge(hi_ready, k * 2 + (n + 1))
            pe.wait_ge(lo_ready, k * 2 + (n + 1))

        def over(eng, n):
            eng.drain().then_inc(phase_over, 1)
            eng.wait_ge(phase_over, 3 * n)

        def ada1_piece(k, n):
            return A["ada"][0].rearrange("(a b) t p f -> a b t p f", b=4)[k, n // 2, n % 2]

        def ada2_first(k, u):
            return (k * 8 + 4 * u) if isinstance(k, int) and k < 2 else k * 6 + (4 + 3 * u)

        def ada2_piece(k, u, q):
            if isinstance(k, int) and k < 2:
                return A["ada"][0, 8 * k + 4 * u + q, 2]
            return A["ada"].rearrange("l (a b) t p f -> (l a) b t p f", b=2)[k + (KT // 2 - 2), u, q]

        @block.sync
        def _(sp):
            sp.dma_start(cols[:, :], A["cols"]).then_inc(cols_in, 16)
            sp.dma_start(ident[:, :], A["ident"]).then_inc(ident_in, 16)
            for n in range(2):
                sp.dma_start(ada1[n][:, :], ada1_piece(0, n)).then_inc(ada1_full[n], 16)
            sp.dma_start(xt[:, :, :], A["x"].rearrange("(a p) d -> p a d", p=P)).then_inc(x_in, 16)
            for n in range(2, A_SLOTS):
                sp.dma_start(ada1[n][:, :], ada1_piece(0, n)).then_inc(ada1_full[n], 16)
            with sp.Fori(1, 2 * KT // A_SLOTS) as k:
                for n in range(A_SLOTS):
                    sp.wait_ge(ada1_used, k * A_SLOTS + (n + 1 - A_SLOTS))
                    sp.dma_start(ada1[n][:, :], ada1_piece(k, n)).then_inc(ada1_full[n], 16)
            load_piece(sp, 0, 0)
            load_piece(sp, 0, 1)
            sp.dma_start(gp[0][:, :], A["rows"][0].partition_broadcast(P)).then_inc(gb_in, 16)
            sp.dma_start(post_b[:, :], A["rows"][1].partition_broadcast(P)).then_inc(gb_in, 16)
            load_piece(sp, 0, 2)
            sp.wait_ge(phase_over, 3)
            sp.dma_start(gp[1][:, :], A["rows"][2].partition_broadcast(P)).then_inc(gp1_in, 16)

            def group_pieces(k, adas):
                for u in range(2):
                    load_piece(sp, k * 2, 2 * u + 3)
                    load_piece(sp, k * 2, 2 * u + 4)
                    for q in range(adas):
                        m = ada2_first(k, u)
                        s = (4 * u + q if adas == 4 else 3 * u + q) % 2
                        if not (isinstance(k, int) and k == 0 and u == 0 and q < 2):
                            sp.wait_ge(ada2_used, m + (q - 1))
                        sp.dma_start(ada2[s][:, :], ada2_piece(k, u, q)).then_inc(ada2_full[s], 16)

            for k in range(2):
                group_pieces(k, 4)
            with sp.Fori(2, 10) as k:
                group_pieces(k, 3)
            sp.wait_ge(mod_ready, 2)
            sp.dma_start(post_b[:, :], A["rows"][3].partition_broadcast(P)).then_inc(gb_in, 16)
            group_pieces(10, 0)
            group_pieces(11, 0)
            sp.wait_ge(phase_over, 6)
            for s in range(2):
                sp.wait_ge(res_stored[s], 16 * 10)
                sp.wait_ge(u_stored[s], 32)
            for name, buf in (("blk1", blk1), ("starts", starts), ("tri", tri), ("corner", corner)):
                sp.dma_start(buf[...], A[name]).then_inc(mask_in, 16)
            with sp.Fori(0, FT // 2) as k:
                sp.wait_ge(phase_over, k * 3 + 6)
                for u in range(2):
                    sp.dma_start(rkv[u][:, :, :], mixed_d.rearrange("(a b) u p t -> b u p a t", a=4)
                                 [k, u, :, 0:3]).then_inc(pair_in[u], 16)
                    sp.dma_start(lora[u][:, :, :], A["lora"][k, u]).then_inc(pair_in[u], 16)
                    sp.dma_start(sg[u][:, :], mixed_d.rearrange("(a b) u p t -> b u p a t", a=4)
                                 [k, u, :, 3]).then_inc(pair_in[u], 16)
            sp.wait_ge(phase_over, 3 * 6)
            for buf, src in ((swap, "swap"), (sign, "sign"), (expo, "expo"), (count, "count"),
                             (lam, "lam"), (bc, "bc")):
                sp.dma_start(buf[...], A[src]).then_inc(s5_in, 16)
            sp.dma_start(d_row[:, :, :].rearrange("p g q -> p (g q)"),
                         A["d"].partition_broadcast(GP)).then_inc(s5_in, 16)

            def load_ucm(b):
                sp.dma_start(ucm[:, :, :], u_d.rearrange("(c j) (b f) -> b c j f", j=T8, f=P)[b])\
                  .then_inc(ucm_in, 16)

            def skewed(b, n):
                sp.wait_ge(kpad_ready, b + (n + 1))
                for i in range(T8):
                    sp.dma_start(w3[n][i * GP:(i + 1) * GP, :, :],
                                 kpad[n][:, :, P - i * GP:2 * P - i * GP]).then_inc(w3_in[n], 16)

            load_ucm(0)
            sp.wait_ge(u_grouped, 1)
            load_ucm(1)
            with sp.Fori(0, FT // 2 - 1) as k:
                for n in range(2):
                    skewed(k * 2, n)
                    sp.wait_ge(u_grouped, k * 2 + (n + 2))
                    load_ucm(k * 2 + (n + 2))
            for n in range(2):
                skewed(FT - 2, n)
            sp.wait_ge(phase_over, 3 * 7)
            sp.dma_start(gy[:, :, :], gy_d.rearrange("f p t -> p f t")).then_inc(gy_in, 16)
            for n in range(2):
                sp.dma_start(sgt[n][:, :, :], sgate_d[n].rearrange("j p t -> p j t"))\
                  .then_inc(sgt_in[n], 16)
            sp.dma_start(mix_tiles[:, 0:FT, :], mix_d[0:4].rearrange("a u p t -> p (a u) t"))\
              .then_inc(mix_in, 16)
            load_piece(sp, 0, P_GLU + 2)
            load_piece(sp, 0, P_GLU + 3)
            for n in range(2, 4):
                load_piece(sp, 0, P_GLU + 2 + n)
                sp.wait_ge(glu_mixed, n - 1)
                sp.dma_start(sgt[n % 2][:, :, :], sgate_d[n].rearrange("j p t -> p j t"))\
                  .then_inc(sgt_in[n % 2], 16)

            sp.wait_ge(glu_mixed, 4)
            sp.dma_start(x6[:, :, :], A["x"].rearrange("(a p) d -> p a d", p=P)).then_inc(h_in, 16)
            with sp.Fori(0, 8) as k:
                load_piece(sp, k, P_OUT0 + 2)
                load_piece(sp, k, P_OUT0 + 3)
            sp.wait_ge(h_ready, 1)
            sp.dma_start(h1_d.rearrange("(a p) d -> p a d", p=P), x6[:, :, :]).then_inc(h_stored, 16)
            sp.wait_ge(phase_over, 3 * 9)
            sp.wait_ge(h_stored, 16)
            sp.dma_start(pos[:, :], A["pos"].partition_broadcast(P)).then_inc(rope_in, 16)
            sp.dma_start(rope_c[:, :], A["rope_c"]).then_inc(rope_in, 16)
            sp.dma_start(fold[:, :], A["fold"]).then_inc(rope_in, 16)
            sp.dma_start(neg_tri[:, :], A["neg_tri"]).then_inc(rope_in, 16)
            load_piece(sp, 0, P_IN1 + 2)
            with sp.Fori(0, 12) as k:
                load_piece(sp, k, P_IN1 + 3)
                load_piece(sp, k, P_IN1 + 4)
            with sp.Fori(0, 8) as k:
                load_piece(sp, k, P_UP + 2)
                load_piece(sp, k, P_UP + 3)
            sp.wait_ge(mix_split, 2 * KT)
            sp.dma_start(x6[:, :, :], h1_d.rearrange("(a p) d -> p a d", p=P)).then_inc(h_in, 16)
            with sp.Fori(0, 7) as k:
                load_piece(sp, k, P_OUT1 + 2)
                load_piece(sp, k, P_OUT1 + 3)
            sp.wait_ge(h_ready, 2)
            sp.dma_start(out[0].rearrange("(a p) d -> p a d", p=P), x6[:, :, :]).then_inc(h_stored, 16)
            sp.wait_ge(h_stored, 32)

        @block.gpsimd
        def _(pool):
            pool.memset(ones[:, :], 1.0).then_inc(consts_set, 1)
            with pool.Fori(0, N_PIECES // 2) as k:
                split_lo(pool, k, 0)
                split_lo(pool, k, 1)

        @block.scalar
        def _(act):
            ch = Chain(act, act_chain)
            act.wait_ge(cols_in, 16)
            act.activation(csilu[:, :], col("c", 0, 16), ACT.Silu).then_inc(csilu_set, 1)

            def norm_stage(layer, xt, ztmp, squares):
                if layer == 0:
                    act.wait_ge(x_in, 16)
                else:
                    act.wait_ge(h_ready, 1)
                for t in range(TT):
                    ch(act.activation(squares[t], xt[:, t, :], ACT.Square, accum_out=small[:, t:t + 1]))
                ch.wait()
                act.activation(small[:, 4:8], small[:, 0:4], ACT.Sqrt, bias=EPS,
                               scale=1.0 / D).then_inc(root_done, 1)
                act.wait_ge(mod_ready, 2 * layer + 1)
                for k in range(KT):
                    act.wait_ge(x_turned, KT * layer + k + 1)
                    if k >= 2:
                        act.wait_ge(z_ready, KT * layer + k - 1)
                    act.activation(ztmp[:, k % 2, :], ps[2 + k % 2][:, :], ACT.Identity,
                                   bias=modc[layer][:, k:k + 1],
                                   scale=modc[layer][:, 16 + k:17 + k]).then_inc(z_scaled, 1)

            norm_stage(0, xt, ztmp, [w[:, :] for w in (*whi, *wlo)])
            split_hi(act, 0, 0)
            over(act, 1)

            split_hi(act, 0, 1)
            act.wait_ge(piece_used, 1)
            act.activation(shift[:, 0, 1:257], ps[7][:, 0:256], ACT.Copy).then_inc(proj_out, 1)
            act.activation(shift[:, 0, 257:], ps[7][:, 256:], ACT.Copy).then_inc(proj_out, 1)
            split_hi(act, 0, 2)
            act.wait_ge(mixed, 1)
            act.activation(lo_in[0:64, :], lo_in[0:64, :], ACT.Tanh)

            def copy_group(k, u):
                split_hi(act, k * 2, 2 * u + 3)
                split_hi(act, k * 2, 2 * u + 4)
                act.wait_ge(piece_used, k * 4 + (2 * u + 3))
                act.wait_ge(mixed, k * 2 + (u + 1))
                ch(act.activation(shift[:, 0, 1:], ps[2 * u][:, :], ACT.Copy))
                act.activation(shift[:, 1, 1:], ps[2 * u + 1][:, :], ACT.Copy).then_inc(proj_out, 1)

            def store_group(k, u, silu):
                act.wait_ge(mixed, k * 2 + (u + 2))
                if silu:
                    ch(act.activation(res[u][:, :, :], res[u][:, :, :], ACT.Silu))
                    ch.wait()
                act.dma_start(mixed_d[k * 2 + u].rearrange("j p t -> p j t"),
                              res[u][:, :, :]).then_inc(res_stored[u], 16)

            with act.Fori(0, 6) as k:
                ch.enter(k, 2)
                for u in range(2):
                    copy_group(k, u)
                    store_group(k, u, False)
                ch.leave(6)
            with act.Fori(6, 8) as k:
                ch.enter(k, 4, 6)
                for u in range(2):
                    copy_group(k, u)
                    store_group(k, u, True)
                ch.leave(2)
            def u_group(k, u, first):
                split_hi(act, k * 2, 2 * u + 3)
                split_hi(act, k * 2, 2 * u + 4)
                act.wait_ge(piece_used, k * 4 + (2 * u + 3))
                if not first:
                    act.wait_ge(u_stored[u], (k - 8) * 16)
                for t in range(TT):
                    o = act.activation(ures[u][:, t, :], ps[4 - 4 * u + t][:, 0:256], ACT.Copy)
                    if t < TT - 1:
                        ch(o)
                o.then_inc(proj_out, 1)
                ch.wait()
                act.wait_ge(proj_out, k * 2 + (u + 3))
                act.dma_start(u_d.rearrange("(a p) (g w) -> g p a w", p=P, w=256)[(k - 8) * 2 + u],
                              ures[u][:, :, :]).then_inc(u_stored[u], 16)

            for k in range(8, 10):
                for u in range(2):
                    u_group(k, u, k == 8)
            for k in range(10, 12):
                for u in range(2):
                    if k * 4 + 2 * u + 4 < P_GLU:
                        split_hi(act, k * 2, 2 * u + 3)
                        split_hi(act, k * 2, 2 * u + 4)
                    act.wait_ge(piece_used, k * 4 + (2 * u + 3))
                    act.wait_ge(res_stored[u], 16 * (k - 2))
                    ch(act.activation(res[u][:, 0, :], ps[4 + 2 * u][:, :], ACT.Silu))
                    act.activation(res[u][:, 1, :], ps[5 + 2 * u][:, :], ACT.Silu).then_inc(proj_out, 1)
                    ch.wait()
                    act.wait_ge(proj_out, k * 2 + (u + 3))
                    act.dma_start(sgate_d[(k - 10) * 2 + u].rearrange("j p t -> p j t"),
                                  res[u][:, :, :]).then_inc(res_stored[u], 16)
            over(act, 2)

            act.wait_ge(state_zero, 6)
            with act.Fori(0, FT // 2) as k:
                ch.enter(k, 2)

                def job(key):
                    act.wait_ge(r_job, k * len(rj.jobs) + rj.number(key))
                    return ps[rj.bank(key)]

                for u in range(2):
                    act.wait_ge(pair_in[u], k * 48 + 48)
                    act.activation(sq[u][:, :], rkv[u][:, 1, :], ACT.Square,
                                   scale=rcol("kk", k, u, 2)).then_inc(key_squared, 1)
                for u in range(2):
                    b = job(("decay", u))
                    act.activation(cum[u][:, :], b[:, :], ACT.Sigmoid,
                                   bias=rcol("w0", k, u, 2)).then_inc(r_act, 1)
                    b = job(("rate", u))
                    act.activation(rate[u][:, :], b[:, :], ACT.Sigmoid,
                                   bias=rcol("a0", k, u, 2)).then_inc(r_act, 1)
                for u in range(2):
                    for h in range(2):
                        act.activation(
                            v_d[u][64 * h:64 * h + 64, :, 64 * h:64 * h + 64],
                            rkv[u][64 * h:64 * h + 64, 2, :].rearrange("p (c t) -> p c t", c=NC),
                            ACT.Copy).then_inc(v_blocks, 1)
                for u in range(2):
                    act.wait_ge(norm_max, k * 2 + (u + 1))
                    act.activation(root[u][:, :], root[u][:, :], ACT.Sqrt).then_inc(norm_root, 1)
                for u in range(2):
                    act.wait_ge(cum_done, k * 2 + (u + 1))
                    ch(act.activation(grow[u][:, :, 1:], cum[u][:, :].rearrange(
                        "p (c t) -> p c t", c=NC), ACT.Exp))
                    act.activation(shrink[u][:, :], cum[u][:, :], ACT.Exp, scale=-1.0)\
                       .then_inc(exp_done, 1)
                for u in range(2):
                    for x, to in (("b", b_t), ("k", k_t), ("v", v_t)):
                        for c in range(0, NC, 4):
                            b = job(("turn", x, u, c))
                            act.activation(to[u][:, c:c + 4, :].rearrange("p c s -> p (c s)"),
                                           b[:, :], ACT.Copy).then_inc(r_act, 1)
                for c in range(NC):
                    for n, x in enumerate("wu"):
                        for u in range(2):
                            b = job((x, c, u))
                            act.activation(wu[u][:, n, :], b[:, 0:P], ACT.Copy).then_inc(r_act, 1)
                for u in range(2):
                    act.wait_ge(y_centred, k * 2 + (u + 1))
                    act.activation(sq[u][:, :], cum[u][:, :], ACT.Square).then_inc(y_squared, 1)
                for u in range(2):
                    b = job(("var", u))
                    act.activation(root[u][:, :], b[:, :], ACT.Sqrt, bias=LNX_EPS,
                                   scale=1.0 / HN).then_inc(r_act, 1)
                for u in range(2):
                    act.wait_ge(y_ready, k * 2 + (u + 1))
                    act.dma_start(mix_d[k, u], cum[u][:, :]).then_inc(mix_stored, 16)
                over(act, k + 3)
                act.wait_ge(mix_stored, k * 32 + 32)
                ch.leave(FT // 2)

            act.wait_ge(s5_in, 16 * 7)
            act.activation(e1[0][:, :], lam[:, 2, :], ACT.Exp).then_inc(s5_mag, 1)
            act.wait_ge(s5_angle, 1)
            act.activation(e1[3][:, :], e1[1][:, :], ACT.Exp).then_inc(s5_mag, 1)
            act.activation(pt1[:, :, :], pw_re[:, :, :], ACT.Exp).then_inc(s5_mag, 1)
            act.activation(mag8[:, :], mag8[:, :], ACT.Exp).then_inc(s5_mag, 1)
            act.activation(e1[4][:, :], e1[2][:, :], ACT.Sin, scale=SAFE_TURN).then_inc(s5_sine, 1)
            act.activation(e1[5][:, :], e1[2][:, :], ACT.Sin, scale=SAFE_TURN / 2).then_inc(s5_sine, 1)
            act.activation(pt2[:, :, :], pw_im[:, :, :], ACT.Sin, scale=SAFE_TURN / 2).then_inc(s5_sine, 1)
            act.wait_ge(s5_sine, 3)
            act.activation(pw_im[:, :, :], pw_im[:, :, :], ACT.Sin, scale=SAFE_TURN).then_inc(s5_sine, 1)

            def job5(turn, key):
                act.wait_ge(s_job, s5_count(turn, key))
                return ps[S5_JOBS[key]]

            def group_u(k, n):
                act.wait_ge(ucm_in, k * 32 + (16 * n + 16))
                act.activation(ugm[:, :, :].rearrange("c g (j p) -> c j g p", j=T8),
                               ucm[:, :, :].rearrange("c j (g p) -> c j g p", g=GB),
                               ACT.Copy).then_inc(u_grouped, 1)

            def sines(k, n):
                act.wait_ge(s5_angle, k * 2 + (n + 2))
                ch(act.activation(cosc[n][:, :, :], turn5[:, :, :], ACT.Sin, scale=SAFE_TURN / 2))
                act.activation(sinc[n][:, :, :], turn5[:, :, :], ACT.Sin, scale=SAFE_TURN)\
                   .then_inc(s5_sine, 1)

            def front5(turn, n):
                p = job5(turn, "uc")
                act.activation(uc[n][:, :, :].rearrange("p g c -> p (g c)"), p[:, :],
                               ACT.Copy).then_inc(s_act, 1)
                for m in range(2):
                    p = job5(turn, f"wv{m}")
                    act.activation(wv[n][:, 4 * m:4 * m + 4, :].rearrange("p g c -> p (g c)"), p[:, :],
                                   ACT.Copy).then_inc(s_act, 1)

            def turn5_act(turn, b, f, g):
                p = job5(turn, "v")
                act.activation(vin[:, :, :].rearrange("p g c -> p (g c)"), p[:, :], ACT.Copy).then_inc(s_act, 1)
                if f:
                    front5(turn, f[1])
                for m in range(2):
                    p = job5(turn, f"y{m}")
                    act.activation(
                        ycm[:, :, 64 * m:64 * m + 64].rearrange("c j (g p) -> c j g p", p=GP),
                        p[0:C8, :].rearrange("c (g j p) -> c j g p", g=4, p=GP), ACT.Copy).then_inc(s_act, 1)
                if g:
                    group_u(*g)
                p = job5(turn, "yt")
                if turn != 1:
                    act.wait_ge(gy_stored, b[0] * 32 + 16 * b[1])
                act.activation(gy_out[:, :].rearrange("p (c j) -> p c j", j=T8),
                               p[:, :].rearrange("p (j c) -> p c j", c=C8),
                               ACT.Gelu_apprx_tanh).then_inc(s_act, 1)
                act.wait_ge(s_act, s5_count(turn, "yt", S5_COPIES))
                act.dma_start(gy_d.rearrange("(a b) p t -> a b p t", b=2)[b[0], b[1]], gy_out[:, :])\
                   .then_inc(gy_stored, 16)
                if g:
                    sines(*g)

            group_u(0, 0)
            sines(0, 0)
            front5(0, 0)
            group_u(0, 1)
            sines(0, 1)

            def act_turn(turn, b, f, g):
                if not isinstance(turn, int) and turn[1] == 0:
                    ch.enter(turn[0], 2, 1)
                turn5_act(turn, b, f, g)
                if not isinstance(turn, int) and turn[1] == 1:
                    ch.leave(FT // 2 - 2)

            s5_turns(act, act_turn)
            act.wait_ge(gy_stored, FT * 16)
            over(act, 7)

            split_hi(act, 0, P_GLU)
            split_hi(act, 0, P_GLU + 1)
            for n in range(4):
                u = n % 2
                if n >= 2:
                    act.wait_ge(glu_mixed, n - 1)
                split_hi(act, 0, P_GLU + 2 + n)
                ch(act.activation(gsig[u][:, 0, :], ps[2 * u][:, :], ACT.Sigmoid, bias=col("glub", 2 * n)))
                act.activation(gsig[u][:, 1, :], ps[2 * u + 1][:, :], ACT.Sigmoid,
                               bias=col("glub", 2 * n + 1)).then_inc(glu_out, 1)

            def out_group(layer, k, u, last=False):
                first = (P_OUT0, P_OUT1)[layer] + 2 * u + 2
                if not last:
                    for h in range(2):
                        split_hi(act, k * 2, first + h)
                act.wait_ge(piece_used, k * 4 + first)
                for t in range(TT):
                    o = act.activation(
                        y6[:, t, :].rearrange("p (a b w) -> p a b w", b=2, w=256)[:, k, u],
                        ps[4 * u + t][:, 0:256], ACT.Copy)
                    ch(o) if t < TT - 1 else o.then_inc(out_read, 1)

            def out_stage(layer):
                act.wait_ge(mix_split, KT * (layer + 1))
                act.sem_inc(out_read, 2)
                with act.Fori(0, 3) as k:
                    ch.enter(k, 6)
                    for u in range(2):
                        out_group(layer, k, u)
                    ch.leave(3)
                for u in range(2):
                    out_group(layer, 3, u, last=(u == 1))
                act.wait_ge(out_read, 10 * layer + 10)
                ch.wait()
                for t in range(TT):
                    ch(act.activation(zl[:, 4 * t:4 * t + 4, :].rearrange("p a b -> p (a b)"),
                                      y6[:, t, :], ACT.Square, accum_out=small[:, t:t + 1]))
                ch.wait()
                act.activation(small[:, 4:8], small[:, 0:4], ACT.Sqrt, bias=EPS,
                               scale=1.0 / D).then_inc(root_done, 1)

            out_stage(0)
            over(act, 8)

            norm_stage(1, x6, ztmp6, [zl[:, 4 * t:4 * t + 4, :].rearrange("p a b -> p (a b)")
                                      for t in range(TT)])
            over(act, 9)

            act.wait_ge(angle, 1)
            act.activation(r2[:, :], r1[:, :], ACT.Sin, scale=SAFE_TURN / 2).then_inc(rope_sine, 1)
            act.wait_ge(rope_sine, 1)
            act.activation(r1[:, :], r1[:, :], ACT.Sin, scale=SAFE_TURN).then_inc(rope_sine, 1)
            for h in range(3):
                split_hi(act, 0, P_IN1 + h)
            act.sem_inc(in1_read, 2)

            def in1_group(k, u, to, func):
                for h in range(2):
                    split_hi(act, k * 2, P_IN1 + 3 + 2 * u + h)
                act.wait_ge(piece_used, k * 4 + (P_IN1 + 3 + 2 * u))
                ch(act.activation(to[0], ps[2 * u][:, :], func))
                act.activation(to[1], ps[2 * u + 1][:, :], func).then_inc(in1_read, 1)

            with act.Fori(0, 2) as k:
                ch.enter(k, 2)
                for u in range(2):
                    in1_group(k, u, [cq[:, :, :].rearrange("p (a b) t -> p a b t", b=4)[:, k, 2 * u + j]
                                     for j in range(2)], ACT.Copy)
                ch.leave(2)
            with act.Fori(0, 4) as k:
                ch.enter(k, 2)
                for u in range(2):
                    in1_group(k + 2, u, [sg1[:, :, :].rearrange("p (a b) t -> p a b t", b=4)[:, k, 2 * u + j]
                                         for j in range(2)], ACT.Silu)
                ch.leave(4)
            over(act, 10)

            for i in range(8):
                if i >= 2:
                    act.wait_ge(c_summed, i - 1)
                act.activation((r1, r2)[i % 2][:, :], cq[:, i, :], ACT.Square).then_inc(c_squared, 1)
            act.wait_ge(c_summed, 8)
            for n, to in enumerate((ktmp, rms_kv)):
                act.activation(to[:, :], ps[6 + n][:, :], ACT.Sqrt, bias=EPS, scale=1.0 / 512)\
                   .then_inc(c_root, 1)
            act.wait_ge(c_split, 8)
            act.sem_inc(a_act, aj.total("act"))
            with act.Fori(0, H // 2) as k:
                def job(key):
                    act.wait_ge(a_job, k * len(aj.jobs) + aj.number(key))
                    return ps[aj.bank(key)]

                for a in range(2):
                    for x, to in (("qn", qn), ("key", key9)):
                        p = job((x, a))
                        act.activation(to[a][:, :], p[:, :], ACT.Copy).then_inc(a_act, 1)
                for n in range(2):
                    p = job(("v", n))
                    act.activation(v9[:, 2 * n:2 * n + 2, :].rearrange("p t v -> p (t v)"), p[:, :],
                                   ACT.Copy).then_inc(a_act, 1)
                split_hi(act, k, P_UP + 2)
                split_hi(act, k, P_UP + 3)
                for a in range(2):
                    for b in range(TT):
                        i, w = TT * a + b, (b + 1) * P
                        act.wait_ge(max_ready, k * 8 + (i + 1))
                        p = job(("s", a, b))
                        act.activation(probs[a][:, b, 0:w], p[:, 0:w], ACT.Exp, scale=SCALE,
                                       bias=stat[:, 0, i:i + 1],
                                       accum_out=stat[:, 1, i:i + 1]).then_inc(a_act, 1)
            over(act, 11)

            out_stage(1)
            over(act, 12)

        @block.tensor
        def _(pe):
            pe.wait_ge(ident_in, 16)
            pe.wait_ge(consts_set, 1)

            def column_sums():
                flat = acc[:, :, :].rearrange("p a b -> p (a b)")
                for j in range(32):
                    last = pe.matmul(ps[0][:, j:j + 1], flat[:, j * P:(j + 1) * P], ones[:, 0:1],
                                     start=True, stop=True)
                return last

            def gate_sums():
                for j in range(4):
                    last = pe.matmul(ps[4 + j][:, :], ones[:, :], acc[:, 2, 512 * j:512 * (j + 1)],
                                     start=True, stop=True)
                return last

            def turn_x(layer, xt):
                pe.wait_ge(x_normed, layer + 1)
                for k in range(KT):
                    if k >= 2:
                        pe.wait_ge(z_scaled, KT * layer + k - 1)
                    for t in range(TT):
                        last = pe.transpose(ps[2 + k % 2][:, t * P:(t + 1) * P],
                                            xt[:, t, k * P:(k + 1) * P], ident[:, :])
                    last.then_inc(x_turned, 1)

            def half_tile(bank, s, h, j, width, wide):
                for kk in range(wide):
                    k = h * wide + kk
                    o = kk * width + j * P
                    hi, lo = whi[s][:, o:o + P], wlo[s][:, o:o + P]
                    for n, (a, b) in enumerate(((hi, zh), (hi, zl), (lo, zh))):
                        last = pe.matmul(bank, a, b[:, k, :], start=(k == 0 and n == 0),
                                         stop=(k == KT - 1 and n == 2))
                return last

            def group(k, n, b):
                for h in range(2):
                    piece_ready(pe, k, n + h)
                    for j in range(2):
                        last = half_tile(ps[b + j][:, :], (n + h) % 2, h, j, 256, 8)
                    last.then_inc(piece_used, 1)
                return last

            pe.wait_ge(acc_ready, 1)
            column_sums().then_inc(mod_sums, 1)
            turn_x(0, xt)
            pe.wait_ge(z_ready, KT)
            over(pe, 1)

            piece_ready(pe, 0, 0)
            half_tile(ps[7][:, :], 0, 0, 0, P, KT).then_inc(piece_used, 1)
            for first, end in ((0, 2), (2, 8)):
                with pe.Fori(first, end) as k:
                    for u in range(2):
                        pe.wait_ge(proj_out, k * 2 + (u + 1))
                        group(k * 2, 2 * u + 1, 2 * u)
                if first == 0:
                    pe.wait_ge(acc_ready, 2)
                    gate_sums().then_inc(mod_sums, 1)
            pe.wait_ge(mod_ready, 2)
            with pe.Fori(8, 10) as k:
                for u in range(2):
                    pe.wait_ge(proj_out, k * 2 + (u + 1))
                    for h in range(2):
                        piece_ready(pe, k * 2, 2 * u + 1 + h)
                        s = (1 + h) % 2
                        for t in range(TT):
                            for kk in range(8):
                                kt = h * 8 + kk
                                hi, lo = (w[s][:, kk * 256:(kk + 1) * 256] for w in (whi, wlo))
                                for n, (a, b) in enumerate(((zh, hi), (zl, hi), (zh, lo))):
                                    last = pe.matmul(ps[4 - 4 * u + t][:, 0:256],
                                                     a[:, kt, t * P:(t + 1) * P], b,
                                                     start=(kt == 0 and n == 0),
                                                     stop=(kt == KT - 1 and n == 2))
                        last.then_inc(piece_used, 1)
            with pe.Fori(10, 12) as k:
                for u in range(2):
                    pe.wait_ge(proj_out, k * 2 + (u + 1))
                    group(k * 2, 2 * u + 1, 4 + 2 * u)
            pe.wait_ge(proj_out, 2 + 24)
            pe.wait_ge(acc_ready, 3)
            column_sums()
            gate_sums().then_inc(mod_sums, 1)
            over(pe, 2)

            pe.wait_ge(mask_in, 64)
            with pe.Fori(0, FT // 2) as k:
                def has_read(*keys):
                    for who, count in (("dve", r_dve), ("act", r_act)):
                        counts = [rj.copies(x) for x in keys if rj.engine(x) == who]
                        if counts:
                            pe.wait_ge(count, k * rj.total(who) + max(counts))

                def bank(key, *needs):
                    old = rj.before(key)
                    has_read(*needs, *([] if old is None else [old]))
                    return ps[rj.bank(key)]

                def mm(out_ap, a, b, start, stop):
                    return pe.matmul(out_ap, a, b, start=start, stop=stop)

                for u in range(2):
                    pe.wait_ge(pair_in[u], k * 48 + 48)
                    for n, x in enumerate(("decay", "rate")):
                        b = bank((x, u))
                        mm(b[:, :], lora[u][:, n, :], lo_in[:, :], True, True).then_inc(r_job, 1)
                for u in range(2):
                    b = bank(("norm", u))
                    pe.wait_ge(key_squared, k * 2 + (u + 1))
                    mm(b[:, :], blk1[:, :], sq[u][:, :], True, True).then_inc(r_job, 1)
                for u in range(2):
                    b = bank(("bonus", u))
                    pe.wait_ge(bonus_in, k * 2 + (u + 1))
                    mm(b[:, :], blk1[:, :], bonus[u][:, :], True, True).then_inc(r_job, 1)
                for u in range(2):
                    for x, src in (("b", b_d), ("k", k_d)):
                        for c in range(0, NC, 2):
                            b = bank(("pairs", x, u, c))
                            pe.wait_ge(operands, k * 2 + (u + 1))
                            for i in range(2):
                                last = mm(b[:, i * 192:i * 192 + 192], src[u][:, c + i, :],
                                          ra[u][:, c + i, :], True, True)
                            last.then_inc(r_job, 1)
                    for x, src in (("b", b_d), ("k", k_d), ("v", v_d)):
                        for c in range(0, NC, 4):
                            b = bank(("turn", x, u, c))
                            if x == "v":
                                pe.wait_ge(v_blocks, k * 4 + (2 * u + 2))
                            for i in range(4):
                                last = pe.transpose(b[:, i * P:(i + 1) * P],
                                                    src[u][:, c + i, :], ident[:, :])
                            last.then_inc(r_job, 1)
                for n in range(LEVELS):
                    for u in range(2):
                        for c in range(0, NC, 4):
                            b = bank(("at", n, u, c), ("inv", n - 1, u, c) if n else
                                     ("pairs", "b", u, c + 2))
                            for i in range(4):
                                last = mm(b[:, i * P:(i + 1) * P], rb[u][:, c + i, CH:],
                                          ident[:, :] if n == 0 else inv[u][:, c + i, :],
                                          True, True)
                            last.then_inc(r_job, 1)
                    for u in range(2):
                        for c in range(0, NC, 4):
                            for x in ("inv", "invT") if n < LEVELS - 1 else ("invT",):
                                b = bank((x, n, u, c), ("at", n, u, c),
                                         *([("invT", n - 1, u, c)] if n else []))
                                for i in range(4):
                                    t = ident[:, :] if n == 0 else inv_t[u][:, c + i, :]
                                    y = at_inv[u][:, c + i, :]
                                    last = mm(b[:, i * P:(i + 1) * P], *((t, y) if x == "inv" else (y, t)),
                                              True, True)
                                last.then_inc(r_job, 1)
                for c in range(NC):
                    old, new = c % 2, (c + 1) % 2
                    for u in range(2):
                        b = bank(("w", c, u), *([] if c else [("turn", "v", u, 4),
                                                              ("pairs", "k", u, 6)]))
                        mm(b[:, 0:P], rk[u][:, c, CH:], v_t[u][:, c, :], True, False)
                        if c:
                            has_read(("s", c - 1, u))
                        else:
                            pe.wait_ge(state_zero, k * 2 + 8)
                        mm(b[:, 0:P], ra[u][:, c, CH:], state[u][:, old, :], False, True)\
                            .then_inc(r_job, 1)
                    for u in range(2):
                        b = bank(("u", c, u), ("w", c, u),
                                 *([] if c else [("invT", LEVELS - 1, u, 4)]))
                        mm(b[:, 0:P], inv_t[u][:, c, :], wu[u][:, 0, :], True, True).then_inc(r_job, 1)
                    for u in range(2):
                        b = bank(("s", c, u))
                        mm(b[:, 0:P], ident[:, :], state[u][:, old, :], True, False)
                        mm(b[:, 0:P], k_t[u][:, c, :], v_t[u][:, c, :], False, False)
                        has_read(("u", c, u))
                        mm(b[:, 0:P], b_t[u][:, c, :], wu[u][:, 1, :], False, True)\
                            .then_inc(r_job, 1)
                    for u in range(2):
                        y = ps[6 + u][:, c * CH:(c + 1) * CH]
                        mm(y, state[u][:, old, :], ra[u][:, c, 0:CH], True, False)
                        mm(y, wu[u][:, 1, :], rb[u][:, c, 0:CH], False, False)
                        last = mm(y, v_t[u][:, c, :], rk[u][:, c, 0:CH], False, True)
                        if c == NC - 1:
                            last.then_inc(y_out, 1)
                for u in range(2):
                    b = bank(("mean", u))
                    pe.wait_ge(y_copied, k * 2 + (u + 1))
                    mm(b[:, :], blk1[:, :], cum[u][:, :], True, True).then_inc(r_job, 1)
                for u in range(2):
                    b = bank(("var", u))
                    pe.wait_ge(y_squared, k * 2 + (u + 1))
                    mm(b[:, :], blk1[:, :], sq[u][:, :], True, True).then_inc(r_job, 1)
                over(pe, k + 3)

            pe.wait_ge(s5_in, 16 * 7)

            def copied(turn, key):
                pe.wait_ge(s_act, s5_count(turn, key, S5_COPIES))

            def turn_tables(turn, k, n):
                p = ps[S5_JOBS["uc"]]
                pe.wait_ge(u_grouped, k * 2 + (n + 1))
                for g in range(GB):
                    last = pe.matmul(p[:, g * C8:(g + 1) * C8], ugm[:, g, :], ident[0:C8, 0:C8],
                                     start=True, stop=True)
                last.then_inc(s_job, 1)
                pe.wait_ge(w_ready, k * 4 + (2 * n + 1))
                for m in range(2):
                    p = ps[S5_JOBS[f"wv{m}"]]
                    for g in range(4):
                        last = pe.transpose(p[:, g * P:(g + 1) * P], wvt[:, 4 * m + g, :, :].rearrange(
                            "p j q -> p (j q)"), ident[:, :])
                    last.then_inc(s_job, 1)

            def response(turn, k, n):
                pe.wait_ge(w_ready, k * 4 + (2 * n + 2))
                for m in range(2):
                    p = ps[S5_JOBS[f"k{m}"]]
                    for g in range(4):
                        last = pe.matmul(p[0:GP, g * P:(g + 1) * P], bb[0][:, 4 * m + g, :],
                                         wc[n][:, 4 * m + g, 0:P], start=True, stop=True)
                    last.then_inc(s_job, 1)

            def pe_turn(turn, b, f, g):
                k, n = b
                if turn == 1:
                    copied(0, "wv1")
                else:
                    copied(turn - 1 if isinstance(turn, int) else (turn[0], turn[1] - 1), "y0")
                p = ps[S5_JOBS["v"]]
                for g in range(GB):
                    last = pe.matmul(p[:, g * C8:(g + 1) * C8], wv[n][:, g, :], uc[n][:, g, :],
                                     start=True, stop=True)
                last.then_inc(s_job, 1)
                copied(turn, "v")
                p = ps[S5_JOBS["vs"]]
                pe.matmul(p[:, :], swap[:, :], vin[:, :, :], start=True, stop=True).then_inc(s_job, 1)
                if f:
                    turn_tables(turn, *f)
                p = ps[S5_JOBS["zs"]]
                pe.wait_ge(x_ready, k * 4 + (2 * n + 1))
                pe.matmul(p[:, :], swap[:, :], zst[:, :, :], start=True, stop=True).then_inc(s_job, 1)
                if f:
                    response(turn, *f)
                pe.wait_ge(x_ready, k * 4 + (2 * n + 2))
                pe.wait_ge(w3_in[n], k * 128 + 128)
                for m in range(2):
                    p = ps[S5_JOBS[f"y{m}"]]
                    for g in range(4):
                        o = p[0:C8, g * P:(g + 1) * P]
                        pe.matmul(o, xst[:, 4 * m + g, :], wc[n][:, 4 * m + g, GP:], start=True, stop=False)
                        last = pe.matmul(o, uc[n][:, 4 * m + g, :], w3[n][:, 4 * m + g, :],
                                         start=False, stop=True)
                    last.then_inc(s_job, 1)
                copied(turn, "y1")
                p = ps[S5_JOBS["yt"]]
                for j in range(T8):
                    last = pe.matmul(p[:, j * C8:(j + 1) * C8], ycm[:, j, :], ident[0:C8, 0:C8],
                                     start=True, stop=True)
                last.then_inc(s_job, 1)

            turn_tables(0, 0, 0)
            response(0, 0, 0)
            s5_turns(pe, pe_turn)
            over(pe, 7)

            pe.wait_ge(gy_split, FT)
            for n in range(4):
                u = n % 2
                if n >= 2:
                    pe.wait_ge(glu_out, n - 1)
                piece_ready(pe, 0, P_GLU + n)
                s = (P_GLU + n) % 2
                for j in range(2):
                    for kt in range(FT):
                        o = kt * 256 + j * P
                        hi, lo = whi[s][:, o:o + P], wlo[s][:, o:o + P]
                        for m, (a, b) in enumerate(((hi, zh), (hi, zl), (lo, zh))):
                            last = pe.matmul(ps[2 * u + j][:, :], a, b[:, FT + kt, :],
                                             start=(kt == 0 and m == 0), stop=(kt == FT - 1 and m == 2))
                last.then_inc(piece_used, 1)

            def out_gemm(layer, first_piece):
                with pe.Fori(0, 4) as k:
                    for u in range(2):
                        pe.wait_ge(out_read, k * 2 + (10 * layer + u + 1))
                        for h in range(2):
                            pe.wait_ge(mix_split, KT * layer + FT * (h + 1))
                            n = first_piece + 2 * u + h
                            piece_ready(pe, k * 2, n)
                            time_major(4 * u, n % 2, h)

            def time_major(bank, s, h):
                for t in range(TT):
                    for kk in range(8):
                        kt = h * 8 + kk
                        hi, lo = (w[s][:, kk * 256:(kk + 1) * 256] for w in (whi, wlo))
                        for n, (a, b) in enumerate(((zh, hi), (zl, hi), (zh, lo))):
                            last = pe.matmul(ps[bank + t][:, 0:256], a[:, kt, t * P:(t + 1) * P], b,
                                             start=(kt == 0 and n == 0), stop=(kt == KT - 1 and n == 2))
                last.then_inc(piece_used, 1)

            out_gemm(0, P_OUT0)
            over(pe, 8)

            turn_x(1, x6)
            pe.wait_ge(z_ready, 2 * KT)
            over(pe, 9)

            piece_ready(pe, 0, P_IN1)
            half_tile(ps[7][:, :], P_IN1 % 2, 0, 0, P, KT).then_inc(piece_used, 1)
            pe.wait_ge(key_rotated, 1)
            pe.matmul(ps[6][:, :], fold[:, :], ktmp[:, :], start=True, stop=True).then_inc(key_folded, 1)
            with pe.Fori(0, 6) as k:
                for u in range(2):
                    pe.wait_ge(in1_read, k * 2 + (u + 1))
                    group(k * 2, P_IN1 + 1 + 2 * u, 2 * u)
            over(pe, 10)

            for i in range(8):
                pe.wait_ge(c_squared, i + 1)
                pe.matmul(ps[6 + i // 4][:, :], ones[:, :], (r1, r2)[i % 2][:, :],
                          start=(i % 4 == 0), stop=(i % 4 == 3)).then_inc(c_summed, 1)
            pe.wait_ge(c_split, 8)
            with pe.Fori(0, H // 2) as k:
                def read9(*keys):
                    for who, count in (("dve", a_dve), ("act", a_act)):
                        turn = aj.total(who)
                        counts = [turn + aj.copies(x) for x in keys if aj.engine(x) == who]
                        if counts:
                            pe.wait_ge(count, k * turn + max(counts))

                def bank9(key, *needs):
                    old, counts = aj.before(key), {"dve": [], "act": []}
                    for x in (*needs, *([old] if old else [])):
                        counts[aj.engine(x)].append(aj.total(aj.engine(x)) + aj.copies(x))
                    if old is None:
                        x = aj.jobs[aj.number(key) - 1 - len(aj.banks)][0]
                        counts[aj.engine(x)].append(aj.copies(x))
                    for who, count in (("dve", a_dve), ("act", a_act)):
                        if counts[who]:
                            pe.wait_ge(count, k * aj.total(who) + max(counts[who]))
                    return ps[aj.bank(key)]

                def up(p, s, first, cs, left=False):
                    for kt in range(4):
                        o = kt * 512 + first
                        hi, lo = whi[s][:, o:o + P], wlo[s][:, o:o + P]
                        for n, (a, b) in enumerate(((hi, zh), (hi, zl), (lo, zh))):
                            last = pe.matmul(p[:, :], a, b[:, cs + kt, :], start=(kt == 0 and n == 0),
                                             stop=(kt == 3 and n == 2))
                            if left and kt == 0 and n == 0:
                                last.then_inc(piece_used, 1)
                    return last

                piece_ready(pe, k, P_UP)
                for a in range(2):
                    for n, x in enumerate(("qn", "qp", "key")):
                        p = bank9((x, a))
                        if x == "key":
                            if a == 0:
                                piece_ready(pe, k, P_UP + 1)
                            last = up(p, (P_UP + 1) % 2, a * P, 4, left=(a == 1))
                        else:
                            last = up(p, P_UP % 2, a * 256 + n * P, 0)
                        last.then_inc(a_job, 1)
                for n in range(2):
                    p = bank9(("v", n))
                    for t in range(2):
                        for kt in range(4):
                            o = kt * 512 + 256
                            s = (P_UP + 1) % 2
                            hi, lo = (w[s][:, o:o + 256] for w in (whi, wlo))
                            for m, (x, y) in enumerate(((zh, hi), (zl, hi), (zh, lo))):
                                tok = (2 * n + t) * P
                                last = pe.matmul(p[:, t * 256:(t + 1) * 256], x[:, 4 + kt, tok:tok + P],
                                                 y, start=(kt == 0 and m == 0), stop=(kt == 3 and m == 2))
                    last.then_inc(a_job, 1)
                for a in range(2):
                    for b in range(TT):
                        w, q = (b + 1) * P, slice(b * P, (b + 1) * P)
                        p = bank9(("s", a, b), ("qn", a), ("qp", a), ("key", a))
                        first = pe.matmul(p[:, 0:w], qn[a][:, q], key9[a][:, 0:w], start=True, stop=False)
                        if a == 0 and b == 0:
                            first.then_inc(piece_used, 1)
                        pe.matmul(p[:, q], ident[:, :], neg_tri[:, :], start=False, stop=False,
                                  skip_group_check=True)
                        pe.matmul(p[:, 0:w], qp[a][:, q], key_pe[:, 0:w], start=False, stop=True)\
                          .then_inc(a_job, 1)

                def turn_probs(i):
                    a, b = divmod(i, TT)
                    p = bank9(("pt", a, b))
                    pe.wait_ge(probs_ready, k * 8 + (i + 1))
                    for n in range(b + 1):
                        last = pe.transpose(p[:, n * P:(n + 1) * P], probs[a][:, b, n * P:(n + 1) * P],
                                            ident[:, :])
                    last.then_inc(a_job, 1)

                def weigh(i):
                    a, b = divmod(i, TT)
                    if b == 0:
                        pe.wait_ge(o_read, k * 2 + (a + 1))
                    read9(("pt", a, b))
                    for n in range(b + 1):
                        last = pe.matmul(ps[6 + a][:, b * P:(b + 1) * P], v9[:, n, a * P:(a + 1) * P],
                                         pt9[i % 2][:, n * P:(n + 1) * P], start=(n == 0), stop=(n == b))
                    if b == TT - 1:
                        last.then_inc(o_ready, 1)

                turn_probs(0)
                for i in range(1, 8):
                    turn_probs(i)
                    weigh(i - 1)
                weigh(7)
            over(pe, 11)

            out_gemm(1, P_OUT1)
            over(pe, 12)

        @block.vector
        def _(dve):
            ch = Chain(dve, dve_chain)
            ch(dve.memset(acc[:, 0:2, :], 0.0))
            dve.wait_ge(csilu_set, 1)
            ch.wait()

            def add_ada(part, piece, c, done):
                dve.scalar_tensor_tensor(acc[:, part, :], piece[:, :], c, acc[:, part, :],
                                         ALU.mult, ALU.add).then_inc(done, 1)

            def add_ada1(k):
                for n in range(A_SLOTS):
                    dve.wait_ge(ada1_full[n], k * 16 + 16)
                    if isinstance(k, int):
                        c = csilu[:, 4 * k + n // 2:4 * k + n // 2 + 1]
                    else:
                        c = csilu[:, :].rearrange("p (a b) -> p a b", b=4)[:, k, n // 2:n // 2 + 1]
                    if n >= 2 or not isinstance(k, int):
                        dve.wait_ge(ada1_used, k * 8 + (n - 1))
                    add_ada(n % 2, ada1[n], c, ada1_used)

            def add_ada2(k, u, adas):
                for q in range(adas):
                    if adas == 4:
                        m = 8 * k + 4 * u + q
                        dve.wait_ge(ada2_full[m % 2], 16 * (m // 2 + 1))
                        if m:
                            dve.wait_ge(ada2_used, m)
                        add_ada(2, ada2[m % 2], csilu[:, m:m + 1], ada2_used)
                    else:
                        dve.wait_ge(ada2_full[(3 * u + q) % 2], k * 48 + 16 * (3 + (3 * u + q) // 2))
                        dve.wait_ge(ada2_used, k * 6 + (2 + 3 * u + q))
                        add_ada(q, ada2[(3 * u + q) % 2], csilu[:, :].rearrange(
                            "p (a b) -> p a b", b=2)[:, k - 2, u:u + 1], ada2_used)

            def finish_columns(layer):
                m = modc[layer]
                ch(dve.tensor_tensor(m[:, :], ps[0][:, 0:32], col(f"ab{layer}", 0, 32), ALU.add))
                ch.wait()
                ch(dve.scalar_tensor_tensor(m[:, 16:32], m[:, 16:32], 1.0, col(f"pre{layer}", 0, 16),
                                            ALU.add, ALU.mult))
                ch.wait()

            def finish_gate(layer):
                dve.wait_ge(gb_in, 16 * (2 + layer))
                if layer == 1:
                    dve.wait_ge(gp1_in, 16)
                for j in range(4):
                    ch(dve.tensor_tensor(gp[layer][:, j * 512:(j + 1) * 512], ps[4 + j][:, :],
                                         gp[layer][:, j * 512:(j + 1) * 512], ALU.add))
                ch.wait()
                ch(dve.tensor_tensor(gp[layer][:, :], gp[layer][:, :], post_b[:, :], ALU.mult))
                ch.wait()

            def norm_x(layer, xt):
                dve.wait_ge(root_done, 2 * layer + 1)
                ch(dve.reciprocal(small[:, 8:12], small[:, 4:8]))
                ch.wait()
                for t in range(TT):
                    o = dve.tensor_scalar(xt[:, t, :], xt[:, t, :], small[:, 8 + t:9 + t], None,
                                          ALU.mult)
                    if t < TT - 1:
                        ch(o)
                ch.wait()
                o.then_inc(x_normed, 1)

            def split_z(layer, ztmp):
                for k in range(KT):
                    dve.wait_ge(z_scaled, KT * layer + k + 1)
                    ch(dve.tensor_copy(zh[:, k, :], ztmp[:, k % 2, :]))
                    ch.wait()
                    dve.tensor_tensor(zl[:, k, :], ztmp[:, k % 2, :], zh[:, k, :].bitcast(F32),
                                      ALU.subtract).then_inc(z_ready, 1)

            add_ada1(0)
            norm_x(0, xt)
            with dve.Fori(1, 2 * KT // A_SLOTS) as k:
                add_ada1(k)
            dve.wait_ge(ada1_used, 2 * KT)
            dve.sem_inc(acc_ready, 1)
            dve.wait_ge(mod_sums, 1)
            finish_columns(0)
            dve.sem_inc(mod_ready, 1)
            split_z(0, ztmp)
            over(dve, 1)

            ch(dve.memset(shift[:, :, 0:1], 0.0))
            ch(dve.memset(acc[:, :, :], 0.0))
            ch.wait()

            def mix(j, out_ap, mu, o_inc=None):
                ch(dve.tensor_tensor(out_ap, shift[:, j, 0:L], shift[:, j, 1:], ALU.subtract))
                ch.wait()
                return dve.scalar_tensor_tensor(out_ap, out_ap, mu, shift[:, j, 1:],
                                                ALU.mult, ALU.add)

            dve.wait_ge(proj_out, 2)
            mix(0, lo_in[:, :], col("mu", 32)).then_inc(mixed, 1)

            def mix_group(k, u, first):
                dve.wait_ge(proj_out, k * 2 + (u + 3))
                if not first:
                    dve.wait_ge(res_stored[u], k * 16)
                ch(mix(0, res[u][:, 0, :], rcol("mu", k, 2 * u, 4)))
                mix(1, res[u][:, 1, :], rcol("mu", k, 2 * u + 1, 4)).then_inc(mixed, 1)

            for k in range(2):
                for u in range(2):
                    add_ada2(k, u, 4)
                    if k == 1 and u == 1:
                        dve.wait_ge(ada2_used, KT)
                        dve.sem_inc(acc_ready, 1)
                    mix_group(k, u, k == 0)
            dve.wait_ge(mod_sums, 2)
            finish_gate(0)
            dve.sem_inc(mod_ready, 1)
            ch(dve.memset(acc[:, :, :], 0.0))
            ch.wait()
            with dve.Fori(2, 8) as k:
                ch.enter(k, 6, 2)
                for u in range(2):
                    add_ada2(k, u, 3)
                    mix_group(k, u, False)
                ch.leave(6)
            with dve.Fori(8, 10) as k:
                for u in range(2):
                    add_ada2(k, u, 3)
            dve.wait_ge(ada2_used, 4 * KT)
            dve.sem_inc(acc_ready, 1)
            dve.wait_ge(mod_sums, 3)
            finish_columns(1)
            finish_gate(1)
            dve.sem_inc(mod_ready, 1)
            over(dve, 2)

            for u in range(2):
                for b in (b_d, k_d, v_d):
                    dve.memset(b[u][:, :, :], 0.0).then_inc(state_zero, 1)
                ch(dve.memset(ra[u][:, :, :], 0.0))
                ch(dve.memset(grow[u][:, :, 0:1], 1.0))
            ch.wait()
            dve.wait_ge(state_zero, 6)
            dve.wait_ge(mask_in, 64)

            def rwkv_turn(k):
                def read(key):
                    dve.wait_ge(r_job, k * len(rj.jobs) + rj.number(key))
                    return ps[rj.bank(key)]

                chunks = lambda ap: ap.rearrange("p (c t) -> p c t", c=NC)
                for u in range(2):
                    dve.memset(state[u][:, 0, :], 0.0).then_inc(state_zero, 1)
                for u in range(2):
                    b = read(("norm", u))
                    ch(dve.tensor_scalar(root[u][:, :], b[:, :], 1e-24, None, ALU.max))
                    ch.wait()
                    dve.sem_inc(norm_max, 1)
                    dve.sem_inc(r_dve, 1)
                for u in range(2):
                    dve.wait_ge(r_act, k * rj.total("act") + rj.copies(("decay", u)))
                    ch(dve.tensor_scalar(cum[u][:, :], cum[u][:, :], -DECAY, None, ALU.mult))
                    ch.wait()
                    dve.tensor_tensor_scan(cum[u][:, :], starts[:, :], cum[u][:, :], 0.0,
                                           ALU.mult, ALU.add).then_inc(cum_done, 1)
                for u in range(2):
                    r, key, v = (rkv[u][:, n, :] for n in range(3))
                    dve.wait_ge(norm_root, k * 2 + (u + 1))
                    dve.wait_ge(r_act, k * rj.total("act") + rj.copies(("rate", u)))
                    ch(dve.reciprocal(root[u][:, :], root[u][:, :]))
                    ch(dve.tensor_scalar(bv[u][:, :], rate[u][:, :], -1.0, rcol("ka", k, u, 2),
                                         ALU.add, ALU.mult))
                    ch.wait()
                    ch(dve.scalar_tensor_tensor(kn[u][:, :], key, rcol("kk", k, u, 2),
                                                root[u][:, :], ALU.mult, ALU.mult))
                    ch(dve.scalar_tensor_tensor(kp[u][:, :], bv[u][:, :], 1.0, key,
                                                ALU.add, ALU.mult))
                    ch.wait()
                    ch(dve.scalar_tensor_tensor(bonus[u][:, :], r, rcol("rk", k, u, 2),
                                                kp[u][:, :], ALU.mult, ALU.mult))
                    ch(dve.tensor_tensor(bv[u][:, :], kn[u][:, :], rate[u][:, :], ALU.mult))
                    ch.wait()
                    dve.sem_inc(bonus_in, 1)
                for u in range(2):
                    dve.wait_ge(exp_done, k * 2 + (u + 1))
                    ch(dve.tensor_tensor(ra[u][:, :, 0:CH], chunks(rkv[u][:, 0, :]),
                                         grow[u][:, :, 1:], ALU.mult))
                    for h in range(2):
                        rows, blk = slice(64 * h, 64 * h + 64), slice(64 * h, 64 * h + 64)
                        ch(dve.scalar_tensor_tensor(
                            ra[u][rows, :, CH + 64 * h:CH + 64 * h + 64], chunks(kn[u][rows, :]),
                            -1.0, grow[u][rows, :, 0:CH], ALU.mult, ALU.mult))
                        ch(dve.tensor_tensor(b_d[u][rows, :, blk], chunks(bv[u][rows, :]),
                                             chunks(shrink[u][rows, :]), ALU.mult))
                        ch(dve.tensor_tensor(k_d[u][rows, :, blk], chunks(kp[u][rows, :]),
                                             chunks(shrink[u][rows, :]), ALU.mult))
                    ch.wait()
                    dve.sem_inc(operands, 1)
                for u in range(2):
                    b = read(("bonus", u))
                    dve.tensor_tensor(bonus[u][:, :], b[:, :], rkv[u][:, 2, :], ALU.mult)\
                       .then_inc(r_dve, 1)
                for u in range(2):
                    for x, to in (("b", rb), ("k", rk)):
                        for c in range(0, NC, 2):
                            b = read(("pairs", x, u, c))
                            dve.tensor_tensor(
                                to[u][:, c:c + 2, :], b[:, 0:384].rearrange("p (c s) -> p c s", c=2),
                                tri[:, :].unsqueeze(1).broadcast_to((P, 2, 3 * CH)), ALU.mult)\
                               .then_inc(r_dve, 1)
                quad = lambda b: b[:, :].rearrange("p (c s) -> p c s", c=4)
                eye = ident[:, :].unsqueeze(1).broadcast_to((P, 4, P))
                for n in range(LEVELS):
                    for u in range(2):
                        for c in range(0, NC, 4):
                            b = read(("at", n, u, c))
                            dve.tensor_tensor(
                                at_inv[u][:, c:c + 4, :], quad(b),
                                corner[:, n, :].unsqueeze(1).broadcast_to((P, 4, P)), ALU.mult)\
                               .then_inc(r_dve, 1)
                    for u in range(2):
                        for c in range(0, NC, 4):
                            if n < LEVELS - 1:
                                b = read(("inv", n, u, c))
                                t = inv[u][:, c:c + 4, :]
                                dve.tensor_tensor(t, quad(b), eye if n == 0 else t, ALU.add)\
                                   .then_inc(r_dve, 1)
                            b = read(("invT", n, u, c))
                            t = inv_t[u][:, c:c + 4, :]
                            dve.tensor_tensor(t, quad(b), eye if n == 0 else t, ALU.add)\
                               .then_inc(r_dve, 1)
                for c in range(NC):
                    for u in range(2):
                        b = read(("s", c, u))
                        dve.tensor_scalar(state[u][:, (c + 1) % 2, :], b[:, 0:P],
                                          grow[u][:, c, CH:], None, ALU.mult).then_inc(r_dve, 1)
                for u in range(2):
                    dve.wait_ge(y_out, k * 2 + (u + 1))
                    dve.tensor_copy(cum[u][:, :], ps[6 + u][:, :]).then_inc(y_copied, 1)
                for u in range(2):
                    b = read(("mean", u))
                    ch(dve.scalar_tensor_tensor(cum[u][:, :], b[:, :], -1.0 / HN, cum[u][:, :],
                                                ALU.mult, ALU.add))
                    ch.wait()
                    dve.sem_inc(r_dve, 1)
                    dve.sem_inc(y_centred, 1)
                for u in range(2):
                    y = cum[u][:, :]
                    dve.wait_ge(r_act, k * rj.total("act") + rj.copies(("var", u)))
                    ch(dve.reciprocal(root[u][:, :], root[u][:, :]))
                    ch.wait()
                    ch(dve.tensor_tensor(y, y, root[u][:, :], ALU.mult))
                    ch.wait()
                    ch(dve.tensor_scalar(y, y, rcol("lnxg", k, u, 2), rcol("lnxb", k, u, 2),
                                         ALU.mult, ALU.add))
                    ch.wait()
                    ch(dve.tensor_tensor(y, y, bonus[u][:, :], ALU.add))
                    ch.wait()
                    dve.tensor_tensor(y, y, sg[u][:, :], ALU.mult).then_inc(y_ready, 1)
                over(dve, k + 3)

            with dve.Fori(0, FT // 2) as k:
                ch.enter(k, 40)
                rwkv_turn(k)
                ch.leave(FT // 2)

            def do(ins):
                ch(ins)
                ch.wait()

            def tt(o, a, b, op):
                do(dve.tensor_tensor(o, a, b, op))

            def ts(o, a, s1, op0, s2=None, op1=ALU.bypass):
                do(dve.tensor_scalar(o, a, s1, s2, op0, op1))

            def fraction(x, tmp):
                ts(tmp, x, MAGIC, ALU.add)
                ts(tmp, tmp, -MAGIC, ALU.add)
                tt(x, x, tmp, ALU.subtract)

            def to_turns(x, tmp):
                ts(tmp, x, 1.0 / TURN, ALU.mult, MAGIC, ALU.add)
                ts(tmp, tmp, -MAGIC, ALU.add)
                do(dve.scalar_tensor_tensor(x, tmp, -TURN_A, x, ALU.mult, ALU.add))
                do(dve.scalar_tensor_tensor(x, tmp, -TURN_B, x, ALU.mult, ALU.add))
                ts(x, x, 1.0 / TURN, ALU.mult, 0.5, ALU.min)
                ts(x, x, -0.5, ALU.max)

            e = [x[:, :] for x in e1]
            lam_re, lam_im = lam[:, 0, :], lam[:, 1, :]
            over_g = lambda ap: ap.unsqueeze(1).broadcast_to((P, NP, G))
            powers = expo[:, :].unsqueeze(2).broadcast_to((P, NP, G))
            dve.wait_ge(s5_in, 16 * 7)
            for n in range(2):
                do(dve.memset(kpad[n][:, :, :], 0.0))
            do(dve.memset(xst[:, :, 0:1], 0.0))
            dve.wait_ge(s5_mag, 1)
            tt(e[1], lam_re, e[0], ALU.mult)
            tt(e[2], lam_im, e[0], ALU.mult)
            to_turns(e[2], e[6])
            tt(pw_re[:, :, :], over_g(e[1]), powers, ALU.mult)
            tt(pw_im[:, :, :], over_g(e[2]), powers, ALU.mult)
            fraction(pw_im[:, :, :], pt2[:, :, :])
            ts(mag8[:, :], e[1], float(T8), ALU.mult)
            ts(turn8[:, :], e[2], float(T8), ALU.mult)
            fraction(turn8[:, :], e[6])
            dve.sem_inc(s5_angle, 1)
            dve.wait_ge(s5_mag, 4)
            dve.wait_ge(s5_sine, 4)
            tt(pt2[:, :, :], pt2[:, :, :], pt2[:, :, :], ALU.mult)
            ts(pt2[:, :, :], pt2[:, :, :], -2.0, ALU.mult, 1.0, ALU.add)
            tt(pw_re[:, :, :], pt2[:, :, :], pt1[:, :, :], ALU.mult)
            do(dve.scalar_tensor_tensor(pw_im[:, :, :], pw_im[:, :, :], sign[:, 1:2], pt1[:, :, :],
                                        ALU.mult, ALU.mult))
            tt(e[5], e[5], e[5], ALU.mult)
            do(dve.scalar_tensor_tensor(e[5], e[5], -2.0, e[3], ALU.mult, ALU.mult))
            do(dve.scalar_tensor_tensor(e[5], e[3], -1.0, e[5], ALU.add, ALU.add))
            tt(e[4], e[4], e[3], ALU.mult)
            tt(e[6], lam_re, lam_re, ALU.mult)
            tt(e[7], lam_im, lam_im, ALU.mult)
            tt(e[6], e[6], e[7], ALU.add)
            do(dve.reciprocal(e[6], e[6]))
            tt(e[7], e[5], lam_re, ALU.mult)
            tt(e[8], e[4], lam_im, ALU.mult)
            tt(e[7], e[7], e[8], ALU.add)
            tt(e[7], e[7], e[6], ALU.mult)
            tt(e[8], e[4], lam_re, ALU.mult)
            tt(e[9], e[5], lam_im, ALU.mult)
            tt(e[8], e[8], e[9], ALU.subtract)
            tt(e[8], e[8], e[6], ALU.mult)
            ts(e[9], e[8], sign[:, 0:1], ALU.mult)
            ts(e[10], e[8], sign[:, 1:2], ALU.mult)
            for n in (2, 3):
                ts(bc[:, n, :, :], bc[:, n, :, :], sign[:, 0:1], ALU.mult)

            def read5(turn, key):
                dve.wait_ge(s_job, s5_count(turn, key))
                return ps[S5_JOBS[key]]

            batch = lambda ap, k, n: ap.rearrange("p (a b g) -> p a b g", b=2, g=GB)[:, k, n]
            batch3 = lambda ap, k, n: ap.rearrange("p (a b g) q -> p a b g q", b=2, g=GB)[:, k, n]
            over_c = lambda ap: ap.unsqueeze(2).broadcast_to((P, GB, C8))
            over_q = lambda ap: ap.unsqueeze(2).broadcast_to((P, GB, GP))

            def tables(turn, k, n):
                if turn is not None:
                    dve.wait_ge(s5_sine, k * 2 + (n + 4))
                tt(turn5[:, :, :], over_c(batch(turn8[:, :], k, n)),
                   count[:, :].unsqueeze(1).broadcast_to((P, GB, C8)), ALU.mult)
                fraction(turn5[:, :, :], turn5_tmp[:, :, :])
                dve.sem_inc(s5_angle, 1)
                for m in range(2):
                    ch(dve.tensor_tensor(bb[m][:, :, :], batch3(bc[:, m], k, n),
                                         over_q(batch(e[7], k, n)), ALU.mult))
                    tt(t5f[:, :, :], batch3(bc[:, 1 - m], k, n), over_q(batch(e[10 - m], k, n)), ALU.mult)
                    tt(bb[m][:, :, :], bb[m][:, :, :], t5f[:, :, :], ALU.add)

                def outer(o, first, powers_n, one, two):
                    m = powers_n
                    shape = (P, GB, m, GP)
                    pr, pi = (ap[:, first:first + m, :].rearrange("p j (a b g) -> p a b g j", b=2, g=GB)
                              [:, k, n].unsqueeze(3).broadcast_to(shape)
                              for ap in (pw_re, pw_im))
                    one, two = (ap.unsqueeze(2).broadcast_to(shape) for ap in (one, two))
                    ch(dve.tensor_tensor(o, pr, one, ALU.mult))
                    ch(dve.tensor_tensor(wvt2[:, :, 0:m, :], pi, two, ALU.mult))
                    ch.wait()
                    return dve.tensor_tensor(o, o, wvt2[:, :, 0:m, :], ALU.add)

                outer(wvt[:, :, :, :], 0, T8, bb[0][:, :, :], bb[1][:, :, :]).then_inc(w_ready, 1)
                dve.wait_ge(w_ready, k * 4 + (2 * n + 1))
                if turn:
                    dve.wait_ge(s_job, s5_count(turn, "y1"))
                outer(wc[n][:, :, :].rearrange("p g (j q) -> p g j q", q=GP), T8, T8 + 1,
                      batch3(bc[:, 2], k, n), batch3(bc[:, 3], k, n)).then_inc(w_ready, 1)

            def response(turn, k, n):
                ch(dve.tensor_tensor(t5f[0:GP, :, :],
                                     ident[0:GP, 0:GP].unsqueeze(1).broadcast_to((GP, GB, GP)),
                                     batch3(d_row, k, n), ALU.mult))
                for m in range(2):
                    p = read5(turn, f"k{m}")
                    ch(dve.tensor_copy(kpad[n][:, 4 * m:4 * m + 4, P:],
                                       p[0:GP, :].rearrange("p (g s) -> p g s", g=4)))
                ch.wait()
                do(dve.tensor_tensor(kpad[n][:, :, P:P + GP], kpad[n][:, :, P:P + GP],
                                     t5f[0:GP, :, :], ALU.add))
                dve.sem_inc(kpad_ready, 1)
                dve.wait_ge(s5_sine, k * 2 + (n + 5))
                ch(dve.tensor_copy(decay8[n][:, :, :], over_c(batch(mag8[:, :], k, n))))
                tt(cosc[n][:, :, :], cosc[n][:, :, :], cosc[n][:, :, :], ALU.mult)
                ch(dve.memset(decay8[n][:, :, 0:1], 0.0))
                ch(dve.tensor_scalar(sinc[n][:, :, :], sinc[n][:, :, :], sign[:, 0:1], None, ALU.mult))
                ts(cosc[n][:, :, :], cosc[n][:, :, :], -2.0, ALU.mult, 1.0, ALU.add)

            def state5(turn, k, n):
                flat = lambda ap: ap.rearrange("p g c -> p (g c)")
                dve.wait_ge(s_act, s5_count(turn, "v", S5_COPIES))
                ch(dve.tensor_tensor(t5b[:, :, :], vin[:, :, :], cosc[n][:, :, :], ALU.mult))
                p = read5(turn, "vs")
                ch(dve.tensor_tensor(flat(t5a[:, :, :]), p[:, :], flat(sinc[n][:, :, :]), ALU.mult))
                ch.wait()
                tt(t5a[:, :, :], t5a[:, :, :], t5b[:, :, :], ALU.add)
                do(dve.tensor_tensor_scan(flat(zst[:, :, :]), flat(decay8[n][:, :, :]),
                                          flat(t5a[:, :, :]), 0.0, ALU.mult, ALU.add))
                dve.sem_inc(x_ready, 1)
                ch(dve.tensor_tensor(t5b[:, :, :], zst[:, :, :], cosc[n][:, :, :], ALU.mult))
                p = read5(turn, "zs")
                ch(dve.tensor_tensor(t5a[:, :, :], p[:, :].rearrange("p (g c) -> p g c", g=GB),
                                     sinc[n][:, :, :], ALU.mult))
                ch.wait()
                do(dve.tensor_tensor(xst[:, :, 1:], t5b[:, :, 0:C8 - 1], t5a[:, :, 0:C8 - 1],
                                     ALU.subtract))
                dve.sem_inc(x_ready, 1)

            def dve_turn(turn, b, f, g):
                if not isinstance(turn, int) and turn[1] == 0:
                    ch.enter(turn[0], 2 * 30, 1)
                state5(turn, *b)
                if f:
                    response(turn, *f)
                if g:
                    tables(turn, *g)
                if not isinstance(turn, int) and turn[1] == 1:
                    ch.leave(FT // 2 - 2)

            tables(None, 0, 0)
            response(0, 0, 0)
            tables(0, 0, 1)
            s5_turns(dve, dve_turn)
            over(dve, 7)

            def split_tiles(first, n, tile, done):
                for i in range(n):
                    ch(dve.tensor_copy(zh[:, first + i, :], tile(i)))
                    ch.wait()
                    dve.tensor_tensor(zl[:, first + i, :], tile(i), zh[:, first + i, :].bitcast(F32),
                                      ALU.subtract).then_inc(done, 1)

            dve.wait_ge(gy_in, 16)
            split_tiles(FT, FT, lambda i: gy[:, i, :], gy_split)
            dve.wait_ge(mix_in, 16)
            split_tiles(0, FT, lambda i: mix_tiles[:, i, :], mix_split)
            for n in range(4):
                u = n % 2
                dve.wait_ge(glu_out, n + 1)
                dve.wait_ge(sgt_in[u], 16 * (n // 2 + 1))
                tt(gsig[u][:, :, :], gsig[u][:, :, :], gy[:, 2 * n:2 * n + 2, :], ALU.mult)
                dve.tensor_tensor(mix_tiles[:, FT + 2 * n:FT + 2 * n + 2, :], gsig[u][:, :, :],
                                  sgt[u][:, :, :], ALU.mult).then_inc(glu_mixed, 1)
            dve.wait_ge(glu_mixed, 4)
            dve.wait_ge(piece_used, P_GLU + 4)
            split_tiles(FT, FT, lambda i: mix_tiles[:, FT + i, :], mix_split)

            def add_residual(layer):
                dve.wait_ge(root_done, 2 * layer + 2)
                ch(dve.reciprocal(small[:, 8:12], small[:, 4:8]))
                ch.wait()
                for t in range(TT):
                    do(dve.scalar_tensor_tensor(y6[:, t, :], y6[:, t, :], small[:, 8 + t:9 + t],
                                                gp[layer][:, :], ALU.mult, ALU.mult))
                dve.wait_ge(h_in, 16 * (layer + 1))
                for t in range(TT):
                    ch(dve.tensor_tensor(x6[:, t, :], x6[:, t, :], y6[:, t, :], ALU.add))
                ch.wait()
                dve.sem_inc(h_ready, 1)

            add_residual(0)
            over(dve, 8)

            dve.wait_ge(h_stored, 16)
            norm_x(1, x6)
            split_z(1, ztmp6)
            over(dve, 9)

            dve.wait_ge(rope_in, 64)
            do(dve.tensor_copy(r1[:, :], pos[:, :]))
            ts(r1[:, :], r1[:, :], rope_c[:, 0:1], ALU.mult)
            to_turns(r1[:, :], r2[:, :])
            dve.sem_inc(angle, 1)
            dve.wait_ge(rope_sine, 2)
            tt(r2[:, :], r2[:, :], r2[:, :], ALU.mult)
            ts(rot[0:64, :], r2[0:64, :], -2.0, ALU.mult, 1.0, ALU.add)
            ts(rot[64:, :], r1[64:, :], rope_c[64:, 1:2], ALU.mult)
            dve.wait_ge(piece_used, P_IN1 + 1)
            dve.tensor_tensor(ktmp[:, :], ps[7][:, :], rot[:, :], ALU.mult).then_inc(key_rotated, 1)
            dve.wait_ge(key_folded, 1)
            do(dve.tensor_copy(key_pe[:, :], ps[6][:, :]))
            over(dve, 10)

            dve.wait_ge(c_root, 2)
            for r in (ktmp, rms_kv):
                do(dve.reciprocal(r[:, :], r[:, :]))
            for i in range(8):
                c, r = cq[:, i, :], (ktmp, rms_kv)[i // 4][:, :]
                do(dve.scalar_tensor_tensor(c, c, col(("qn", "kvn")[i // 4], i % 4), r,
                                            ALU.mult, ALU.mult))
                do(dve.tensor_copy(zh[:, i, :], c))
                dve.tensor_tensor(zl[:, i, :], c, zh[:, i, :].bitcast(F32),
                                  ALU.subtract).then_inc(c_split, 1)
            dve.wait_ge(c_split, 8)
            dve.sem_inc(a_dve, aj.total("dve"))
            dve.sem_inc(o_read, 2)

            def attention_turn(k):
                def job(key):
                    dve.wait_ge(a_job, k * len(aj.jobs) + aj.number(key))
                    return ps[aj.bank(key)]

                for a in range(2):
                    p = job(("qp", a))
                    dve.tensor_tensor(qp[a][:, :], p[:, :], rot[:, :], ALU.mult).then_inc(a_dve, 1)
                for i in range(10):
                    if i < 8:
                        a, b = divmod(i, TT)
                        p = job(("s", a, b))
                        do(dve.tensor_reduce(stat[:, 0, i:i + 1], p[:, 0:(b + 1) * P], AX.X, ALU.max))
                        do(dve.tensor_scalar(stat[:, 0, i:i + 1], stat[:, 0, i:i + 1], -SCALE, None,
                                             ALU.mult))
                        dve.sem_inc(max_ready, 1)
                    if i >= 2:
                        n = i - 2
                        a, b = divmod(n, TT)
                        dve.wait_ge(a_act, k * aj.total("act") + (aj.total("act") + aj.copies(("s", a, b))))
                        do(dve.reciprocal(stat[:, 2, n:n + 1], stat[:, 1, n:n + 1]))
                        pr = probs[a][:, b, 0:(b + 1) * P]
                        dve.tensor_scalar(pr, pr, stat[:, 2, n:n + 1], None, ALU.mult)\
                           .then_inc(probs_ready, 1)
                for i in range(8):
                    a, b = divmod(i, TT)
                    p = job(("pt", a, b))
                    w = (b + 1) * P
                    dve.tensor_copy(pt9[i % 2][:, 0:w], p[:, 0:w]).then_inc(a_dve, 1)
                    if i in (5, 7):
                        a = (i - 5) // 2
                        dve.wait_ge(o_ready, k * 2 + (a + 1))
                        o = sg1[:, :, :].rearrange("p (h a) t -> p h a t", a=2)[:, k, a]
                        dve.tensor_tensor(o, o, ps[6 + a][:, :], ALU.mult).then_inc(o_read, 1)

            with dve.Fori(0, H // 2) as k:
                ch.enter(k, 24)
                attention_turn(k)
                ch.leave(H // 2)
            dve.wait_ge(o_read, H + 2)
            over(dve, 11)

            split_tiles(0, KT, lambda i: sg1[:, i, :], mix_split)
            add_residual(1)
            over(dve, 12)


def arrange(i):
    f = lambda n: np.ascontiguousarray(i[n])

    def groups(w, rows, width):
        n = w.shape[1] // width
        w = w.reshape(rows // P, P, n, width).transpose(2, 1, 0, 3)
        return w.reshape(-1, P, rows // P * width)

    def halves(g):
        n = g.shape[0]
        return g.reshape(n, P, 2, PIECE).transpose(0, 2, 1, 3).reshape(2 * n, P, PIECE)

    w0 = f("ev_w_in")[0]
    a_in = 4 * W + 128
    pieces = [groups(w0[:, 4 * W:a_in], D, P),
              halves(groups(np.concatenate([w0[:, :4 * W], w0[:, a_in:]], 1), D, 256)),
              groups(f("ev_glu_w")[0], W, 256),
              halves(groups(f("ev_w_out")[0], D, 256))]
    w1 = f("od_w_in")[0]
    pe = w1[:, 1024:1088]
    pe_both = np.concatenate([pe, pe[:, 32:], pe[:, :32]], 1)
    pieces += [groups(pe_both, D, P),
               halves(groups(np.concatenate([w1[:, :1024], w1[:, 1088:]], 1), D, 256))]
    q = f("od_w_q_up")[0].reshape(512, 16, 192)
    q = np.concatenate([q, q[:, :, 160:192], q[:, :, 128:160]], 2)
    kv = f("od_w_kv_up")[0].reshape(512, 16, 256)
    for hp in range(8):
        pieces.append(groups(q[:, 2 * hp:2 * hp + 2].reshape(512, 512), 512, 512))
        k2 = kv[:, 2 * hp:2 * hp + 2, :128].reshape(512, 256)
        v2 = kv[:, 2 * hp:2 * hp + 2, 128:].reshape(512, 256)
        pieces.append(groups(np.concatenate([k2, v2], 1), 512, 512))
    pieces.append(halves(groups(f("od_w_out")[0], D, 256)))
    ws = np.concatenate(pieces, 0)
    assert ws.shape == (N_PIECES, P, PIECE), ws.shape
    ada = np.stack([f("ev_ada_w")[0], f("od_ada_w")[0]]).reshape(2, KT, P, 3, D)
    vec = {"c": f("c")[0], "mu": f("ev_mu")[0], "pre0": f("ev_norm_pre")[0],
           "ab0": f("ev_ada_b")[0, :2 * D], "w0": f("ev_w0")[0], "a0": f("ev_a0")[0],
           "kk": f("ev_k_k")[0], "ka": f("ev_k_a")[0], "rk": f("ev_r_k")[0],
           "lnxg": f("ev_lnx_g")[0], "lnxb": f("ev_lnx_b")[0], "glub": f("ev_glu_b")[0],
           "pre1": f("od_norm_pre")[0], "ab1": f("od_ada_b")[0, :2 * D],
           "qn": f("od_q_norm")[0], "kvn": f("od_kv_norm")[0]}
    cols = np.concatenate([vec[n].reshape(k, P).T for n, k in VECTORS], 1)
    return {
        **lora_and_masks(f), **s5_layout(f),
        "ws": ws.reshape(N_PIECES // 2, 2, P, PIECE), "ada": np.ascontiguousarray(ada.transpose(0, 1, 3, 2, 4)),
        "cols": np.ascontiguousarray(cols), "ident": np.eye(P, dtype=np.float32),
        "rows": np.stack([f("ev_ada_b")[0, 2 * D:], f("ev_norm_post")[0],
                          f("od_ada_b")[0, 2 * D:], f("od_norm_post")[0]]),
        "x": f("x")[0], **rotary_layout(), "pos": f("positions")[0],
    }


def rotary_layout():
    i = np.arange(P)
    freq = np.float32(1) / np.float32(10000) ** ((2 * (i % 32)).astype(np.float32) / np.float32(64))
    sign = np.where(i < 64, 0, np.where(i < 96, -1, 1))
    return {"rope_c": np.stack([freq, sign], 1).astype(np.float32),
            "fold": (i[:, None] % 64 == i[None] % 64).astype(np.float32),
            "neg_tri": np.where(i[None] > i[:, None], -1e30, 0).astype(np.float32)}


def lora_and_masks(f):
    w2, a2 = (f(n)[0].reshape(64, FT // 2, 2, P).transpose(1, 2, 0, 3) for n in ("ev_w2", "ev_a2"))
    zero = np.zeros_like(w2)
    lora = np.stack([np.concatenate([w2, zero], 2), np.concatenate([zero, a2], 2)], 3)
    i = np.arange(P)
    head, t = i // CH, i % CH
    tri = np.concatenate([t[:, None] <= np.arange(CH)[None],
                          (head[:, None] == head[None]) & (t[:, None] < t[None])], 1)
    corner = np.stack([(i[:, None] // (2 * m) == i[None] // (2 * m)) & (i[:, None] // m % 2 == 1)
                       & (i[None] // m % 2 == 0) for m in (2 ** n for n in range(LEVELS))], 1)
    return {"lora": lora, "tri": tri.astype(np.float32), "corner": corner.astype(np.float32),
            "blk1": (head[:, None] == head[None]).astype(np.float32),
            "starts": np.tile((np.arange(L) % CH != 0).astype(np.float32), (P, 1))}


def s5_layout(f):
    half = np.repeat(np.array([1, -1], np.float32), NS)
    both = lambda a: np.concatenate([a, a], 0)
    step = np.broadcast_to(f("ev_log_dt")[0], (P, G))
    lam = np.stack([both(f("ev_lam_re")[0].T), both(f("ev_lam_im")[0].T), step], 1)
    br, bi = (f(n)[0].transpose(1, 0, 2) for n in ("ev_b_re", "ev_b_im"))
    cr, ci = (f(n)[0].transpose(2, 0, 1) for n in ("ev_c_re", "ev_c_im"))
    bc = np.stack([np.concatenate(x, 0) for x in ((br, bi), (bi, br), (cr, ci), (ci, cr))], 1)
    swap = np.eye(P, dtype=np.float32)[(np.arange(P) + NS) % P]
    expo = np.array([*range(T8 - 1, -1, -1), *range(T8 + 1)], np.float32)
    return {"lam": np.ascontiguousarray(lam), "bc": np.ascontiguousarray(bc), "swap": swap,
            "sign": np.stack([half, -half], 1), "expo": np.tile(expo, (P, 1)),
            "count": np.tile(np.arange(C8, dtype=np.float32), (P, 1)), "d": f("ev_d")[0]}


def kernel(**inputs):
    import concourse.bacc as bacc
    from concourse.bass_utils import run_bass_kernel_spmd

    nc = bacc.Bacc("TRN2", target_bir_lowering=False, num_devices=1)
    arrays, aps = {}, {}
    for name, a in arrange({n: np.asarray(a) for n, a in inputs.items()}).items():
        a = np.ascontiguousarray(a)
        arrays[f"in_{name}_dram"] = a
        aps[name] = nc.dram_tensor(f"in_{name}_dram", a.shape, mybir.dt.from_np(a.dtype),
                                   kind="ExternalInput").ap()
    out = nc.dram_tensor("out_0_dram", (1, L, D), F32, kind="ExternalOutput").ap()
    trunk(nc, aps, out)
    result = run_bass_kernel_spmd(nc, [arrays], core_ids=[0])
    return result.results[0]["out_0_dram"]
```

```python
import concourse.bass as bass
from concourse import mybir
from contextlib import ExitStack
import numpy as np

F32 = mybir.dt.float32
F32R = mybir.dt.float32r
ALU = mybir.AluOpType
ACT = mybir.ActivationFunctionType
AX = mybir.AxisListType

P = 128
D = 2048
L = 512
KT = D // P
TT = L // P
W = D // 2
FT = W // P
HN = 64
CH = 64
NC = L // CH
LEVELS = 6
DECAY = float(np.exp(-0.5))
G, GP, NS = 64, 16, 64
T8 = P // GP
C8 = L // T8
GB = P // GP
NP = 2 * T8 + 1
MAGIC = 12582912.0
TURN = 6.283185307179586
TURN_A = 6.28125
TURN_B = TURN - TURN_A
SAFE_TURN = 6.283185
EPS = 1e-6
LNX_EPS = 64e-5
H = 16
SCALE = 192 ** -0.5
PIECE = 2048
A_SLOTS = 8

P_IN0 = 0
P_GLU = P_IN0 + 1 + 24 * 2
P_OUT0 = P_GLU + 4
P_IN1 = P_OUT0 + 16
P_UP = P_IN1 + 1 + 12 * 2
P_OUT1 = P_UP + 16
N_PIECES = P_OUT1 + 16

VECTORS = (("c", 16), ("mu", 33), ("pre0", 16), ("ab0", 32), ("w0", 8), ("a0", 8),
           ("kk", 8), ("ka", 8), ("rk", 8), ("lnxg", 8), ("lnxb", 8), ("glub", 8),
           ("pre1", 16), ("ab1", 32), ("qn", 4), ("kvn", 4))
COLS, NCOLS = {}, 0
for _name, _n in VECTORS:
    COLS[_name] = (NCOLS, _n)
    NCOLS += _n


class Chain:

    def __init__(self, eng, sem):
        self.eng, self.sem, self.base, self.n = eng, sem, 0, 0

    def __call__(self, ins):
        ins.then_inc(self.sem, 1)
        self.n += 1

    def at(self):
        return self.base + self.n

    def wait(self):
        self.eng.wait_ge(self.sem, self.base + self.n)

    def enter(self, i, per, first=0):
        self.saved, self.per = self.base + self.n, per
        self.base, self.n = i * per + (self.saved - first * per), 0

    def leave(self, turns):
        assert self.n == self.per, (self.n, self.per)
        self.base, self.n = self.saved + turns * self.per, 0


class Banks:

    def __init__(self, banks):
        self.banks, self.jobs = banks, []

    def add(self, key, reader):
        self.jobs.append((key, reader))

    def number(self, key):
        return [k for k, _ in self.jobs].index(key) + 1

    def engine(self, key):
        return dict(self.jobs)[key]

    def copies(self, key):
        who = self.engine(key)
        return [k for k, r in self.jobs if r == who].index(key) + 1

    def total(self, who):
        return sum(r == who for _, r in self.jobs)

    def bank(self, key):
        return self.banks[(self.number(key) - 1) % len(self.banks)]

    def before(self, key):
        n = self.number(key) - 1 - len(self.banks)
        return self.jobs[n][0] if n >= 0 else None


def rwkv_jobs():
    jobs = Banks(range(6))
    for u in range(2):
        jobs.add(("decay", u), "act")
        jobs.add(("rate", u), "act")
    for u in range(2):
        jobs.add(("norm", u), "dve")
    for u in range(2):
        jobs.add(("bonus", u), "dve")
        for x in "bk":
            for c in range(0, NC, 2):
                jobs.add(("pairs", x, u, c), "dve")
        for x in "bkv":
            for c in range(0, NC, 4):
                jobs.add(("turn", x, u, c), "act")
    for n in range(LEVELS):
        for u in range(2):
            for c in range(0, NC, 4):
                jobs.add(("at", n, u, c), "dve")
        for u in range(2 if n else 0):
            for c in range(0, NC, 4):
                if n < LEVELS - 1:
                    jobs.add(("inv", n, u, c), "dve")
                jobs.add(("invT", n, u, c), "dve")
    for c in range(NC):
        for x, who in (("w", "act"), ("u", "act"), ("s", "dve")):
            for u in range(2):
                jobs.add((x, c, u), who)
    for x in ("mean", "var"):
        for u in range(2):
            jobs.add((x, u), "dve" if x == "mean" else "act")
    return jobs


S5_JOBS = {"v": 0, "vs": 1, "uc": 2, "wv0": 3, "wv1": 4, "zs": 5, "k0": 6, "k1": 7,
           "y0": 0, "y1": 1, "yt": 2}
S5_FRONT = ("uc", "wv0", "wv1", "k0", "k1")
S5_COPIES = ("v", "uc", "wv0", "wv1", "y0", "y1", "yt")


def s5_count(turn, key, among=tuple(S5_JOBS)):
    front = [x for x in among if x in S5_FRONT]
    if not isinstance(turn, int):
        k, odd = turn
        return k * (2 * len(among)) + ((odd - 1) * len(among) + len(front) + among.index(key) + 1)
    if turn == 0:
        return front.index(key) + 1
    here = [x for x in among if x not in S5_FRONT] if turn == FT else among
    return (turn - 1) * len(among) + len(front) + here.index(key) + 1


def s5_turns(engine, turn):
    def static(t):
        turn(t, *[divmod(x, 2) if x < FT else None for x in (t - 1, t, t + 1)])

    static(1)
    with engine.Fori(1, FT // 2 - 1) as k:
        turn((k, 0), (k - 1, 1), (k, 0), (k, 1))
        turn((k, 1), (k, 0), (k, 1), (k + 1, 0))
    for t in range(FT - 2, FT + 1):
        static(t)


def attention_jobs():
    jobs = Banks(range(6))
    for a in range(2):
        jobs.add(("qn", a), "act")
        jobs.add(("qp", a), "dve")
        jobs.add(("key", a), "act")
    for a in range(2):
        for b in range(TT):
            jobs.add(("s", a, b), "act")
    for n in range(2):
        jobs.add(("v", n), "act")
    for a in range(2):
        for b in range(TT):
            jobs.add(("pt", a, b), "dve")
    assert len(jobs.jobs) % 6 == 0
    return jobs


def trunk(nc, A, out):
    ctx = ExitStack()
    with ctx:
        slab_bytes = (nc.sbuf_usable_end - nc.sbuf_base - 1024) // 32 * 32
        slab = nc.alloc_sbuf_tensor("slab", [P, slab_bytes // 4], F32)
        start = nc.sbuf_base - slab_bytes
        top = [start]

        def sb(name, shape, dt=F32):
            size = 4
            for n in shape[1:]:
                size *= n
            here = top[0]
            top[0] += (size + 31) // 32 * 32
            assert top[0] <= start + slab_bytes, (name, top[0] - start - slab_bytes)
            return nc.alloc_sbuf_tensor_at(name, shape, dt, offset=here)

        def sem(name):
            return ctx.enter_context(nc.semaphore(name))

        def dram(name, shape):
            return nc.dram_tensor(name, shape, F32).ap()

        mixed_d = dram("mixed_d", [16, 2, P, L])
        sgate_d = dram("sgate_d", [4, 2, P, L])
        mix_d = dram("mix_d", [4, 2, P, L])
        gy_d = dram("gy_d", [FT, P, L])
        h1_d = dram("h1_d", [L, D])
        u_d = dram("u_d", [L, W])

        raw = [sb(f"raw{s}", [P, PIECE]) for s in range(2)]
        whi = [sb(f"whi{s}", [P, PIECE], F32R) for s in range(2)]
        wlo = [sb(f"wlo{s}", [P, PIECE], F32R) for s in range(2)]
        cols = sb("cols", [P, NCOLS])
        ident = sb("ident", [P, P])
        ones = sb("ones", [P, P])
        csilu = sb("csilu", [P, 16])
        modc = [sb(f"modc{i}", [P, 32]) for i in range(2)]
        small = sb("small", [P, 12])
        sum_parts = sb("sum_parts", [P, TT, 8])
        gp = [sb("gp0", [P, D]), None]
        keep = top[0]

        xt = sb("xt", [P, TT, D])
        top1 = top[0]
        top[0] = keep
        gp[1] = sb("gp1", [P, D])
        lo_in = sb("lo_in", [P, L])
        shift = sb("shift", [P, 2, L + 1])
        res = [sb(f"res{s}", [P, 2, L]) for s in range(2)]
        ures = [sb(f"ures{s}", [P, TT, 256]) for s in range(2)]
        assert top[0] <= top1
        keep2 = keep + (D + L) * 4
        top[0] = top1
        post_b = sb("post_b", [P, D])
        acc = sb("acc", [P, 3, D])
        here = top[0]
        ztmp = sb("ztmp", [P, 2, L])
        top[0] = here
        diag1 = acc[:, 2, 0:TT * P].rearrange("p (t q) -> p t q", t=TT)
        ada2 = [sb(f"ada2_{s}", [P, D]) for s in range(2)]
        here = top[0]
        ada1 = [sb(f"ada1_{s}", [P, D]) for s in range(A_SLOTS)]
        top[0] = here
        zh = sb("zh", [P, KT, L], F32R)
        zl = sb("zl", [P, KT, L], F32R)

        top[0] = keep2
        blk1 = sb("blk1", [P, P])
        starts = sb("starts", [P, L])
        tri = sb("tri", [P, 3 * CH])
        corner = sb("corner", [P, LEVELS + 1, P])
        two = lambda name, shape: [sb(f"{name}{u}", shape) for u in range(2)]
        rkv = two("rkv", [P, 3, L])
        lora = two("lora", [P, 2, P])
        rwkv_gate = top[0]
        sg = two("sg", [P, L])
        rate = two("rate", [P, L])
        cum = two("cum", [P, L])
        grow = two("grow", [P, NC, CH + 1])
        bonus = two("bonus", [P, L])
        ra = two("ra", [P, NC, 3 * CH])
        wu = two("wu", [P, 2, P])
        state = two("state", [P, 2, P])
        kept = two("kept", [P, P])
        b_t, k_t, v_t = two("b_t", [P, NC, P]), two("k_t", [P, NC, P]), two("v_t", [P, NC, P])
        here = top[0]
        shrink, kn, sq, root, kp, bv = zip(*[[sb(f"{n}{u}", [P, L]) for n in (
            "shrink", "kn", "sq", "root", "kp", "bv")] for u in range(2)])
        top[0] = here
        rb, rk = zip(*[[sb(f"{n}{u}", [P, NC, 3 * CH]) for n in ("rb", "rk_")] for u in range(2)])
        b_d, k_d, v_d = two("b_d", [P, NC, P]), two("k_d", [P, NC, P]), two("v_d", [P, NC, P])
        inv, at_inv, inv_t = b_d, k_d, v_d
        rj = rwkv_jobs()
        y_t = [k_t[u][:, 0:4, :].rearrange("p c s -> p (c s)") for u in range(2)]

        top[0] = keep2
        top[0] = keep2 + P * 4
        swap = sb("swap", [P, P])
        sign = sb("sign", [P, 2])
        expo = sb("expo", [P, NP])
        count = sb("count", [P, C8])
        lam = sb("lam", [P, 3, G])
        assert top[0] <= keep2 + (P + L) * 4
        top[0] = keep2 + (P + L) * 4
        bc = sb("bc", [P, 4, G, GP])
        top[0] = rwkv_gate - 2 * P * 2 * 4
        d_row = sb("d_row", [GP, G, GP])
        zst = sb("zst", [P, GB, C8])
        assert top[0] == rwkv_gate + 2 * L * 4
        e1 = [sb(f"e1_{n}", [P, G]) for n in range(12)]
        pw_re, pw_im, pt1, pt2 = (sb(n, [P, NP, G]) for n in ("pw_re", "pw_im", "pt1", "pt2"))
        turn8, mag8 = sb("turn8", [P, G]), sb("mag8", [P, G])
        bb = [sb(f"bb{n}", [P, GB, GP]) for n in range(2)]
        t5f = sb("t5f", [P, GB, GP])
        turn5 = sb("turn5", [P, GB, C8])
        turn5_tmp = sb("turn5_tmp", [P, GB, C8])
        wvt = sb("wvt", [P, GB, T8, GP])
        wvt2 = sb("wvt2", [P, GB, T8 + 1, GP])
        ucm = sb("ucm", [C8, T8, P])
        ugm = sb("ugm", [C8, GB, P])
        cosc, sinc, decay8, uc = (two(n, [P, GB, C8]) for n in ("cosc", "sinc", "decay8", "uc"))
        wc = two("wc", [P, GB, (T8 + 1) * GP])
        wv, w3 = two("wv", [P, GB, P]), two("w3", [P, GB, P])
        kpad = [sb(f"kpad{n}", [GP, GB, 2 * P]) for n in range(2)]
        t5a, t5b = sb("t5a", [P, GB, C8]), sb("t5b", [P, GB, C8])
        vin, xst = sb("vin", [P, GB, C8]), sb("xst", [P, GB, C8])
        ycm = sb("ycm", [C8, T8, P])
        gy_out = sb("gy_out", [P, L])

        top[0] = keep2
        gy = sb("gy", [P, FT, L])
        gsig = [sb(f"gsig{s}", [P, 2, L]) for s in range(2)]
        sgt = [sb(f"sgt{s}", [P, 2, L]) for s in range(2)]
        assert top[0] <= keep2 + TT * D * 4

        top[0] = keep2
        x6 = sb("x6", [P, TT, D])
        y6 = sb("y6", [P, TT, D])
        ztmp6 = sb("ztmp6", [P, 2, L])
        diag6 = sb("diag6", [P, TT, P])
        assert top[0] <= keep + 80 * 1024

        top[0] = keep2
        sg1 = sb("sg1", [P, H, L])
        key_pe = sb("key_pe", [P, L])
        rot = sb("rot", [P, L])
        rope_c = sb("rope_c", [P, 2])
        fold = sb("fold", [P, P])
        here = top[0]
        cq = sb("cq", [P, 8, L])
        ktmp = sb("ktmp", [P, L])
        pos = sb("pos", [P, L], mybir.dt.int32)
        r1, r2, rms_kv = sb("r1", [P, L]), sb("r2", [P, L]), sb("rms_kv", [P, L])
        assert top[0] <= keep + 80 * 1024
        top[0] = here
        probs = [sb(f"probs{a}", [P, TT, L]) for a in range(2)]
        qn, qp, key9 = ([sb(f"{n}{a}", [P, L]) for a in range(2)] for n in ("qn", "qp", "key"))
        v9 = sb("v9", [P, TT, 2 * P])
        assert top[0] <= keep + 80 * 1024
        top[0] = keep + 144 * 1024
        pt9 = [sb(f"pt9{n}", [P, L]) for n in range(2)]
        neg_tri = sb("neg_tri", [P, P])
        stat = sum_parts
        aj = attention_jobs()

        mix_tiles = y6[:, :, :].rearrange("p a (b t) -> p (a b) t", t=L)

        ps = [ctx.enter_context(nc.psum_tensor(f"ps{i}", [P, 512], F32)) for i in range(8)]

        def col(name, i, n=1):
            o = COLS[name][0]
            return cols[:, o + i:o + i + n]

        def rcol(name, i, j=0, step=1, rows=slice(0, P)):
            o, n = COLS[name]
            return cols[rows, o:o + n // step * step].rearrange("p (a b) -> p a b", b=step)[:, i, j:j + 1]

        raw_full = [sem(f"raw_full{s}") for s in range(2)]
        hi_ready, lo_ready, piece_used = sem("hi_ready"), sem("lo_ready"), sem("piece_used")
        phase_over = sem("phase_over")
        dve_chain, act_chain = sem("dve_chain"), sem("act_chain")
        cols_in, ident_in, x_in, gb_in, gp1_in = (sem(n) for n in (
            "cols_in", "ident_in", "x_in", "gb_in", "gp1_in"))
        consts_set, csilu_set = sem("consts_set"), sem("csilu_set")
        ada1_full = [sem(f"ada1_full{s}") for s in range(A_SLOTS)]
        ada2_full = [sem(f"ada2_full{s}") for s in range(2)]
        ada1_used, ada2_used = sem("ada1_used"), sem("ada2_used")
        acc_ready, mod_sums, mod_ready = sem("acc_ready"), sem("mod_sums"), sem("mod_ready")
        x_normed, x_turned, z_scaled = sem("x_normed"), sem("x_turned"), sem("z_scaled")
        z_ready, root_done = sem("z_ready"), sem("root_done")
        proj_out = sem("proj_out")
        mixed = sem("mixed")
        res_stored = [sem(f"res_stored{s}") for s in range(2)]
        u_stored = [sem(f"u_stored{s}") for s in range(2)]

        mask_in = sem("mask_in")
        pair_in, sg_in = ([sem(f"{n}{u}") for u in range(2)] for n in ("pair_in", "sg_in"))
        r_job, r_dve, r_act = sem("r_job"), sem("r_dve"), sem("r_act")
        blocks_zero, keys_decayed, inv_begun = (sem(n) for n in (
            "blocks_zero", "keys_decayed", "inv_begun"))
        key_squared, cum_done, exp_done, norm_max = (sem(n) for n in (
            "key_squared", "cum_done", "exp_done", "norm_max"))
        norm_root, bonus_ready, bonus_in, operands, v_blocks, state_zero = (sem(n) for n in (
            "norm_root", "bonus_ready", "bonus_in", "operands", "v_blocks", "state_zero"))
        y_out, y_centred, y_squared = sem("y_out"), sem("y_centred"), sem("y_squared")
        y_ready, y_copied, y_normed, y_summed = (sem(n) for n in (
            "y_ready", "y_copied", "y_normed", "y_summed"))
        mix_stored = sem("mix_stored")

        s5_in, d_in, ucm_in, kpad_ready, u_grouped, zeros_set = (sem(n) for n in (
            "s5_in", "d_in", "ucm_in", "kpad_ready", "u_grouped", "zeros_set"))
        s_job, s_act = sem("s_job"), sem("s_act")
        s5_angle, s5_sine, s5_mag = sem("s5_angle"), sem("s5_sine"), sem("s5_mag")
        w_ready, x_ready, w3_in = sem("w_ready"), sem("x_ready"), [sem(f"w3_in{n}") for n in range(2)]
        gy_stored = sem("gy_stored")
        gy_in, sgt_in = ([sem(f"{n}{s}") for s in range(2)] for n in ("gy_in", "sgt_in"))
        gy_split, glu_out, glu_mixed = sem("gy_split"), sem("glu_out"), sem("glu_mixed")

        mix_in, mix_split, out_read, h_in, out_scaled, squares_summed = (sem(n) for n in (
            "mix_in", "mix_split", "out_read", "h_in", "out_scaled", "squares_summed"))
        h_ready, h_stored = sem("h_ready"), sem("h_stored")
        rope_in, angle, rope_sine = sem("rope_in"), sem("angle"), sem("rope_sine")
        in1_read, key_rotated, key_folded = (sem(n) for n in (
            "in1_read", "key_rotated", "key_folded"))
        c_squared, c_summed, c_root, c_hi, c_split = (sem(n) for n in (
            "c_squared", "c_summed", "c_root", "c_hi", "c_split"))
        a_job, a_act, a_dve = sem("a_job"), sem("a_act"), sem("a_dve")
        max_ready, probs_ready, o_ready, o_read = (sem(n) for n in (
            "max_ready", "probs_ready", "o_ready", "o_read"))

        block = ctx.enter_context(nc.Block())

        def load_piece(sp, k, n):
            s = n % 2
            if isinstance(k, int) and k == 0 and n < 2:
                pass
            else:
                sp.wait_ge(hi_ready, k * 2 + (n - 1))
                sp.wait_ge(lo_ready, k * 2 + (n - 1))
            sp.dma_start(raw[s][:, :], A["ws"][k + n // 2, s]).then_inc(raw_full[s], 16)

        def split_hi(act, k, n):
            s = n % 2
            act.wait_ge(raw_full[s], k * 16 + (n // 2 + 1) * 16)
            if not (isinstance(k, int) and k == 0 and n < 2):
                act.wait_ge(piece_used, k * 2 + (n - 1))
            act.activation(whi[s][:, :], raw[s][:, :], ACT.Copy).then_inc(hi_ready, 1)

        def split_lo(pool, k, n):
            s = n % 2
            pool.wait_ge(hi_ready, k * 2 + (n + 1))
            pool.tensor_tensor(wlo[s][:, :], raw[s][:, :], whi[s][:, :].bitcast(F32),
                               ALU.subtract).then_inc(lo_ready, 1)

        def piece_ready(pe, k, n):
            pe.wait_ge(hi_ready, k * 2 + (n + 1))
            pe.wait_ge(lo_ready, k * 2 + (n + 1))

        def over(eng, n):
            eng.drain().then_inc(phase_over, 1)
            eng.wait_ge(phase_over, 3 * n)

        def ada1_piece(k, n):
            return A["ada"][0].rearrange("(a b) t p f -> a b t p f", b=4)[k, n // 2, n % 2]

        def ada2_first(k, u):
            return (k * 8 + 4 * u) if isinstance(k, int) and k < 2 else k * 6 + (4 + 3 * u)

        def ada2_piece(k, u, q):
            if isinstance(k, int) and k < 2:
                return A["ada"][0, 8 * k + 4 * u + q, 2]
            return A["ada"].rearrange("l (a b) t p f -> (l a) b t p f", b=2)[k + (KT // 2 - 2), u, q]

        @block.sync
        def _(sp):
            sp.dma_start(cols[:, :], A["cols"]).then_inc(cols_in, 16)
            sp.dma_start(ident[:, :], A["ident"]).then_inc(ident_in, 16)
            for n in range(2):
                sp.dma_start(ada1[n][:, :], ada1_piece(0, n)).then_inc(ada1_full[n], 16)
            sp.dma_start(xt[:, :, :], A["x"].rearrange("(a p) d -> p a d", p=P)).then_inc(x_in, 16)
            for n in range(2, A_SLOTS):
                sp.dma_start(ada1[n][:, :], ada1_piece(0, n)).then_inc(ada1_full[n], 16)
            with sp.Fori(1, 2 * KT // A_SLOTS) as k:
                for n in range(A_SLOTS):
                    sp.wait_ge(ada1_used, k * A_SLOTS + (n + 1 - A_SLOTS))
                    sp.dma_start(ada1[n][:, :], ada1_piece(k, n)).then_inc(ada1_full[n], 16)
            load_piece(sp, 0, 0)
            load_piece(sp, 0, 1)
            sp.dma_start(gp[0][:, :], A["rows"][0].partition_broadcast(P)).then_inc(gb_in, 16)
            sp.dma_start(post_b[:, :], A["rows"][1].partition_broadcast(P)).then_inc(gb_in, 16)
            load_piece(sp, 0, 2)
            sp.wait_ge(phase_over, 3)
            sp.dma_start(gp[1][:, :], A["rows"][2].partition_broadcast(P)).then_inc(gp1_in, 16)

            def group_pieces(k, adas):
                for u in range(2):
                    load_piece(sp, k * 2, 2 * u + 3)
                    load_piece(sp, k * 2, 2 * u + 4)
                    for q in range(adas):
                        m = ada2_first(k, u)
                        s = (4 * u + q if adas == 4 else 3 * u + q) % 2
                        if not (isinstance(k, int) and k == 0 and u == 0 and q < 2):
                            sp.wait_ge(ada2_used, m + (q - 1))
                        sp.dma_start(ada2[s][:, :], ada2_piece(k, u, q)).then_inc(ada2_full[s], 16)

            for k in range(2):
                group_pieces(k, 4)
            with sp.Fori(2, 10) as k:
                group_pieces(k, 3)
            sp.wait_ge(mod_ready, 2)
            sp.dma_start(post_b[:, :], A["rows"][3].partition_broadcast(P)).then_inc(gb_in, 16)
            group_pieces(10, 0)
            group_pieces(11, 0)
            sp.wait_ge(phase_over, 6)
            for s in range(2):
                sp.wait_ge(res_stored[s], 16 * 10)
                sp.wait_ge(u_stored[s], 32)
            of_pair = mixed_d.rearrange("(a b) u p t -> b u p a t", a=4)

            def load_pair(k, u):
                sp.dma_start(rkv[u][:, :, :], of_pair[k, u, :, 0:3]).then_inc(pair_in[u], 16)

            def load_lora(k, u):
                sp.dma_start(lora[u][:, :, :], A["lora"][k, u]).then_inc(pair_in[u], 16)

            def load_gate(k, u):
                sp.dma_start(sg[u][:, :], of_pair[k, u, :, 3]).then_inc(sg_in[u], 16)

            def store_pair(k):
                for u in range(2):
                    sp.wait_ge(y_ready, k * 2 + (u + 3))
                    sp.dma_start(mix_d[k, u], sg[u][:, :]).then_inc(mix_stored, 16)
                sp.wait_ge(mix_stored, k * 32 + 32)

            for u in range(2):
                load_lora(0, u)
                load_pair(0, u)
            for name, buf in (("blk1", blk1), ("starts", starts), ("tri", tri), ("corner", corner)):
                sp.dma_start(buf[...], A[name]).then_inc(mask_in, 16)
            for u in range(2):
                load_gate(0, u)
            with sp.Fori(0, FT // 2 - 1) as k:
                sp.wait_ge(r_job, k * len(rj.jobs) + rj.number(("rate", 1)))
                for u in range(2):
                    load_lora(k + 1, u)
                sp.wait_ge(v_blocks, k * 4 + 4)
                sp.wait_ge(r_dve, k * rj.total("dve") + (1 + rj.copies(("bonus", 1))))
                for u in range(2):
                    load_pair(k + 1, u)
                store_pair(k)
                for u in range(2):
                    load_gate(k + 1, u)
            sp.wait_ge(r_dve, (FT // 2 - 1) * rj.total("dve") + 1 + rj.copies(("invT", LEVELS - 1, 1, 4)))
            for buf, src in ((lam, "lam"), (sign, "sign"), (expo, "expo"), (count, "count"),
                             (swap, "swap"), (bc, "bc")):
                sp.dma_start(buf[...], A[src]).then_inc(s5_in, 16)
            store_pair(FT // 2 - 1)
            sp.wait_ge(phase_over, 3 * 3)
            sp.dma_start(d_row[:, :, :].rearrange("p g q -> p (g q)"),
                         A["d"].partition_broadcast(GP)).then_inc(d_in, 16)

            def load_ucm(b):
                sp.dma_start(ucm[:, :, :], u_d.rearrange("(c j) (b f) -> b c j f", j=T8, f=P)[b])\
                  .then_inc(ucm_in, 16)

            def skewed(b, n):
                sp.wait_ge(kpad_ready, b + (n + 1))
                for i in range(T8):
                    sp.dma_start(w3[n][i * GP:(i + 1) * GP, :, :],
                                 kpad[n][:, :, P - i * GP:2 * P - i * GP]).then_inc(w3_in[n], 16)

            load_ucm(0)
            sp.wait_ge(u_grouped, 1)
            load_ucm(1)
            with sp.Fori(0, FT // 2 - 1) as k:
                for n in range(2):
                    skewed(k * 2, n)
                    sp.wait_ge(u_grouped, k * 2 + (n + 2))
                    load_ucm(k * 2 + (n + 2))
            for n in range(2):
                skewed(FT - 2, n)
            sp.wait_ge(phase_over, 3 * 4)
            for h in range(2):
                half = slice(h * FT // 2, (h + 1) * FT // 2)
                sp.dma_start(gy[:, half, :], gy_d[half].rearrange("f p t -> p f t"))\
                  .then_inc(gy_in[h], 16)
            for n in range(2):
                sp.dma_start(sgt[n][:, :, :], sgate_d[n].rearrange("j p t -> p j t"))\
                  .then_inc(sgt_in[n], 16)
            sp.dma_start(mix_tiles[:, 0:FT, :], mix_d[0:4].rearrange("a u p t -> p (a u) t"))\
              .then_inc(mix_in, 16)
            load_piece(sp, 0, P_GLU + 2)
            load_piece(sp, 0, P_GLU + 3)
            for n in range(2, 4):
                load_piece(sp, 0, P_GLU + 2 + n)
                sp.wait_ge(glu_mixed, n - 1)
                sp.dma_start(sgt[n % 2][:, :, :], sgate_d[n].rearrange("j p t -> p j t"))\
                  .then_inc(sgt_in[n % 2], 16)

            def store_h(to, layer):
                for t in range(TT):
                    sp.wait_ge(h_ready, TT * layer + t + 1)
                    sp.dma_start(to.rearrange("(a p) d -> a p d", p=P)[t], x6[:, t, :])\
                      .then_inc(h_stored, 16)

            sp.wait_ge(glu_mixed, 4)
            sp.dma_start(x6[:, :, :], A["x"].rearrange("(a p) d -> p a d", p=P)).then_inc(h_in, 16)
            with sp.Fori(0, 8) as k:
                load_piece(sp, k, P_OUT0 + 2)
                load_piece(sp, k, P_OUT0 + 3)
            store_h(h1_d, 0)
            sp.wait_ge(phase_over, 3 * 5)
            sp.dma_start(pos[:, :], A["pos"].partition_broadcast(P)).then_inc(rope_in, 16)
            sp.dma_start(rope_c[:, :], A["rope_c"]).then_inc(rope_in, 16)
            sp.dma_start(fold[:, :], A["fold"]).then_inc(rope_in, 16)
            sp.dma_start(neg_tri[:, :], A["neg_tri"]).then_inc(rope_in, 16)
            load_piece(sp, 0, P_IN1 + 2)
            with sp.Fori(0, 12) as k:
                load_piece(sp, k, P_IN1 + 3)
                load_piece(sp, k, P_IN1 + 4)
            with sp.Fori(0, 8) as k:
                load_piece(sp, k, P_UP + 2)
                load_piece(sp, k, P_UP + 3)
            for first, end in ((0, 2), (2, 7)):
                with sp.Fori(first, end) as k:
                    load_piece(sp, k, P_OUT1 + 2)
                    load_piece(sp, k, P_OUT1 + 3)
                if first == 0:
                    sp.wait_ge(mix_split, 2 * KT)
                    sp.dma_start(x6[:, :, :], h1_d.rearrange("(a p) d -> p a d", p=P)).then_inc(h_in, 16)
            store_h(out[0], 1)
            sp.wait_ge(h_stored, 32 * TT)

        @block.gpsimd
        def _(pool):
            pool.memset(ones[:, :], 1.0).then_inc(consts_set, 1)
            with pool.Fori(0, P_GLU // 2) as k:
                split_lo(pool, k, 0)
                split_lo(pool, k, 1)
            split_lo(pool, P_GLU // 2, 0)
            pool.wait_ge(phase_over, 6)
            for b in (v_d, b_d, k_d):
                for u in range(2):
                    pool.memset(b[u][:, :, :], 0.0).then_inc(blocks_zero, 1)
            pool.sem_inc(y_ready, 2)
            with pool.Fori(0, FT // 2) as k:
                for u in range(2):
                    pool.wait_ge(exp_done, k * 2 + (u + 1))
                    pool.wait_ge(bonus_in, k * 2 + (u + 1))
                    for h in range(2):
                        rows, blk = slice(64 * h, 64 * h + 64), slice(64 * h, 64 * h + 64)
                        pool.tensor_tensor(
                            k_d[u][rows, :, blk], kp[u][rows, :].rearrange("p (c t) -> p c t", c=NC),
                            shrink[u][rows, :].rearrange("p (c t) -> p c t", c=NC), ALU.mult)\
                            .then_inc(keys_decayed, 1)
                pool.wait_ge(keys_decayed, k * 4 + 4)
                for u in range(2):
                    pool.wait_ge(r_job, k * len(rj.jobs) + rj.number(("turn", "v", u, 4)))
                    pool.wait_ge(r_dve, k * rj.total("dve") + (1 + rj.copies(("pairs", "b", u, NC - 2))))
                    for c in range(0, NC, 4):
                        over_4 = lambda m: m.unsqueeze(1).broadcast_to((P, 4, P))
                        t = inv_t[u][:, c:c + 4, :]
                        pool.tensor_tensor(t, rb[u][:, c:c + 4, CH:], over_4(corner[:, LEVELS, :]),
                                           ALU.mult).then_inc(inv_begun, 1)
                        pool.wait_ge(inv_begun, k * 8 + (4 * u + c // 2 + 1))
                        pool.tensor_tensor(t, t, over_4(ident[:, :]), ALU.add).then_inc(inv_begun, 1)
                for u in range(2):
                    pool.wait_ge(bonus_ready, k * 2 + (u + 1))
                    pool.wait_ge(y_normed, k * 2 + (u + 3))
                    pool.tensor_tensor(y_t[u], y_t[u], bonus[u][:, :], ALU.add).then_inc(y_summed, 1)
                    pool.wait_ge(y_summed, k * 2 + (u + 1))
                    pool.wait_ge(sg_in[u], k * 16 + 16)
                    pool.tensor_tensor(sg[u][:, :], y_t[u], sg[u][:, :], ALU.mult).then_inc(y_ready, 1)
            pool.wait_ge(phase_over, 3 * 3)
            for zeros in (kpad[0][:, :, :], kpad[1][:, :, :], xst[:, :, 0:1]):
                pool.memset(zeros, 0.0).then_inc(zeros_set, 1)
            split_lo(pool, P_GLU // 2, 1)
            with pool.Fori(P_GLU // 2 + 1, N_PIECES // 2) as k:
                split_lo(pool, k, 0)
                split_lo(pool, k, 1)

        @block.scalar
        def _(act):
            ch = Chain(act, act_chain)
            act.wait_ge(cols_in, 16)
            act.activation(csilu[:, :], col("c", 0, 16), ACT.Silu).then_inc(csilu_set, 1)

            def norm_stage(layer, xt, ztmp, squares):
                if layer == 0:
                    act.wait_ge(x_in, 16)
                for t in range(TT):
                    if layer == 1:
                        act.wait_ge(h_ready, t + 1)
                    ch(act.activation(squares[t], xt[:, t, :], ACT.Square, accum_out=small[:, t:t + 1]))
                ch.wait()
                act.activation(small[:, 4:8], small[:, 0:4], ACT.Sqrt, bias=EPS,
                               scale=1.0 / D).then_inc(root_done, 1)
                if layer == 0:
                    split_hi(act, 0, 0)
                act.wait_ge(mod_ready, 3 * layer + 1)
                for k in range(KT):
                    act.wait_ge(x_turned, KT * layer + k + 1)
                    if k >= 2:
                        act.wait_ge(z_ready, KT * layer + k - 1)
                    act.activation(ztmp[:, k % 2, :], ps[2 + k % 2][:, :], ACT.Identity,
                                   bias=modc[layer][:, k:k + 1],
                                   scale=modc[layer][:, 16 + k:17 + k]).then_inc(z_scaled, 1)

            norm_stage(0, xt, ztmp, [w[:, :] for w in (*whi, *wlo)])
            over(act, 1)

            split_hi(act, 0, 1)
            act.wait_ge(piece_used, 1)
            act.activation(shift[:, 0, 1:257], ps[7][:, 0:256], ACT.Copy).then_inc(proj_out, 1)
            act.activation(shift[:, 0, 257:], ps[7][:, 256:], ACT.Copy).then_inc(proj_out, 1)
            split_hi(act, 0, 2)
            act.wait_ge(mixed, 1)
            act.activation(lo_in[0:64, :], lo_in[0:64, :], ACT.Tanh)

            def copy_group(k, u):
                split_hi(act, k * 2, 2 * u + 3)
                split_hi(act, k * 2, 2 * u + 4)
                act.wait_ge(piece_used, k * 4 + (2 * u + 3))
                act.wait_ge(mixed, k * 2 + (u + 1))
                ch(act.activation(shift[:, 0, 1:], ps[2 * u][:, :], ACT.Copy))
                act.activation(shift[:, 1, 1:], ps[2 * u + 1][:, :], ACT.Copy).then_inc(proj_out, 1)

            def store_group(k, u, silu):
                act.wait_ge(mixed, k * 2 + (u + 2))
                if silu:
                    ch(act.activation(res[u][:, :, :], res[u][:, :, :], ACT.Silu))
                    ch.wait()
                act.dma_start(mixed_d[k * 2 + u].rearrange("j p t -> p j t"),
                              res[u][:, :, :]).then_inc(res_stored[u], 16)

            with act.Fori(0, 6) as k:
                ch.enter(k, 2)
                for u in range(2):
                    copy_group(k, u)
                    store_group(k, u, False)
                ch.leave(6)
            with act.Fori(6, 8) as k:
                ch.enter(k, 4, 6)
                for u in range(2):
                    copy_group(k, u)
                    store_group(k, u, True)
                ch.leave(2)
            def u_group(k, u, first):
                split_hi(act, k * 2, 2 * u + 3)
                split_hi(act, k * 2, 2 * u + 4)
                act.wait_ge(piece_used, k * 4 + (2 * u + 3))
                if not first:
                    act.wait_ge(u_stored[u], (k - 8) * 16)
                for t in range(TT):
                    o = act.activation(ures[u][:, t, :], ps[4 - 4 * u + t][:, 0:256], ACT.Copy)
                    if t < TT - 1:
                        ch(o)
                o.then_inc(proj_out, 1)
                ch.wait()
                act.wait_ge(proj_out, k * 2 + (u + 3))
                act.dma_start(u_d.rearrange("(a p) (g w) -> g p a w", p=P, w=256)[(k - 8) * 2 + u],
                              ures[u][:, :, :]).then_inc(u_stored[u], 16)

            for k in range(8, 10):
                for u in range(2):
                    u_group(k, u, k == 8)
            for k in range(10, 12):
                for u in range(2):
                    if k * 4 + 2 * u + 4 < P_GLU:
                        split_hi(act, k * 2, 2 * u + 3)
                        split_hi(act, k * 2, 2 * u + 4)
                    act.wait_ge(piece_used, k * 4 + (2 * u + 3))
                    act.wait_ge(res_stored[u], 16 * (k - 2))
                    ch(act.activation(res[u][:, 0, :], ps[2 * u][:, :], ACT.Silu))
                    act.activation(res[u][:, 1, :], ps[2 * u + 1][:, :], ACT.Silu).then_inc(proj_out, 1)
                    ch.wait()
                    act.wait_ge(proj_out, k * 2 + (u + 3))
                    act.dma_start(sgate_d[(k - 10) * 2 + u].rearrange("j p t -> p j t"),
                                  res[u][:, :, :]).then_inc(res_stored[u], 16)
            over(act, 2)

            act.wait_ge(blocks_zero, 6)
            act.sem_inc(r_act, 1)
            with act.Fori(0, FT // 2) as k:
                ch.enter(k, 2)

                def job(key):
                    act.wait_ge(r_job, k * len(rj.jobs) + rj.number(key))
                    return ps[rj.bank(key)]

                for u in range(2):
                    act.wait_ge(pair_in[u], k * 32 + 32)
                    act.activation(sq[u][:, :], rkv[u][:, 1, :], ACT.Square,
                                   scale=rcol("kk", k, u, 2)).then_inc(key_squared, 1)
                for u in range(2):
                    b = job(("decay", u))
                    act.activation(cum[u][:, :], b[:, :], ACT.Sigmoid,
                                   bias=rcol("w0", k, u, 2)).then_inc(r_act, 1)
                    b = job(("rate", u))
                    act.activation(rate[u][:, :], b[:, :], ACT.Sigmoid,
                                   bias=rcol("a0", k, u, 2)).then_inc(r_act, 1)
                for u in range(2):
                    act.wait_ge(norm_max, k * 2 + (u + 1))
                    act.activation(root[u][:, :], root[u][:, :], ACT.Sqrt).then_inc(norm_root, 1)
                for u in range(2):
                    act.wait_ge(cum_done, k * 2 + (u + 1))
                    ch(act.activation(grow[u][:, :, 1:], cum[u][:, :].rearrange(
                        "p (c t) -> p c t", c=NC), ACT.Exp, scale=-DECAY))
                    act.activation(shrink[u][:, :], cum[u][:, :], ACT.Exp, scale=DECAY)\
                       .then_inc(exp_done, 1)
                for u in range(2):
                    for h in range(2):
                        act.activation(
                            v_d[u][64 * h:64 * h + 64, :, 64 * h:64 * h + 64],
                            rkv[u][64 * h:64 * h + 64, 2, :].rearrange("p (c t) -> p c t", c=NC),
                            ACT.Copy).then_inc(v_blocks, 1)
                act.wait_ge(y_ready, k * 2 + 2)
                for u in range(2):
                    for x, to in (("b", b_t), ("k", k_t), ("v", v_t)):
                        for c in range(0, NC, 4):
                            b = job(("turn", x, u, c))
                            act.activation(to[u][:, c:c + 4, :].rearrange("p c s -> p (c s)"),
                                           b[:, :], ACT.Copy).then_inc(r_act, 1)
                for u in range(2):
                    act.wait_ge(r_dve, k * rj.total("dve") + (1 + rj.copies(("bonus", u))))
                    act.activation(bonus[u][:, :], bonus[u][:, :], ACT.Identity,
                                   bias=rcol("lnxb", k, u, 2)).then_inc(bonus_ready, 1)
                for c in range(NC):
                    for n, x in enumerate("wu"):
                        for u in range(2):
                            b = job((x, c, u))
                            act.activation(wu[u][:, n, :], b[:, 0:P], ACT.Copy).then_inc(r_act, 1)
                for u in range(2):
                    act.wait_ge(y_centred, k * 2 + (u + 1))
                    act.activation(sq[u][:, :], y_t[u], ACT.Square).then_inc(y_squared, 1)
                for u in range(2):
                    b = job(("var", u))
                    act.activation(root[u][:, :], b[:, :], ACT.Sqrt, bias=LNX_EPS,
                                   scale=1.0 / HN).then_inc(r_act, 1)
                ch.leave(FT // 2)
            over(act, 3)

            act.wait_ge(y_ready, FT + 2)
            act.wait_ge(s5_in, 16 * 6)
            act.activation(e1[0][:, :], lam[:, 2, :], ACT.Exp).then_inc(s5_mag, 1)
            act.wait_ge(s5_angle, 1)
            act.activation(e1[3][:, :], e1[1][:, :], ACT.Exp).then_inc(s5_mag, 1)
            act.activation(pt1[:, :, :], pw_re[:, :, :], ACT.Exp).then_inc(s5_mag, 1)
            act.activation(mag8[:, :], mag8[:, :], ACT.Exp).then_inc(s5_mag, 1)
            act.activation(e1[4][:, :], e1[2][:, :], ACT.Sin, scale=SAFE_TURN).then_inc(s5_sine, 1)
            act.activation(e1[5][:, :], e1[2][:, :], ACT.Sin, scale=SAFE_TURN / 2).then_inc(s5_sine, 1)
            act.activation(pt2[:, :, :], pw_im[:, :, :], ACT.Sin, scale=SAFE_TURN / 2).then_inc(s5_sine, 1)
            act.wait_ge(s5_sine, 3)
            act.activation(pw_im[:, :, :], pw_im[:, :, :], ACT.Sin, scale=SAFE_TURN).then_inc(s5_sine, 1)

            def job5(turn, key):
                act.wait_ge(s_job, s5_count(turn, key))
                return ps[S5_JOBS[key]]

            def group_u(k, n):
                act.wait_ge(ucm_in, k * 32 + (16 * n + 16))
                act.activation(ugm[:, :, :].rearrange("c g (j p) -> c j g p", j=T8),
                               ucm[:, :, :].rearrange("c j (g p) -> c j g p", g=GB),
                               ACT.Copy).then_inc(u_grouped, 1)

            def sines(k, n):
                act.wait_ge(s5_angle, k * 2 + (n + 2))
                ch(act.activation(cosc[n][:, :, :], turn5[:, :, :], ACT.Sin, scale=SAFE_TURN / 2))
                act.activation(sinc[n][:, :, :], turn5[:, :, :], ACT.Sin, scale=SAFE_TURN)\
                   .then_inc(s5_sine, 1)

            def front5(turn, n):
                p = job5(turn, "uc")
                act.activation(uc[n][:, :, :].rearrange("p g c -> p (g c)"), p[:, :],
                               ACT.Copy).then_inc(s_act, 1)
                for m in range(2):
                    p = job5(turn, f"wv{m}")
                    act.activation(wv[n][:, 4 * m:4 * m + 4, :].rearrange("p g c -> p (g c)"), p[:, :],
                                   ACT.Copy).then_inc(s_act, 1)

            def turn5_act(turn, b, f, g):
                p = job5(turn, "v")
                act.activation(vin[:, :, :].rearrange("p g c -> p (g c)"), p[:, :], ACT.Copy).then_inc(s_act, 1)
                if f:
                    front5(turn, f[1])
                for m in range(2):
                    p = job5(turn, f"y{m}")
                    act.activation(
                        ycm[:, :, 64 * m:64 * m + 64].rearrange("c j (g p) -> c j g p", p=GP),
                        p[0:C8, :].rearrange("c (g j p) -> c j g p", g=4, p=GP), ACT.Copy).then_inc(s_act, 1)
                if g:
                    group_u(*g)
                p = job5(turn, "yt")
                if turn != 1:
                    act.wait_ge(gy_stored, b[0] * 32 + 16 * b[1])
                act.activation(gy_out[:, :].rearrange("p (c j) -> p c j", j=T8),
                               p[:, :].rearrange("p (j c) -> p c j", c=C8),
                               ACT.Gelu_apprx_tanh).then_inc(s_act, 1)
                act.wait_ge(s_act, s5_count(turn, "yt", S5_COPIES))
                act.dma_start(gy_d.rearrange("(a b) p t -> a b p t", b=2)[b[0], b[1]], gy_out[:, :])\
                   .then_inc(gy_stored, 16)
                if g:
                    sines(*g)

            group_u(0, 0)
            sines(0, 0)
            front5(0, 0)
            group_u(0, 1)
            sines(0, 1)

            def act_turn(turn, b, f, g):
                if not isinstance(turn, int) and turn[1] == 0:
                    ch.enter(turn[0], 2, 1)
                turn5_act(turn, b, f, g)
                if not isinstance(turn, int) and turn[1] == 1:
                    ch.leave(FT // 2 - 2)

            s5_turns(act, act_turn)
            act.wait_ge(gy_stored, FT * 16)
            over(act, 4)

            split_hi(act, 0, P_GLU)
            split_hi(act, 0, P_GLU + 1)
            for n in range(4):
                u = n % 2
                if n >= 2:
                    act.wait_ge(glu_mixed, n - 1)
                split_hi(act, 0, P_GLU + 2 + n)
                ch(act.activation(gsig[u][:, 0, :], ps[2 * u][:, :], ACT.Sigmoid, bias=col("glub", 2 * n)))
                act.activation(gsig[u][:, 1, :], ps[2 * u + 1][:, :], ACT.Sigmoid,
                               bias=col("glub", 2 * n + 1)).then_inc(glu_out, 1)

            def out_group(layer, k, u, last=False):
                first = (P_OUT0, P_OUT1)[layer] + 2 * u + 2
                if not last:
                    for h in range(2):
                        split_hi(act, k * 2, first + h)
                act.wait_ge(out_scaled, k * 2 + (8 * layer + u + 1))
                act.wait_ge(out_read, k * 2 + (10 * layer + u + 2))
                ch.wait()
                for t in range(TT):
                    parts = sum_parts[:, t, :].rearrange("p (a b) -> p a b", b=2)[:, k, u:u + 1]
                    o = act.activation(ztmp6[:, :, :].rearrange("p a b -> p (a b)")[:, 256 * t:256 * t + 256],
                                       ps[4 * u + t][:, 0:256], ACT.Square, accum_out=parts)
                    ch(o) if t < TT - 1 else o.then_inc(out_read, 1)

            def out_stage(layer):
                if layer == 0:
                    act.wait_ge(glu_out, 4)
                    ch.wait()
                act.sem_inc(out_read, 2)
                turns = 3 if layer else 4
                with act.Fori(0, turns) as k:
                    ch.enter(k, 6)
                    for u in range(2):
                        out_group(layer, k, u)
                    ch.leave(turns)
                if layer:
                    for u in range(2):
                        out_group(layer, 3, u, last=(u == 1))
                act.wait_ge(squares_summed, layer + 1)
                act.activation(small[:, 4:8], small[:, 0:4], ACT.Sqrt, bias=EPS,
                               scale=1.0 / D).then_inc(root_done, 1)

            out_stage(0)

            norm_stage(1, x6, ztmp6, [zl[:, 4 * t:4 * t + 4, :].rearrange("p a b -> p (a b)")
                                      for t in range(TT)])
            over(act, 5)

            split_hi(act, 0, P_IN1 + 2)
            act.sem_inc(in1_read, 2)
            act.wait_ge(angle, 1)
            act.activation(r2[:, :], r1[:, :], ACT.Sin, scale=SAFE_TURN / 2).then_inc(rope_sine, 1)
            act.wait_ge(rope_sine, 1)
            act.activation(r1[:, :], r1[:, :], ACT.Sin, scale=SAFE_TURN).then_inc(rope_sine, 1)

            def in1_group(k, u, to, func):
                for h in range(2):
                    split_hi(act, k * 2, P_IN1 + 3 + 2 * u + h)
                act.wait_ge(piece_used, k * 4 + (P_IN1 + 3 + 2 * u))
                ch(act.activation(to[0], ps[2 * u][:, :], func))
                act.activation(to[1], ps[2 * u + 1][:, :], func).then_inc(in1_read, 1)

            with act.Fori(0, 2) as k:
                ch.enter(k, 2)
                for u in range(2):
                    in1_group(k, u, [cq[:, :, :].rearrange("p (a b) t -> p a b t", b=4)[:, k, 2 * u + j]
                                     for j in range(2)], ACT.Copy)
                ch.leave(2)
            for first, end in ((0, 2), (2, 4)):
                with act.Fori(first, end) as k:
                    ch.enter(k, 2, first)
                    for u in range(2):
                        in1_group(k + 2, u, [sg1[:, :, :].rearrange("p (a b) t -> p a b t", b=4)
                                             [:, k, 2 * u + j] for j in range(2)], ACT.Silu)
                    ch.leave(2)
                if first == 0:
                    act.wait_ge(c_summed, 1)
                    for n, to in enumerate((ktmp, rms_kv)):
                        act.activation(to[:, :], ps[4 + n][:, :], ACT.Sqrt, bias=EPS,
                                       scale=1.0 / 512).then_inc(c_root, 1)
            over(act, 6)

            for i in range(8):
                act.activation(zh[:, i, :], cq[:, i, :], ACT.Copy).then_inc(c_hi, 1)
            act.wait_ge(c_split, 8)
            act.sem_inc(a_act, aj.total("act"))
            with act.Fori(0, H // 2) as k:
                def job(key):
                    act.wait_ge(a_job, k * len(aj.jobs) + aj.number(key))
                    return ps[aj.bank(key)]

                for a in range(2):
                    for x, to in (("qn", qn), ("key", key9)):
                        p = job((x, a))
                        act.activation(to[a][:, :], p[:, :], ACT.Copy).then_inc(a_act, 1)
                for a in range(2):
                    for b in range(TT):
                        i, w = TT * a + b, (b + 1) * P
                        act.wait_ge(max_ready, k * 8 + (i + 1))
                        p = job(("s", a, b))
                        act.activation(probs[a][:, b, 0:w], p[:, 0:w], ACT.Exp, scale=SCALE,
                                       bias=stat[:, 0, i:i + 1],
                                       accum_out=stat[:, 1, i:i + 1]).then_inc(a_act, 1)
                for n in range(2):
                    p = job(("v", n))
                    act.activation(v9[:, 2 * n:2 * n + 2, :].rearrange("p t v -> p (t v)"), p[:, :],
                                   ACT.Copy).then_inc(a_act, 1)
                split_hi(act, k, P_UP + 2)
                split_hi(act, k, P_UP + 3)
            over(act, 7)

            out_stage(1)
            over(act, 8)

        @block.tensor
        def _(pe):
            pe.wait_ge(ident_in, 16)
            pe.wait_ge(consts_set, 1)

            def column_sums(bank):
                flat = acc[:, :, :].rearrange("p a b -> p (a b)")
                for j in range(32):
                    last = pe.matmul(bank[:, j:j + 1], flat[:, j * P:(j + 1) * P], ones[:, 0:1],
                                     start=True, stop=True)
                return last

            def gate_sums():
                for j in range(4):
                    last = pe.matmul(ps[4 + j][:, :], ones[:, :], acc[:, 2, 512 * j:512 * (j + 1)],
                                     start=True, stop=True)
                return last

            def normed_input(layer, xt, diag, piece):
                def product(k):
                    if k == 0:
                        piece_ready(pe, 0, piece)
                    pe.wait_ge(z_ready, KT * layer + k + 1)
                    hi, lo = (w[piece % 2][:, k * P:(k + 1) * P] for w in (whi, wlo))
                    for n, (a, b) in enumerate(((hi, zh), (hi, zl), (lo, zh))):
                        last = pe.matmul(ps[7][:, :], a, b[:, k, :], start=(k == 0 and n == 0),
                                         stop=(k == KT - 1 and n == 2))
                    return last

                pe.wait_ge(x_normed, layer + 1)
                for k in range(KT):
                    if k >= 2:
                        pe.wait_ge(z_scaled, KT * layer + k - 1)
                    for t in range(TT):
                        last = pe.matmul(ps[2 + k % 2][:, t * P:(t + 1) * P], xt[:, t, k * P:(k + 1) * P],
                                         diag[:, t, :], start=True, stop=True)
                    last.then_inc(x_turned, 1)
                    if k >= 2:
                        product(k - 2)
                product(KT - 2)
                product(KT - 1).then_inc(piece_used, 1)

            def half_tile(bank, s, h, j, width, wide):
                for kk in range(wide):
                    k = h * wide + kk
                    o = kk * width + j * P
                    hi, lo = whi[s][:, o:o + P], wlo[s][:, o:o + P]
                    for n, (a, b) in enumerate(((hi, zh), (hi, zl), (lo, zh))):
                        last = pe.matmul(bank, a, b[:, k, :], start=(k == 0 and n == 0),
                                         stop=(k == KT - 1 and n == 2))
                return last

            def group(k, n, b):
                for h in range(2):
                    piece_ready(pe, k, n + h)
                    for j in range(2):
                        last = half_tile(ps[b + j][:, :], (n + h) % 2, h, j, 256, 8)
                    last.then_inc(piece_used, 1)
                return last

            pe.wait_ge(acc_ready, 1)
            column_sums(ps[0]).then_inc(mod_sums, 1)
            normed_input(0, xt, diag1, 0)
            over(pe, 1)

            for first, end in ((0, 2), (2, 8)):
                with pe.Fori(first, end) as k:
                    for u in range(2):
                        pe.wait_ge(proj_out, k * 2 + (u + 1))
                        group(k * 2, 2 * u + 1, 2 * u)
                if first == 0:
                    pe.wait_ge(acc_ready, 2)
                    gate_sums().then_inc(mod_sums, 1)
            pe.wait_ge(mod_ready, 2)
            with pe.Fori(8, 10) as k:
                for u in range(2):
                    pe.wait_ge(proj_out, k * 2 + (u + 1))
                    for h in range(2):
                        piece_ready(pe, k * 2, 2 * u + 1 + h)
                        s = (1 + h) % 2
                        for t in range(TT):
                            for kk in range(8):
                                kt = h * 8 + kk
                                hi, lo = (w[s][:, kk * 256:(kk + 1) * 256] for w in (whi, wlo))
                                for n, (a, b) in enumerate(((zh, hi), (zl, hi), (zh, lo))):
                                    last = pe.matmul(ps[4 - 4 * u + t][:, 0:256],
                                                     a[:, kt, t * P:(t + 1) * P], b,
                                                     start=(kt == 0 and n == 0),
                                                     stop=(kt == KT - 1 and n == 2))
                        last.then_inc(piece_used, 1)
            pe.wait_ge(acc_ready, 3)
            pe.wait_ge(proj_out, 21)
            gate_sums().then_inc(mod_sums, 1)
            for k in range(10, 12):
                for u in range(2):
                    pe.wait_ge(proj_out, max(22, k * 2 + u + 1))
                    group(k * 2, 2 * u + 1, 2 * u)
                if k == 10:
                    pe.wait_ge(mod_ready, 3)
                    column_sums(ps[4]).then_inc(mod_sums, 1)
            pe.wait_ge(proj_out, 2 + 24)
            over(pe, 2)

            with pe.Fori(0, FT // 2) as k:
                def has_read(*keys):
                    for who, count in (("dve", r_dve), ("act", r_act)):
                        counts = [1 + rj.copies(x) for x in keys if rj.engine(x) == who]
                        if counts:
                            pe.wait_ge(count, k * rj.total(who) + max(counts))

                def bank(key, *needs):
                    old = rj.before(key)
                    has_read(*needs, *([] if old is None else [old]))
                    return ps[rj.bank(key)]

                def mm(out_ap, a, b, start, stop):
                    return pe.matmul(out_ap, a, b, start=start, stop=stop)

                pe.wait_ge(r_act, k * rj.total("act") + 1)
                pe.wait_ge(r_dve, k * rj.total("dve") + 1)
                for u in range(2):
                    pe.wait_ge(pair_in[u], k * 32 + 32)
                    for n, x in enumerate(("decay", "rate")):
                        b = bank((x, u))
                        mm(b[:, :], lora[u][:, n, :], lo_in[:, :], True, True).then_inc(r_job, 1)
                for u in range(2):
                    b = bank(("norm", u))
                    pe.wait_ge(mask_in, 64)
                    pe.wait_ge(key_squared, k * 2 + (u + 1))
                    mm(b[:, :], blk1[:, :], sq[u][:, :], True, True).then_inc(r_job, 1)
                for u in range(2):
                    b = bank(("bonus", u))
                    pe.wait_ge(bonus_in, k * 2 + (u + 1))
                    mm(b[:, :], blk1[:, :], bonus[u][:, :], True, True).then_inc(r_job, 1)
                    for x, src in (("b", b_d), ("k", k_d)):
                        for c in range(0, NC, 2):
                            b = bank(("pairs", x, u, c))
                            if x == "b":
                                pe.wait_ge(operands, k * 2 + (u + 1))
                            else:
                                pe.wait_ge(keys_decayed, k * 4 + (2 * u + 2))
                            for i in range(2):
                                last = mm(b[:, i * 192:i * 192 + 192], src[u][:, c + i, :],
                                          ra[u][:, c + i, :], True, True)
                            last.then_inc(r_job, 1)
                    for x, src in (("b", b_d), ("k", k_d), ("v", v_d)):
                        for c in range(0, NC, 4):
                            b = bank(("turn", x, u, c))
                            if x == "v":
                                pe.wait_ge(v_blocks, k * 4 + (2 * u + 2))
                            for i in range(4):
                                last = pe.transpose(b[:, i * P:(i + 1) * P],
                                                    src[u][:, c + i, :], ident[:, :])
                            last.then_inc(r_job, 1)
                for n in range(LEVELS):
                    for u in range(2):
                        for c in range(0, NC, 4):
                            b = bank(("at", n, u, c), ("pairs", "b", u, c + 2) if n == 0 else
                                     ("at", 0, u, c) if n == 1 else ("inv", n - 1, u, c))
                            for i in range(4):
                                if n == 0:
                                    last = pe.transpose(b[:, i * P:(i + 1) * P],
                                                        rb[u][:, c + i, CH:], ident[:, :])
                                else:
                                    last = mm(b[:, i * P:(i + 1) * P], rb[u][:, c + i, CH:],
                                              inv[u][:, c + i, :], True, True)
                            last.then_inc(r_job, 1)
                    for u in range(2 if n else 0):
                        for c in range(0, NC, 4):
                            for x in ("inv", "invT") if n < LEVELS - 1 else ("invT",):
                                if n == 1:
                                    pe.wait_ge(inv_begun, k * 8 + (4 * u + c // 2 + 2))
                                b = bank((x, n, u, c), ("at", n, u, c),
                                         *([("invT", n - 1, u, c)] if n > 1 else []))
                                for i in range(4):
                                    t = inv_t[u][:, c + i, :]
                                    y = at_inv[u][:, c + i, :]
                                    last = mm(b[:, i * P:(i + 1) * P], *((t, y) if x == "inv" else (y, t)),
                                              True, True)
                                last.then_inc(r_job, 1)
                for c in range(NC):
                    old, new = c % 2, (c + 1) % 2
                    for u in range(2):
                        b = bank(("w", c, u), *([] if c else [("turn", "v", u, 4),
                                                              ("pairs", "k", u, 6)]))
                        mm(b[:, 0:P], rk[u][:, c, CH:], v_t[u][:, c, :], True, False)
                        if c:
                            has_read(("s", c - 1, u))
                        else:
                            pe.wait_ge(state_zero, k * 2 + 2)
                        mm(b[:, 0:P], ra[u][:, c, CH:], state[u][:, old, :], False, True)\
                            .then_inc(r_job, 1)
                    for u in range(2):
                        mm(bank(("s", c, u))[:, 0:P], k_t[u][:, c, :], v_t[u][:, c, :], True, False)
                    for u in range(2):
                        b = bank(("u", c, u), ("w", c, u),
                                 *([] if c else [("invT", LEVELS - 1, u, 4)]))
                        mm(b[:, 0:P], inv_t[u][:, c, :], wu[u][:, 0, :], True, True).then_inc(r_job, 1)
                    for u in range(2):
                        y = ps[6 + u][:, c * CH:(c + 1) * CH]
                        mm(y, state[u][:, old, :], ra[u][:, c, 0:CH], True, False)
                        mm(y, v_t[u][:, c, :], rk[u][:, c, 0:CH], False, False)
                    for u in range(2):
                        has_read(("u", c, u))
                        mm(ps[rj.bank(("s", c, u))][:, 0:P], b_t[u][:, c, :], wu[u][:, 1, :], False, True)\
                            .then_inc(r_job, 1)
                    for u in range(2):
                        last = mm(ps[6 + u][:, c * CH:(c + 1) * CH], wu[u][:, 1, :],
                                  rb[u][:, c, 0:CH], False, True)
                        if c == NC - 1:
                            last.then_inc(y_out, 1)
                for u in range(2):
                    b = bank(("mean", u))
                    pe.wait_ge(y_copied, k * 2 + (u + 1))
                    mm(b[:, :], blk1[:, :], y_t[u], True, True).then_inc(r_job, 1)
                for u in range(2):
                    b = bank(("var", u))
                    pe.wait_ge(y_squared, k * 2 + (u + 1))
                    mm(b[:, :], blk1[:, :], sq[u][:, :], True, True).then_inc(r_job, 1)
            over(pe, 3)

            pe.wait_ge(s5_in, 16 * 6)

            def copied(turn, key):
                pe.wait_ge(s_act, s5_count(turn, key, S5_COPIES))

            def turn_tables(turn, k, n):
                p = ps[S5_JOBS["uc"]]
                pe.wait_ge(u_grouped, k * 2 + (n + 1))
                for g in range(GB):
                    last = pe.matmul(p[:, g * C8:(g + 1) * C8], ugm[:, g, :], ident[0:C8, 0:C8],
                                     start=True, stop=True)
                last.then_inc(s_job, 1)
                pe.wait_ge(w_ready, k * 4 + (2 * n + 1))
                for m in range(2):
                    p = ps[S5_JOBS[f"wv{m}"]]
                    for g in range(4):
                        last = pe.transpose(p[:, g * P:(g + 1) * P], wvt[:, 4 * m + g, :, :].rearrange(
                            "p j q -> p (j q)"), ident[:, :])
                    last.then_inc(s_job, 1)

            def response(turn, k, n):
                pe.wait_ge(w_ready, k * 4 + (2 * n + 2))
                for m in range(2):
                    p = ps[S5_JOBS[f"k{m}"]]
                    for g in range(4):
                        last = pe.matmul(p[0:GP, g * P:(g + 1) * P], bb[0][:, 4 * m + g, :],
                                         wc[n][:, 4 * m + g, 0:P], start=True, stop=True)
                    last.then_inc(s_job, 1)

            def pe_turn(turn, b, f, g):
                k, n = b
                if turn == 1:
                    copied(0, "wv1")
                else:
                    copied(turn - 1 if isinstance(turn, int) else (turn[0], turn[1] - 1), "y0")
                p = ps[S5_JOBS["v"]]
                for g in range(GB):
                    last = pe.matmul(p[:, g * C8:(g + 1) * C8], wv[n][:, g, :], uc[n][:, g, :],
                                     start=True, stop=True)
                last.then_inc(s_job, 1)
                copied(turn, "v")
                p = ps[S5_JOBS["vs"]]
                pe.matmul(p[:, :], swap[:, :], vin[:, :, :], start=True, stop=True).then_inc(s_job, 1)
                if f:
                    turn_tables(turn, *f)
                p = ps[S5_JOBS["zs"]]
                pe.wait_ge(x_ready, k * 4 + (2 * n + 1))
                pe.matmul(p[:, :], swap[:, :], zst[:, :, :], start=True, stop=True).then_inc(s_job, 1)
                if f:
                    response(turn, *f)
                pe.wait_ge(x_ready, k * 4 + (2 * n + 2))
                pe.wait_ge(w3_in[n], k * 128 + 128)
                for m in range(2):
                    p = ps[S5_JOBS[f"y{m}"]]
                    for g in range(4):
                        o = p[0:C8, g * P:(g + 1) * P]
                        pe.matmul(o, xst[:, 4 * m + g, :], wc[n][:, 4 * m + g, GP:], start=True, stop=False)
                        last = pe.matmul(o, uc[n][:, 4 * m + g, :], w3[n][:, 4 * m + g, :],
                                         start=False, stop=True)
                    last.then_inc(s_job, 1)
                copied(turn, "y1")
                p = ps[S5_JOBS["yt"]]
                for j in range(T8):
                    last = pe.matmul(p[:, j * C8:(j + 1) * C8], ycm[:, j, :], ident[0:C8, 0:C8],
                                     start=True, stop=True)
                last.then_inc(s_job, 1)

            turn_tables(0, 0, 0)
            response(0, 0, 0)
            s5_turns(pe, pe_turn)
            over(pe, 4)

            for n in range(4):
                u = n % 2
                if n >= 2:
                    pe.wait_ge(glu_out, n - 1)
                piece_ready(pe, 0, P_GLU + n)
                s = (P_GLU + n) % 2
                for j in range(2):
                    for kt in range(FT):
                        if n == 0 and j == 0:
                            pe.wait_ge(gy_split, kt + 1)
                        o = kt * 256 + j * P
                        hi, lo = whi[s][:, o:o + P], wlo[s][:, o:o + P]
                        for m, (a, b) in enumerate(((hi, zh), (hi, zl), (lo, zh))):
                            last = pe.matmul(ps[2 * u + j][:, :], a, b[:, FT + kt, :],
                                             start=(kt == 0 and m == 0), stop=(kt == FT - 1 and m == 2))
                last.then_inc(piece_used, 1)

            def out_gemm(layer, first_piece):
                with pe.Fori(0, 4) as k:
                    for u in range(2):
                        pe.wait_ge(out_read, k * 2 + (10 * layer + u + 1))
                        for h in range(2):
                            pe.wait_ge(mix_split, KT * layer + FT * (h + 1))
                            n = first_piece + 2 * u + h
                            piece_ready(pe, k * 2, n)
                            time_major(4 * u, n % 2, h, FT * layer)

            def time_major(bank, s, h, at):
                for t in range(TT):
                    for kk in range(8):
                        kt = h * 8 + kk
                        hi, lo = (w[s][:, kk * 256:(kk + 1) * 256] for w in (whi, wlo))
                        for n, (a, b) in enumerate(((zh, hi), (zl, hi), (zh, lo))):
                            last = pe.matmul(ps[bank + t][:, 0:256], a[:, (at + kt) % KT, t * P:(t + 1) * P], b,
                                             start=(kt == 0 and n == 0), stop=(kt == KT - 1 and n == 2))
                last.then_inc(piece_used, 1)

            out_gemm(0, P_OUT0)

            normed_input(1, x6, diag6, P_IN1)
            over(pe, 5)

            for first, end in ((0, 4), (4, 6)):
                with pe.Fori(first, end) as k:
                    for u in range(2):
                        pe.wait_ge(in1_read, k * 2 + (u + 1))
                        group(k * 2, P_IN1 + 1 + 2 * u, 2 * u)
                if first == 0:
                    pe.wait_ge(key_rotated, 1)
                    pe.matmul(ps[6][:, :], fold[:, :], ktmp[:, :], start=True, stop=True)\
                      .then_inc(key_folded, 1)
                    pe.wait_ge(c_squared, 1)
                    pe.matmul(ps[4][:, :], ones[:, :], r1[:, :], start=True, stop=True)
                    pe.matmul(ps[5][:, :], ones[:, :], r2[:, :], start=True, stop=True)\
                      .then_inc(c_summed, 1)
            over(pe, 6)

            with pe.Fori(0, H // 2) as k:
                def read9(*keys):
                    for who, count in (("dve", a_dve), ("act", a_act)):
                        turn = aj.total(who)
                        counts = [turn + aj.copies(x) for x in keys if aj.engine(x) == who]
                        if counts:
                            pe.wait_ge(count, k * turn + max(counts))

                def bank9(key, *needs):
                    old, counts = aj.before(key), {"dve": [], "act": []}
                    for x in (*needs, *([old] if old else [])):
                        counts[aj.engine(x)].append(aj.total(aj.engine(x)) + aj.copies(x))
                    if old is None:
                        x = aj.jobs[aj.number(key) - 1 - len(aj.banks)][0]
                        counts[aj.engine(x)].append(aj.copies(x))
                    for who, count in (("dve", a_dve), ("act", a_act)):
                        if counts[who]:
                            pe.wait_ge(count, k * aj.total(who) + max(counts[who]))
                    return ps[aj.bank(key)]

                def up(p, s, first, cs, left=False):
                    for kt in range(4):
                        o = kt * 512 + first
                        hi, lo = whi[s][:, o:o + P], wlo[s][:, o:o + P]
                        for n, (a, b) in enumerate(((hi, zh), (hi, zl), (lo, zh))):
                            last = pe.matmul(p[:, :], a, b[:, cs + kt, :], start=(kt == 0 and n == 0),
                                             stop=(kt == 3 and n == 2))
                            if left and kt == 0 and n == 0:
                                last.then_inc(piece_used, 1)
                    return last

                piece_ready(pe, k, P_UP)
                for a in range(2):
                    for n, x in enumerate(("qn", "qp", "key")):
                        p = bank9((x, a))
                        pe.wait_ge(c_split, 8 if x == "key" else 4)
                        if x == "key":
                            if a == 0:
                                piece_ready(pe, k, P_UP + 1)
                            last = up(p, (P_UP + 1) % 2, a * P, 4, left=(a == 1))
                        else:
                            last = up(p, P_UP % 2, a * 256 + n * P, 0)
                        last.then_inc(a_job, 1)
                for a in range(2):
                    for b in range(TT):
                        w, q = (b + 1) * P, slice(b * P, (b + 1) * P)
                        p = bank9(("s", a, b), ("qn", a), ("qp", a), ("key", a))
                        pe.matmul(p[:, 0:w], qn[a][:, q], key9[a][:, 0:w], start=True, stop=False)
                        pe.matmul(p[:, q], ident[:, :], neg_tri[:, :], start=False, stop=False,
                                  skip_group_check=True)
                        pe.matmul(p[:, 0:w], qp[a][:, q], key_pe[:, 0:w], start=False, stop=True)\
                          .then_inc(a_job, 1)

                for n in range(2):
                    p = bank9(("v", n))
                    for t in range(2):
                        for kt in range(4):
                            o = kt * 512 + 256
                            s = (P_UP + 1) % 2
                            hi, lo = (w[s][:, o:o + 256] for w in (whi, wlo))
                            for m, (x, y) in enumerate(((zh, hi), (zl, hi), (zh, lo))):
                                tok = (2 * n + t) * P
                                last = pe.matmul(p[:, t * 256:(t + 1) * 256], x[:, 4 + kt, tok:tok + P],
                                                 y, start=(kt == 0 and m == 0), stop=(kt == 3 and m == 2))
                    last.then_inc(a_job, 1)
                def turn_probs(i):
                    a, b = divmod(i, TT)
                    p = bank9(("pt", a, b))
                    pe.wait_ge(probs_ready, k * 8 + (i + 1))
                    for n in range(b + 1):
                        last = pe.transpose(p[:, n * P:(n + 1) * P], probs[a][:, b, n * P:(n + 1) * P],
                                            ident[:, :])
                        if i == 1 and n == 0:
                            last.then_inc(piece_used, 1)
                    last.then_inc(a_job, 1)

                def weigh(i):
                    a, b = divmod(i, TT)
                    if b == 0:
                        pe.wait_ge(o_read, k * 2 + (a + 1))
                    if i == 0:
                        read9(("v", 1))
                    read9(("pt", a, b))
                    for n in range(b + 1):
                        last = pe.matmul(ps[6 + a][:, b * P:(b + 1) * P], v9[:, n, a * P:(a + 1) * P],
                                         pt9[i % 2][:, n * P:(n + 1) * P], start=(n == 0), stop=(n == b))
                    if b == TT - 1:
                        last.then_inc(o_ready, 1)

                turn_probs(0)
                for i in range(1, 8):
                    turn_probs(i)
                    weigh(i - 1)
                weigh(7)
            over(pe, 7)

            out_gemm(1, P_OUT1)
            over(pe, 8)

        @block.vector
        def _(dve):
            ch = Chain(dve, dve_chain)
            ch(dve.memset(acc[:, 0:2, :], 0.0))
            dve.wait_ge(csilu_set, 1)
            ch.wait()

            def add_ada(part, piece, c, done):
                dve.scalar_tensor_tensor(acc[:, part, :], piece[:, :], c, acc[:, part, :],
                                         ALU.mult, ALU.add).then_inc(done, 1)

            def add_ada1(k):
                for n in range(A_SLOTS):
                    dve.wait_ge(ada1_full[n], k * 16 + 16)
                    if isinstance(k, int):
                        c = csilu[:, 4 * k + n // 2:4 * k + n // 2 + 1]
                    else:
                        c = csilu[:, :].rearrange("p (a b) -> p a b", b=4)[:, k, n // 2:n // 2 + 1]
                    if n >= 2 or not isinstance(k, int):
                        dve.wait_ge(ada1_used, k * 8 + (n - 1))
                    add_ada(n % 2, ada1[n], c, ada1_used)

            def add_ada2(k, u, adas):
                for q in range(adas):
                    if adas == 4:
                        m = 8 * k + 4 * u + q
                        dve.wait_ge(ada2_full[m % 2], 16 * (m // 2 + 1))
                        if m:
                            dve.wait_ge(ada2_used, m)
                        add_ada(2, ada2[m % 2], csilu[:, m:m + 1], ada2_used)
                    else:
                        dve.wait_ge(ada2_full[(3 * u + q) % 2], k * 48 + 16 * (3 + (3 * u + q) // 2))
                        dve.wait_ge(ada2_used, k * 6 + (2 + 3 * u + q))
                        add_ada(q, ada2[(3 * u + q) % 2], csilu[:, :].rearrange(
                            "p (a b) -> p a b", b=2)[:, k - 2, u:u + 1], ada2_used)

            def finish_columns(layer, bank):
                m = modc[layer]
                ch(dve.tensor_tensor(m[:, :], bank[:, 0:32], col(f"ab{layer}", 0, 32), ALU.add))
                ch.wait()
                ch(dve.scalar_tensor_tensor(m[:, 16:32], m[:, 16:32], 1.0, col(f"pre{layer}", 0, 16),
                                            ALU.add, ALU.mult))
                ch.wait()

            def finish_gate(layer):
                dve.wait_ge(gb_in, 16 * (2 + layer))
                if layer == 1:
                    dve.wait_ge(gp1_in, 16)
                for j in range(4):
                    ch(dve.tensor_tensor(gp[layer][:, j * 512:(j + 1) * 512], ps[4 + j][:, :],
                                         gp[layer][:, j * 512:(j + 1) * 512], ALU.add))
                ch.wait()
                ch(dve.tensor_tensor(gp[layer][:, :], gp[layer][:, :], post_b[:, :], ALU.mult))
                ch.wait()

            def norm_x(layer, diag):
                dve.wait_ge(root_done, 2 * layer + 1)
                ch(dve.reciprocal(small[:, 8:12], small[:, 4:8]))
                ch.wait()
                for t in range(TT):
                    ch(dve.tensor_scalar(diag[:, t, :], ident[:, :], small[:, 8 + t:9 + t], None,
                                         ALU.mult))
                ch.wait()
                dve.sem_inc(x_normed, 1)

            def split_z(layer, ztmp):
                for k in range(KT):
                    dve.wait_ge(z_scaled, KT * layer + k + 1)
                    ch(dve.tensor_copy(zh[:, k, :], ztmp[:, k % 2, :]))
                    ch.wait()
                    dve.tensor_tensor(zl[:, k, :], ztmp[:, k % 2, :], zh[:, k, :].bitcast(F32),
                                      ALU.subtract).then_inc(z_ready, 1)

            add_ada1(0)
            dve.wait_ge(ident_in, 16)
            norm_x(0, diag1)
            with dve.Fori(1, 2 * KT // A_SLOTS) as k:
                add_ada1(k)
            dve.wait_ge(ada1_used, 2 * KT)
            dve.sem_inc(acc_ready, 1)
            dve.wait_ge(mod_sums, 1)
            finish_columns(0, ps[0])
            dve.sem_inc(mod_ready, 1)
            split_z(0, ztmp)
            over(dve, 1)

            ch(dve.memset(shift[:, :, 0:1], 0.0))
            ch(dve.memset(acc[:, :, :], 0.0))
            ch.wait()

            def mix(j, out_ap, mu, o_inc=None):
                ch(dve.tensor_tensor(out_ap, shift[:, j, 0:L], shift[:, j, 1:], ALU.subtract))
                ch.wait()
                return dve.scalar_tensor_tensor(out_ap, out_ap, mu, shift[:, j, 1:],
                                                ALU.mult, ALU.add)

            dve.wait_ge(proj_out, 2)
            mix(0, lo_in[:, :], col("mu", 32)).then_inc(mixed, 1)

            def mix_group(k, u, first):
                dve.wait_ge(proj_out, k * 2 + (u + 3))
                if not first:
                    dve.wait_ge(res_stored[u], k * 16)
                ch(mix(0, res[u][:, 0, :], rcol("mu", k, 2 * u, 4)))
                mix(1, res[u][:, 1, :], rcol("mu", k, 2 * u + 1, 4)).then_inc(mixed, 1)

            for k in range(2):
                for u in range(2):
                    add_ada2(k, u, 4)
                    if k == 1 and u == 1:
                        dve.wait_ge(ada2_used, KT)
                        dve.sem_inc(acc_ready, 1)
                    mix_group(k, u, k == 0)
            dve.wait_ge(mod_sums, 2)
            finish_gate(0)
            dve.sem_inc(mod_ready, 1)
            ch(dve.memset(acc[:, :, :], 0.0))
            ch.wait()
            with dve.Fori(2, 8) as k:
                ch.enter(k, 6, 2)
                for u in range(2):
                    add_ada2(k, u, 3)
                    mix_group(k, u, False)
                ch.leave(6)
            with dve.Fori(8, 10) as k:
                for u in range(2):
                    add_ada2(k, u, 3)
            dve.wait_ge(ada2_used, 4 * KT)
            dve.sem_inc(acc_ready, 1)
            dve.wait_ge(mod_sums, 3)
            finish_gate(1)
            dve.sem_inc(mod_ready, 1)
            dve.wait_ge(mod_sums, 4)
            finish_columns(1, ps[4])
            dve.sem_inc(mod_ready, 1)
            over(dve, 2)

            for u in range(2):
                ch(dve.memset(ra[u][:, :, :], 0.0))
                ch(dve.memset(grow[u][:, :, 0:1], 1.0))
            ch.wait()
            dve.wait_ge(blocks_zero, 6)
            dve.wait_ge(mask_in, 64)

            def rwkv_turn(k):
                def read(key):
                    dve.wait_ge(r_job, k * len(rj.jobs) + rj.number(key))
                    return ps[rj.bank(key)]

                chunks = lambda ap: ap.rearrange("p (c t) -> p c t", c=NC)
                for u in range(2):
                    dve.memset(state[u][:, 0, :], 0.0).then_inc(state_zero, 1)
                dve.wait_ge(y_normed, k * 2 + 2)
                for u in range(2):
                    b = read(("norm", u))
                    ch(dve.tensor_scalar(root[u][:, :], b[:, :], 1e-24, None, ALU.max))
                    ch.wait()
                    dve.sem_inc(norm_max, 1)
                    dve.sem_inc(r_dve, 1)
                for u in range(2):
                    dve.wait_ge(r_act, k * rj.total("act") + 1 + rj.copies(("decay", u)))
                    dve.tensor_tensor_scan(cum[u][:, :], starts[:, :], cum[u][:, :], 0.0,
                                           ALU.mult, ALU.add).then_inc(cum_done, 1)
                def keys(u):
                    r, key = (rkv[u][:, n, :] for n in range(2))
                    dve.wait_ge(y_ready, k * 2 + 2)
                    dve.wait_ge(norm_root, k * 2 + (u + 1))
                    dve.wait_ge(r_act, k * rj.total("act") + 1 + rj.copies(("rate", u)))
                    ch(dve.reciprocal(root[u][:, :], root[u][:, :]))
                    ch(dve.tensor_scalar(bv[u][:, :], rate[u][:, :], -1.0, rcol("ka", k, u, 2),
                                         ALU.add, ALU.mult))
                    ch.wait()
                    ch(dve.scalar_tensor_tensor(kn[u][:, :], key, rcol("kk", k, u, 2),
                                                root[u][:, :], ALU.mult, ALU.mult))
                    ch(dve.scalar_tensor_tensor(kp[u][:, :], bv[u][:, :], 1.0, key,
                                                ALU.add, ALU.mult))
                    ch.wait()
                    ch(dve.scalar_tensor_tensor(bonus[u][:, :], r, rcol("rk", k, u, 2),
                                                kp[u][:, :], ALU.mult, ALU.mult))
                    ch(dve.tensor_tensor(bv[u][:, :], kn[u][:, :], rate[u][:, :], ALU.mult))
                    ch.wait()
                    dve.sem_inc(bonus_in, 1)

                def decayed(u):
                    dve.wait_ge(exp_done, k * 2 + (u + 1))
                    ch(dve.tensor_tensor(ra[u][:, :, 0:CH], chunks(rkv[u][:, 0, :]),
                                         grow[u][:, :, 1:], ALU.mult))
                    for h in range(2):
                        rows, blk = slice(64 * h, 64 * h + 64), slice(64 * h, 64 * h + 64)
                        ch(dve.scalar_tensor_tensor(
                            ra[u][rows, :, CH + 64 * h:CH + 64 * h + 64], chunks(kn[u][rows, :]),
                            -1.0, grow[u][rows, :, 0:CH], ALU.mult, ALU.mult))
                        ch(dve.tensor_tensor(b_d[u][rows, :, blk], chunks(bv[u][rows, :]),
                                             chunks(shrink[u][rows, :]), ALU.mult))
                    ch.wait()
                    dve.sem_inc(operands, 1)

                def take_pairs(u):
                    b = read(("bonus", u))
                    dve.tensor_tensor(bonus[u][:, :], b[:, :], rkv[u][:, 2, :], ALU.mult)\
                       .then_inc(r_dve, 1)
                    for x, to in (("b", rb), ("k", rk)):
                        for c in range(0, NC, 2):
                            b = read(("pairs", x, u, c))
                            dve.tensor_tensor(
                                to[u][:, c:c + 2, :], b[:, 0:384].rearrange("p (c s) -> p c s", c=2),
                                tri[:, :].unsqueeze(1).broadcast_to((P, 2, 3 * CH)), ALU.mult)\
                               .then_inc(r_dve, 1)

                keys(0)
                decayed(0)
                keys(1)
                dve.wait_ge(keys_decayed, k * 4 + 2)
                take_pairs(0)
                decayed(1)
                dve.wait_ge(keys_decayed, k * 4 + 4)
                take_pairs(1)
                quad = lambda b: b[:, :].rearrange("p (c s) -> p c s", c=4)
                eye = ident[:, :].unsqueeze(1).broadcast_to((P, 4, P))
                for u in range(2):
                    for c in range(0, NC, 4):
                        b = read(("at", 0, u, c))
                        over_4 = lambda m: m.unsqueeze(1).broadcast_to((P, 4, P))
                        t = inv[u][:, c:c + 4, :]
                        ch(dve.tensor_tensor(t, quad(b), over_4(corner[:, 0, :]), ALU.mult))
                        ch.wait()
                        dve.tensor_tensor(t, t, eye, ALU.add).then_inc(r_dve, 1)
                for n in range(1, LEVELS):
                    for u in range(2):
                        for c in range(0, NC, 4):
                            b = read(("at", n, u, c))
                            dve.tensor_tensor(
                                at_inv[u][:, c:c + 4, :], quad(b),
                                corner[:, n, :].unsqueeze(1).broadcast_to((P, 4, P)), ALU.mult)\
                               .then_inc(r_dve, 1)
                    for u in range(2):
                        for c in range(0, NC, 4):
                            for x, to in (("inv", inv), ("invT", inv_t)) if n < LEVELS - 1 else \
                                    (("invT", inv_t),):
                                b = read((x, n, u, c))
                                t = to[u][:, c:c + 4, :]
                                dve.tensor_tensor(t, quad(b), t, ALU.add).then_inc(r_dve, 1)
                for c in range(NC):
                    for u in range(2):
                        b, g = read(("s", c, u)), grow[u][:, c, CH:]
                        new = state[u][:, (c + 1) % 2, :]
                        if c == 0:
                            o = dve.tensor_scalar(new, b[:, 0:P], g, None, ALU.mult)
                        else:
                            ch.wait()
                            o = dve.scalar_tensor_tensor(new, b[:, 0:P], g, kept[u][:, :],
                                                         ALU.mult, ALU.add)
                        o.then_inc(r_dve, 1)
                    if c < NC - 1:
                        for u in range(2):
                            dve.wait_ge(r_dve, k * rj.total("dve") + (1 + rj.copies(("s", c, u))))
                            ch(dve.tensor_scalar(kept[u][:, :], state[u][:, (c + 1) % 2, :],
                                                 grow[u][:, c + 1, CH:], None, ALU.mult))
                for u in range(2):
                    dve.wait_ge(y_out, k * 2 + (u + 1))
                    dve.tensor_copy(y_t[u], ps[6 + u][:, :]).then_inc(y_copied, 1)
                for u in range(2):
                    b = read(("mean", u))
                    ch(dve.scalar_tensor_tensor(y_t[u], b[:, :], -1.0 / HN, y_t[u],
                                                ALU.mult, ALU.add))
                    ch.wait()
                    dve.sem_inc(r_dve, 1)
                    dve.sem_inc(y_centred, 1)
                for u in range(2):
                    y = y_t[u]
                    dve.wait_ge(r_act, k * rj.total("act") + 1 + rj.copies(("var", u)))
                    ch(dve.reciprocal(root[u][:, :], root[u][:, :]))
                    ch.wait()
                    dve.scalar_tensor_tensor(y, y, rcol("lnxg", k, u, 2), root[u][:, :],
                                             ALU.mult, ALU.mult).then_inc(y_normed, 1)

            dve.sem_inc(r_dve, 1)
            dve.sem_inc(y_normed, 2)
            with dve.Fori(0, FT // 2) as k:
                ch.enter(k, 46)
                rwkv_turn(k)
                ch.leave(FT // 2)
            over(dve, 3)

            def do(ins):
                ch(ins)
                ch.wait()

            def tt(o, a, b, op):
                do(dve.tensor_tensor(o, a, b, op))

            def ts(o, a, s1, op0, s2=None, op1=ALU.bypass):
                do(dve.tensor_scalar(o, a, s1, s2, op0, op1))

            def fraction(x, tmp):
                ts(tmp, x, MAGIC, ALU.add)
                ts(tmp, tmp, -MAGIC, ALU.add)
                tt(x, x, tmp, ALU.subtract)

            def to_turns(x, tmp):
                ts(tmp, x, 1.0 / TURN, ALU.mult, MAGIC, ALU.add)
                ts(tmp, tmp, -MAGIC, ALU.add)
                do(dve.scalar_tensor_tensor(x, tmp, -TURN_A, x, ALU.mult, ALU.add))
                do(dve.scalar_tensor_tensor(x, tmp, -TURN_B, x, ALU.mult, ALU.add))
                ts(x, x, 1.0 / TURN, ALU.mult, 0.5, ALU.min)
                ts(x, x, -0.5, ALU.max)

            e = [x[:, :] for x in e1]
            lam_re, lam_im = lam[:, 0, :], lam[:, 1, :]
            over_g = lambda ap: ap.unsqueeze(1).broadcast_to((P, NP, G))
            powers = expo[:, :].unsqueeze(2).broadcast_to((P, NP, G))
            dve.wait_ge(y_ready, FT + 2)
            dve.wait_ge(s5_in, 16 * 6)
            dve.wait_ge(s5_mag, 1)
            tt(e[1], lam_re, e[0], ALU.mult)
            tt(e[2], lam_im, e[0], ALU.mult)
            to_turns(e[2], e[6])
            tt(pw_re[:, :, :], over_g(e[1]), powers, ALU.mult)
            tt(pw_im[:, :, :], over_g(e[2]), powers, ALU.mult)
            fraction(pw_im[:, :, :], pt2[:, :, :])
            ts(mag8[:, :], e[1], float(T8), ALU.mult)
            ts(turn8[:, :], e[2], float(T8), ALU.mult)
            fraction(turn8[:, :], e[6])
            dve.sem_inc(s5_angle, 1)
            dve.wait_ge(s5_mag, 4)
            dve.wait_ge(s5_sine, 4)
            tt(pt2[:, :, :], pt2[:, :, :], pt2[:, :, :], ALU.mult)
            ts(pt2[:, :, :], pt2[:, :, :], -2.0, ALU.mult, 1.0, ALU.add)
            tt(pw_re[:, :, :], pt2[:, :, :], pt1[:, :, :], ALU.mult)
            do(dve.scalar_tensor_tensor(pw_im[:, :, :], pw_im[:, :, :], sign[:, 1:2], pt1[:, :, :],
                                        ALU.mult, ALU.mult))
            tt(e[5], e[5], e[5], ALU.mult)
            do(dve.scalar_tensor_tensor(e[5], e[5], -2.0, e[3], ALU.mult, ALU.mult))
            do(dve.scalar_tensor_tensor(e[5], e[3], -1.0, e[5], ALU.add, ALU.add))
            tt(e[4], e[4], e[3], ALU.mult)
            tt(e[6], lam_re, lam_re, ALU.mult)
            tt(e[7], lam_im, lam_im, ALU.mult)
            tt(e[6], e[6], e[7], ALU.add)
            do(dve.reciprocal(e[6], e[6]))
            tt(e[7], e[5], lam_re, ALU.mult)
            tt(e[8], e[4], lam_im, ALU.mult)
            tt(e[7], e[7], e[8], ALU.add)
            tt(e[7], e[7], e[6], ALU.mult)
            tt(e[8], e[4], lam_re, ALU.mult)
            tt(e[9], e[5], lam_im, ALU.mult)
            tt(e[8], e[8], e[9], ALU.subtract)
            tt(e[8], e[8], e[6], ALU.mult)
            ts(e[9], e[8], sign[:, 0:1], ALU.mult)
            ts(e[10], e[8], sign[:, 1:2], ALU.mult)
            for n in (2, 3):
                ts(bc[:, n, :, :], bc[:, n, :, :], sign[:, 0:1], ALU.mult)

            def read5(turn, key):
                dve.wait_ge(s_job, s5_count(turn, key))
                return ps[S5_JOBS[key]]

            batch = lambda ap, k, n: ap.rearrange("p (a b g) -> p a b g", b=2, g=GB)[:, k, n]
            batch3 = lambda ap, k, n: ap.rearrange("p (a b g) q -> p a b g q", b=2, g=GB)[:, k, n]
            over_c = lambda ap: ap.unsqueeze(2).broadcast_to((P, GB, C8))
            over_q = lambda ap: ap.unsqueeze(2).broadcast_to((P, GB, GP))

            def tables(turn, k, n):
                if turn is not None:
                    dve.wait_ge(s5_sine, k * 2 + (n + 4))
                tt(turn5[:, :, :], over_c(batch(turn8[:, :], k, n)),
                   count[:, :].unsqueeze(1).broadcast_to((P, GB, C8)), ALU.mult)
                fraction(turn5[:, :, :], turn5_tmp[:, :, :])
                dve.sem_inc(s5_angle, 1)
                for m in range(2):
                    ch(dve.tensor_tensor(bb[m][:, :, :], batch3(bc[:, m], k, n),
                                         over_q(batch(e[7], k, n)), ALU.mult))
                    tt(t5f[:, :, :], batch3(bc[:, 1 - m], k, n), over_q(batch(e[10 - m], k, n)), ALU.mult)
                    tt(bb[m][:, :, :], bb[m][:, :, :], t5f[:, :, :], ALU.add)

                def outer(o, first, powers_n, one, two):
                    m = powers_n
                    shape = (P, GB, m, GP)
                    pr, pi = (ap[:, first:first + m, :].rearrange("p j (a b g) -> p a b g j", b=2, g=GB)
                              [:, k, n].unsqueeze(3).broadcast_to(shape)
                              for ap in (pw_re, pw_im))
                    one, two = (ap.unsqueeze(2).broadcast_to(shape) for ap in (one, two))
                    ch(dve.tensor_tensor(o, pr, one, ALU.mult))
                    ch(dve.tensor_tensor(wvt2[:, :, 0:m, :], pi, two, ALU.mult))
                    ch.wait()
                    return dve.tensor_tensor(o, o, wvt2[:, :, 0:m, :], ALU.add)

                outer(wvt[:, :, :, :], 0, T8, bb[0][:, :, :], bb[1][:, :, :]).then_inc(w_ready, 1)
                dve.wait_ge(w_ready, k * 4 + (2 * n + 1))
                if turn:
                    dve.wait_ge(s_job, s5_count(turn, "y1"))
                outer(wc[n][:, :, :].rearrange("p g (j q) -> p g j q", q=GP), T8, T8 + 1,
                      batch3(bc[:, 2], k, n), batch3(bc[:, 3], k, n)).then_inc(w_ready, 1)

            def response(turn, k, n):
                ch(dve.tensor_tensor(t5f[0:GP, :, :],
                                     ident[0:GP, 0:GP].unsqueeze(1).broadcast_to((GP, GB, GP)),
                                     batch3(d_row, k, n), ALU.mult))
                for m in range(2):
                    p = read5(turn, f"k{m}")
                    ch(dve.tensor_copy(kpad[n][:, 4 * m:4 * m + 4, P:],
                                       p[0:GP, :].rearrange("p (g s) -> p g s", g=4)))
                ch.wait()
                do(dve.tensor_tensor(kpad[n][:, :, P:P + GP], kpad[n][:, :, P:P + GP],
                                     t5f[0:GP, :, :], ALU.add))
                dve.sem_inc(kpad_ready, 1)
                dve.wait_ge(s5_sine, k * 2 + (n + 5))
                ch(dve.tensor_copy(decay8[n][:, :, :], over_c(batch(mag8[:, :], k, n))))
                tt(cosc[n][:, :, :], cosc[n][:, :, :], cosc[n][:, :, :], ALU.mult)
                ch(dve.memset(decay8[n][:, :, 0:1], 0.0))
                ch(dve.tensor_scalar(sinc[n][:, :, :], sinc[n][:, :, :], sign[:, 0:1], None, ALU.mult))
                ts(cosc[n][:, :, :], cosc[n][:, :, :], -2.0, ALU.mult, 1.0, ALU.add)

            def state5(turn, k, n):
                flat = lambda ap: ap.rearrange("p g c -> p (g c)")
                dve.wait_ge(s_act, s5_count(turn, "v", S5_COPIES))
                ch(dve.tensor_tensor(t5b[:, :, :], vin[:, :, :], cosc[n][:, :, :], ALU.mult))
                p = read5(turn, "vs")
                ch(dve.tensor_tensor(flat(t5a[:, :, :]), p[:, :], flat(sinc[n][:, :, :]), ALU.mult))
                ch.wait()
                tt(t5a[:, :, :], t5a[:, :, :], t5b[:, :, :], ALU.add)
                do(dve.tensor_tensor_scan(flat(zst[:, :, :]), flat(decay8[n][:, :, :]),
                                          flat(t5a[:, :, :]), 0.0, ALU.mult, ALU.add))
                dve.sem_inc(x_ready, 1)
                ch(dve.tensor_tensor(t5b[:, :, :], zst[:, :, :], cosc[n][:, :, :], ALU.mult))
                p = read5(turn, "zs")
                ch(dve.tensor_tensor(t5a[:, :, :], p[:, :].rearrange("p (g c) -> p g c", g=GB),
                                     sinc[n][:, :, :], ALU.mult))
                ch.wait()
                do(dve.tensor_tensor(xst[:, :, 1:], t5b[:, :, 0:C8 - 1], t5a[:, :, 0:C8 - 1],
                                     ALU.subtract))
                dve.sem_inc(x_ready, 1)

            def dve_turn(turn, b, f, g):
                if not isinstance(turn, int) and turn[1] == 0:
                    ch.enter(turn[0], 2 * 30, 1)
                state5(turn, *b)
                if f:
                    response(turn, *f)
                if g:
                    tables(turn, *g)
                if not isinstance(turn, int) and turn[1] == 1:
                    ch.leave(FT // 2 - 2)

            dve.wait_ge(mix_stored, FT * 16)
            dve.wait_ge(zeros_set, 3)
            dve.wait_ge(d_in, 16)
            tables(None, 0, 0)
            response(0, 0, 0)
            tables(0, 0, 1)
            s5_turns(dve, dve_turn)
            over(dve, 4)

            def split_tiles(first, n, tile, done):
                for i in range(n):
                    ch(dve.tensor_copy(zh[:, first + i, :], tile(i)))
                    ch.wait()
                    dve.tensor_tensor(zl[:, first + i, :], tile(i), zh[:, first + i, :].bitcast(F32),
                                      ALU.subtract).then_inc(done, 1)

            for h in range(2):
                dve.wait_ge(gy_in[h], 16)
                split_tiles(FT + 4 * h, 4, lambda i: gy[:, 4 * h + i, :], gy_split)
            dve.wait_ge(mix_in, 16)
            split_tiles(0, FT, lambda i: mix_tiles[:, i, :], mix_split)
            for n in range(4):
                u = n % 2
                dve.wait_ge(glu_out, n + 1)
                dve.wait_ge(sgt_in[u], 16 * (n // 2 + 1))
                tt(gsig[u][:, :, :], gsig[u][:, :, :], gy[:, 2 * n:2 * n + 2, :], ALU.mult)
                dve.tensor_tensor(mix_tiles[:, FT + 2 * n:FT + 2 * n + 2, :], gsig[u][:, :, :],
                                  sgt[u][:, :, :], ALU.mult).then_inc(glu_mixed, 1)
            dve.wait_ge(glu_mixed, 4)
            dve.wait_ge(piece_used, P_GLU + 4)
            split_tiles(FT, FT, lambda i: mix_tiles[:, FT + i, :], mix_split)

            def take_group(layer, k, u):
                dve.wait_ge(piece_used, k * 4 + ((P_OUT0, P_OUT1)[layer] + 2 * u + 2))
                cut = lambda ap: ap.rearrange("p (a b w) -> p a b w", b=2, w=256)[:, k, u]
                for t in range(TT):
                    ch(dve.tensor_tensor(cut(y6[:, t, :]), ps[4 * u + t][:, 0:256],
                                         cut(gp[layer][:, :]), ALU.mult))
                ch.wait()
                dve.sem_inc(out_scaled, 1)

            def finish_layer(layer):
                dve.wait_ge(mix_split, KT * (layer + 1))
                with dve.Fori(0, 4) as k:
                    ch.enter(k, 8)
                    for u in range(2):
                        take_group(layer, k, u)
                    ch.leave(4)
                dve.wait_ge(out_read, 10 * layer + 10)
                ch(dve.tensor_reduce(small[:, 0:4], sum_parts[:, :, :], AX.X, ALU.add))
                ch.wait()
                dve.sem_inc(squares_summed, 1)
                dve.wait_ge(root_done, 2 * layer + 2)
                ch(dve.reciprocal(small[:, 8:12], small[:, 4:8]))
                ch.wait()
                dve.wait_ge(h_in, 16 * (layer + 1))
                for t in range(TT):
                    dve.scalar_tensor_tensor(x6[:, t, :], y6[:, t, :], small[:, 8 + t:9 + t],
                                             x6[:, t, :], ALU.mult, ALU.add).then_inc(h_ready, 1)

            finish_layer(0)

            norm_x(1, diag6)
            split_z(1, ztmp6)
            dve.wait_ge(h_stored, 16 * TT)
            over(dve, 5)

            dve.wait_ge(rope_in, 64)
            do(dve.tensor_copy(r1[:, :], pos[:, :]))
            ts(r1[:, :], r1[:, :], rope_c[:, 0:1], ALU.mult)
            to_turns(r1[:, :], r2[:, :])
            dve.sem_inc(angle, 1)
            dve.wait_ge(rope_sine, 2)
            tt(r2[:, :], r2[:, :], r2[:, :], ALU.mult)
            ts(rot[0:64, :], r2[0:64, :], -2.0, ALU.mult, 1.0, ALU.add)
            ts(rot[64:, :], r1[64:, :], rope_c[64:, 1:2], ALU.mult)
            dve.wait_ge(piece_used, P_IN1 + 1)
            dve.tensor_tensor(ktmp[:, :], ps[7][:, :], rot[:, :], ALU.mult).then_inc(key_rotated, 1)
            dve.wait_ge(in1_read, 6)
            for n, total in enumerate((r1, r2)):
                tt(total[:, :], cq[:, 4 * n, :], cq[:, 4 * n, :], ALU.mult)
                for i in range(4 * n + 1, 4 * n + 4):
                    tt(rms_kv[:, :], cq[:, i, :], cq[:, i, :], ALU.mult)
                    tt(total[:, :], total[:, :], rms_kv[:, :], ALU.add)
            dve.sem_inc(c_squared, 1)
            dve.wait_ge(key_folded, 1)
            do(dve.tensor_copy(key_pe[:, :], ps[6][:, :]))
            dve.wait_ge(c_root, 2)
            for r in (ktmp, rms_kv):
                do(dve.reciprocal(r[:, :], r[:, :]))
            for i in range(8):
                c, r = cq[:, i, :], (ktmp, rms_kv)[i // 4][:, :]
                do(dve.scalar_tensor_tensor(c, c, col(("qn", "kvn")[i // 4], i % 4), r,
                                            ALU.mult, ALU.mult))
            over(dve, 6)

            for i in range(8):
                dve.wait_ge(c_hi, i + 1)
                dve.tensor_tensor(zl[:, i, :], cq[:, i, :], zh[:, i, :].bitcast(F32),
                                  ALU.subtract).then_inc(c_split, 1)
            dve.wait_ge(c_split, 8)
            dve.sem_inc(a_dve, aj.total("dve"))
            dve.sem_inc(o_read, 2)

            def attention_turn(k, split):
                def job(key):
                    dve.wait_ge(a_job, k * len(aj.jobs) + aj.number(key))
                    return ps[aj.bank(key)]

                for a in range(2):
                    p = job(("qp", a))
                    dve.tensor_tensor(qp[a][:, :], p[:, :], rot[:, :], ALU.mult).then_inc(a_dve, 1)
                for i in range(10):
                    if i < 8:
                        a, b = divmod(i, TT)
                        p = job(("s", a, b))
                        do(dve.tensor_reduce(stat[:, 0, i:i + 1], p[:, 0:(b + 1) * P], AX.X, ALU.max))
                        do(dve.tensor_scalar(stat[:, 0, i:i + 1], stat[:, 0, i:i + 1], -SCALE, None,
                                             ALU.mult))
                        dve.sem_inc(max_ready, 1)
                    if i >= 2:
                        n = i - 2
                        a, b = divmod(n, TT)
                        dve.wait_ge(a_act, k * aj.total("act") + (aj.total("act") + aj.copies(("s", a, b))))
                        do(dve.reciprocal(stat[:, 2, n:n + 1], stat[:, 1, n:n + 1]))
                        pr = probs[a][:, b, 0:(b + 1) * P]
                        dve.tensor_scalar(pr, pr, stat[:, 2, n:n + 1], None, ALU.mult)\
                           .then_inc(probs_ready, 1)
                for i in range(8):
                    a, b = divmod(i, TT)
                    p = job(("pt", a, b))
                    w = (b + 1) * P
                    dve.tensor_copy(pt9[i % 2][:, 0:w], p[:, 0:w]).then_inc(a_dve, 1)
                    if i in (5, 7):
                        a = (i - 5) // 2
                        dve.wait_ge(o_ready, k * 2 + (a + 1))
                        o = sg1[:, :, :].rearrange("p (h a) t -> p h a t", a=2)[:, k, a]
                        dve.tensor_tensor(o, o, ps[6 + a][:, :], ALU.mult).then_inc(o_read, 1)
                        if split:
                            dve.wait_ge(o_read, k * 2 + (a + 3))
                            hi, lo = (z[:, :, :].rearrange("p (h a) t -> p h a t", a=2)
                                      [:, k + FT // 2, a] for z in (zh, zl))
                            ch(dve.tensor_copy(hi, o))
                            ch.wait()
                            dve.tensor_tensor(lo, o, hi.bitcast(F32), ALU.subtract)\
                               .then_inc(mix_split, 1)

            with dve.Fori(0, FT // 2) as k:
                ch.enter(k, 26)
                attention_turn(k, True)
                ch.leave(FT // 2)
            with dve.Fori(FT // 2, H // 2) as k:
                ch.enter(k, 24, FT // 2)
                attention_turn(k, False)
                ch.leave(H // 2 - FT // 2)
            dve.wait_ge(o_read, H + 2)
            over(dve, 7)

            split_tiles(0, FT, lambda i: sg1[:, FT + i, :], mix_split)
            finish_layer(1)
            over(dve, 8)


def arrange(i):
    f = lambda n: np.ascontiguousarray(i[n])

    def groups(w, rows, width):
        n = w.shape[1] // width
        w = w.reshape(rows // P, P, n, width).transpose(2, 1, 0, 3)
        return w.reshape(-1, P, rows // P * width)

    def halves(g):
        n = g.shape[0]
        return g.reshape(n, P, 2, PIECE).transpose(0, 2, 1, 3).reshape(2 * n, P, PIECE)

    w0 = f("ev_w_in")[0]
    a_in = 4 * W + 128
    pieces = [groups(w0[:, 4 * W:a_in], D, P),
              halves(groups(np.concatenate([w0[:, :4 * W], w0[:, a_in:]], 1), D, 256)),
              groups(f("ev_glu_w")[0], W, 256),
              halves(groups(f("ev_w_out")[0], D, 256))]
    w1 = f("od_w_in")[0]
    pe = w1[:, 1024:1088]
    pe_both = np.concatenate([pe, pe[:, 32:], pe[:, :32]], 1)
    pieces += [groups(pe_both, D, P),
               halves(groups(np.concatenate([w1[:, :1024], w1[:, 1088:]], 1), D, 256))]
    q = f("od_w_q_up")[0].reshape(512, 16, 192)
    q = np.concatenate([q, q[:, :, 160:192], q[:, :, 128:160]], 2)
    kv = f("od_w_kv_up")[0].reshape(512, 16, 256)
    for hp in range(8):
        pieces.append(groups(q[:, 2 * hp:2 * hp + 2].reshape(512, 512), 512, 512))
        k2 = kv[:, 2 * hp:2 * hp + 2, :128].reshape(512, 256)
        v2 = kv[:, 2 * hp:2 * hp + 2, 128:].reshape(512, 256)
        pieces.append(groups(np.concatenate([k2, v2], 1), 512, 512))
    pieces.append(halves(groups(f("od_w_out")[0], D, 256)))
    ws = np.concatenate(pieces, 0)
    assert ws.shape == (N_PIECES, P, PIECE), ws.shape
    ada = np.stack([f("ev_ada_w")[0], f("od_ada_w")[0]]).reshape(2, KT, P, 3, D)
    vec = {"c": f("c")[0], "mu": f("ev_mu")[0], "pre0": f("ev_norm_pre")[0],
           "ab0": f("ev_ada_b")[0, :2 * D], "w0": f("ev_w0")[0], "a0": f("ev_a0")[0],
           "kk": f("ev_k_k")[0], "ka": f("ev_k_a")[0], "rk": f("ev_r_k")[0],
           "lnxg": f("ev_lnx_g")[0], "lnxb": f("ev_lnx_b")[0], "glub": f("ev_glu_b")[0],
           "pre1": f("od_norm_pre")[0], "ab1": f("od_ada_b")[0, :2 * D],
           "qn": f("od_q_norm")[0], "kvn": f("od_kv_norm")[0]}
    cols = np.concatenate([vec[n].reshape(k, P).T for n, k in VECTORS], 1)
    return {
        **lora_and_masks(f), **s5_layout(f),
        "ws": ws.reshape(N_PIECES // 2, 2, P, PIECE), "ada": np.ascontiguousarray(ada.transpose(0, 1, 3, 2, 4)),
        "cols": np.ascontiguousarray(cols), "ident": np.eye(P, dtype=np.float32),
        "rows": np.stack([f("ev_ada_b")[0, 2 * D:], f("ev_norm_post")[0],
                          f("od_ada_b")[0, 2 * D:], f("od_norm_post")[0]]),
        "x": f("x")[0], **rotary_layout(), "pos": f("positions")[0],
    }


def rotary_layout():
    i = np.arange(P)
    freq = np.float32(1) / np.float32(10000) ** ((2 * (i % 32)).astype(np.float32) / np.float32(64))
    sign = np.where(i < 64, 0, np.where(i < 96, -1, 1))
    return {"rope_c": np.stack([freq, sign], 1).astype(np.float32),
            "fold": (i[:, None] % 64 == i[None] % 64).astype(np.float32),
            "neg_tri": np.where(i[None] > i[:, None], -1e30, 0).astype(np.float32)}


def lora_and_masks(f):
    w2, a2 = (f(n)[0].reshape(64, FT // 2, 2, P).transpose(1, 2, 0, 3) for n in ("ev_w2", "ev_a2"))
    zero = np.zeros_like(w2)
    lora = np.stack([np.concatenate([w2, zero], 2), np.concatenate([zero, a2], 2)], 3)
    i = np.arange(P)
    head, t = i // CH, i % CH
    tri = np.concatenate([t[:, None] <= np.arange(CH)[None],
                          (head[:, None] == head[None]) & (t[:, None] < t[None])], 1)
    corner = np.stack([(i[:, None] // (2 * m) == i[None] // (2 * m)) & (i[:, None] // m % 2 == 1)
                       & (i[None] // m % 2 == 0) for m in (2 ** n for n in range(LEVELS))], 1)
    corner = np.concatenate([corner, corner[:, :1].transpose(2, 1, 0)], 1)
    return {"lora": lora, "tri": tri.astype(np.float32), "corner": corner.astype(np.float32),
            "blk1": (head[:, None] == head[None]).astype(np.float32),
            "starts": np.tile((np.arange(L) % CH != 0).astype(np.float32), (P, 1))}


def s5_layout(f):
    half = np.repeat(np.array([1, -1], np.float32), NS)
    both = lambda a: np.concatenate([a, a], 0)
    step = np.broadcast_to(f("ev_log_dt")[0], (P, G))
    lam = np.stack([both(f("ev_lam_re")[0].T), both(f("ev_lam_im")[0].T), step], 1)
    br, bi = (f(n)[0].transpose(1, 0, 2) for n in ("ev_b_re", "ev_b_im"))
    cr, ci = (f(n)[0].transpose(2, 0, 1) for n in ("ev_c_re", "ev_c_im"))
    bc = np.stack([np.concatenate(x, 0) for x in ((br, bi), (bi, br), (cr, ci), (ci, cr))], 1)
    swap = np.eye(P, dtype=np.float32)[(np.arange(P) + NS) % P]
    expo = np.array([*range(T8 - 1, -1, -1), *range(T8 + 1)], np.float32)
    return {"lam": np.ascontiguousarray(lam), "bc": np.ascontiguousarray(bc), "swap": swap,
            "sign": np.stack([half, -half], 1), "expo": np.tile(expo, (P, 1)),
            "count": np.tile(np.arange(C8, dtype=np.float32), (P, 1)), "d": f("ev_d")[0]}


def kernel(**inputs):
    import concourse.bacc as bacc
    from concourse.bass_utils import run_bass_kernel_spmd

    nc = bacc.Bacc("TRN2", target_bir_lowering=False, num_devices=1)
    arrays, aps = {}, {}
    for name, a in arrange({n: np.asarray(a) for n, a in inputs.items()}).items():
        a = np.ascontiguousarray(a)
        arrays[f"in_{name}_dram"] = a
        aps[name] = nc.dram_tensor(f"in_{name}_dram", a.shape, mybir.dt.from_np(a.dtype),
                                   kind="ExternalInput").ap()
    out = nc.dram_tensor("out_0_dram", (1, L, D), F32, kind="ExternalOutput").ap()
    trunk(nc, aps, out)
    result = run_bass_kernel_spmd(nc, [arrays], core_ids=[0])
    return result.results[0]["out_0_dram"]
```
